# Optimizing a Trainium2 kernel written in Bass

```python
import math
import jax, jax.numpy as jnp
from jax import lax
import numpy as np

D_MODEL = 1024
BATCH = 1
SEQ = 512
DEPTH = 1

D_LRU = 1024
LRU_HEADS = 16
LRU_HEAD_DIM = D_LRU // LRU_HEADS
CONV_WIDTH = 4
LRU_C = 8.0
D_POOL = 512
POOL_WINDOWS = (2, 4, 8, 16)
POOL_GROUPS = len(POOL_WINDOWS)
POOL_GROUP_DIM = D_POOL // POOL_GROUPS
D_IN = 2 * D_LRU + D_POOL + 2 * D_MODEL
N_GROUPS = 4
EXPERTS_PER_GROUP = 8
N_EXPERTS = N_GROUPS * EXPERTS_PER_GROUP
TOP_K_EXPERT = 2
D_EXPERT = 512
EXPERT_BLOCK = 256
PLE_DIM = 256
EPS = 1e-6

kernel_name = "hybrid_rglru_pool_hmoe_ple"

def rms_norm(x, g):
    xf = x.astype(jnp.float32)
    y = xf * lax.rsqrt(jnp.mean(xf * xf, axis=-1, keepdims=True) + EPS)
    return (y * g.astype(jnp.float32)).astype(x.dtype)

def causal_depthwise_conv(x, w, b):
    c = x.shape[-1]
    y = lax.conv_general_dilated(x, w[:, None, :].astype(x.dtype), window_strides=(1,),
                                 padding=[(CONV_WIDTH - 1, 0)],
                                 dimension_numbers=('NWC', 'WIO', 'NWC'),
                                 feature_group_count=c)
    return y + b.astype(x.dtype)

def _lin_rec_combine(c1, c2):
    a1, b1 = c1
    a2, b2 = c2
    return a1 * a2, a2 * b1 + b2

def rg_lru(x, w_r, b_r, w_i, b_i, lam):
    bsz, s, _ = x.shape
    xf = x.astype(jnp.float32)
    xh = xf.reshape(bsz, s, LRU_HEADS, LRU_HEAD_DIM)
    r = jax.nn.sigmoid(jnp.einsum('bshi,hij->bshj', xh, w_r.astype(jnp.float32)).reshape(bsz, s, D_LRU) + b_r.astype(jnp.float32))
    i = jax.nn.sigmoid(jnp.einsum('bshi,hij->bshj', xh, w_i.astype(jnp.float32)).reshape(bsz, s, D_LRU) + b_i.astype(jnp.float32))
    log_a = -LRU_C * r * jax.nn.softplus(-lam.astype(jnp.float32))
    a = jnp.exp(log_a)
    mult = jnp.sqrt(-jnp.expm1(2.0 * log_a))
    u = mult * (i * xf)
    _, h = lax.associative_scan(_lin_rec_combine, (a, u), axis=1)
    return h.astype(x.dtype)

def multiscale_pool(x, w_pool, scale):
    bsz, s, _ = x.shape
    xg = x.astype(jnp.float32).reshape(bsz, s, POOL_GROUPS, POOL_GROUP_DIM)
    csum = jnp.cumsum(xg, axis=1)
    pos = jnp.arange(s, dtype=jnp.float32)
    outs = []
    for g, w in enumerate(POOL_WINDOWS):
        c = csum[:, :, g]
        shifted = jnp.pad(c, ((0, 0), (w, 0), (0, 0)))[:, :s]
        count = jnp.minimum(pos + 1.0, float(w))[None, :, None]
        outs.append((c - shifted) / count - xg[:, :, g])
    pooled = jnp.stack(outs, axis=2)
    mixed = jnp.einsum('bsgc,gcd->bsgd', pooled, w_pool.astype(jnp.float32)).reshape(bsz, s, D_POOL)
    return (mixed * scale.astype(jnp.float32)).astype(x.dtype)

def hierarchical_moe(u, w_rg, b_rg, w_re, b_re, w_gate_e, w_up_e, w_down_e):
    n, d = u.shape
    uf = u.astype(jnp.float32)
    group_logits = uf @ w_rg.astype(jnp.float32) + b_rg.astype(jnp.float32)
    g_idx = jnp.argmax(group_logits, axis=-1)
    p_group = jnp.take_along_axis(jax.nn.softmax(group_logits, axis=-1), g_idx[:, None], axis=-1)
    exp_logits = (uf @ w_re.astype(jnp.float32) + b_re.astype(jnp.float32)).reshape(n, N_GROUPS, EXPERTS_PER_GROUP)
    sel = jnp.take_along_axis(exp_logits, g_idx[:, None, None], axis=1)[:, 0]
    top_v, top_i = lax.top_k(sel, TOP_K_EXPERT)
    gates = p_group * jax.nn.softmax(top_v, axis=-1)
    expert_ids = g_idx[:, None].astype(jnp.int32) * EXPERTS_PER_GROUP + top_i.astype(jnp.int32)

    a_tot = n * TOP_K_EXPERT
    flat_e = expert_ids.reshape(-1)
    flat_tok = jnp.repeat(jnp.arange(n, dtype=jnp.int32), TOP_K_EXPERT)
    flat_w = gates.reshape(-1)
    order = jnp.argsort(flat_e)
    e_s = flat_e[order]
    tok_s = flat_tok[order]
    w_s = flat_w[order]
    counts = jnp.bincount(flat_e, length=N_EXPERTS)
    padded = ((counts + EXPERT_BLOCK - 1) // EXPERT_BLOCK) * EXPERT_BLOCK
    pad_end = jnp.cumsum(padded)
    pad_start = pad_end - padded
    start = jnp.cumsum(counts) - counts
    dest = pad_start[e_s] + (jnp.arange(a_tot, dtype=jnp.int32) - start[e_s])
    num_blocks = (a_tot + N_EXPERTS * (EXPERT_BLOCK - 1) + EXPERT_BLOCK - 1) // EXPERT_BLOCK
    rows = num_blocks * EXPERT_BLOCK
    row_tok = jnp.full((rows,), n, dtype=jnp.int32).at[dest].set(tok_s)
    u_pad = jnp.concatenate([u, jnp.zeros((1, d), u.dtype)], axis=0)
    xb = u_pad[row_tok].reshape(num_blocks, EXPERT_BLOCK, d)
    block_expert = jnp.minimum(
        jnp.searchsorted(pad_end, jnp.arange(num_blocks, dtype=jnp.int32) * EXPERT_BLOCK, side='right'),
        N_EXPERTS - 1)

    def expert_block(args):
        xblk, e = args
        h = jax.nn.silu(xblk @ w_gate_e[e]) * (xblk @ w_up_e[e])
        return h @ w_down_e[e]

    y = lax.map(expert_block, (xb, block_expert)).reshape(rows, d)
    contrib = y[dest] * w_s[:, None].astype(y.dtype)
    return jax.ops.segment_sum(contrib, tok_s, num_segments=n)

def setup_inputs(seed: int = 0) -> dict:
    key = jax.random.key(seed)
    ks = jax.random.split(key, 32)
    L, D = DEPTH, D_MODEL
    nrm = lambda k, shape, scale: jax.random.normal(k, shape, jnp.float32) * scale
    a_lo, a_hi = 0.9 ** (1.0 / LRU_C), 0.999 ** (1.0 / LRU_C)
    a0 = jax.random.uniform(ks[9], (L, D_LRU), jnp.float32, a_lo, a_hi)
    return {
        "x": nrm(ks[0], (BATCH, SEQ, D), 1.0),
        "p": nrm(ks[1], (DEPTH, BATCH, SEQ, PLE_DIM), 1.0),
        "norm_mix_g": 1.0 + nrm(ks[2], (L, D), 0.05),
        "w_in": nrm(ks[3], (L, D, D_IN), D ** -0.5),
        "conv_w": nrm(ks[4], (L, CONV_WIDTH, D_LRU), CONV_WIDTH ** -0.5),
        "conv_b": nrm(ks[5], (L, D_LRU), 0.02),
        "w_rg": nrm(ks[6], (L, LRU_HEADS, LRU_HEAD_DIM, LRU_HEAD_DIM), LRU_HEAD_DIM ** -0.5),
        "b_rg": nrm(ks[7], (L, D_LRU), 0.02),
        "w_ig": nrm(ks[8], (L, LRU_HEADS, LRU_HEAD_DIM, LRU_HEAD_DIM), LRU_HEAD_DIM ** -0.5),
        "b_ig": nrm(ks[10], (L, D_LRU), 0.02),
        "lru_lambda": jnp.log(a0) - jnp.log1p(-a0),
        "w_pool": nrm(ks[11], (L, POOL_GROUPS, POOL_GROUP_DIM, POOL_GROUP_DIM), POOL_GROUP_DIM ** -0.5),
        "pool_scale": 1.0 + nrm(ks[12], (L, D_POOL), 0.05),
        "w_up_a": nrm(ks[13], (L, D_LRU, D), D_LRU ** -0.5),
        "w_up_b": nrm(ks[14], (L, D_POOL, D), D_POOL ** -0.5),
        "w_out": nrm(ks[15], (L, D, D), D ** -0.5),
        "norm_ffn_g": 1.0 + nrm(ks[16], (L, D), 0.05),
        "w_router_group": nrm(ks[17], (L, D, N_GROUPS), D ** -0.5),
        "b_router_group": nrm(ks[18], (L, N_GROUPS), 0.01),
        "w_router_expert": nrm(ks[19], (L, D, N_EXPERTS), D ** -0.5),
        "b_router_expert": nrm(ks[20], (L, N_EXPERTS), 0.01),
        "w_gate_e": nrm(ks[21], (L, N_EXPERTS, D, D_EXPERT), D ** -0.5),
        "w_up_e": nrm(ks[22], (L, N_EXPERTS, D, D_EXPERT), D ** -0.5),
        "w_down_e": nrm(ks[23], (L, N_EXPERTS, D_EXPERT, D), D_EXPERT ** -0.5),
        "norm_ple_g": 1.0 + nrm(ks[24], (L, D), 0.05),
        "w_ple": nrm(ks[25], (L, PLE_DIM, D), PLE_DIM ** -0.5),
        "w_ple_gate": nrm(ks[26], (L, D, D), D ** -0.5),
        "final_norm_g": 1.0 + nrm(ks[27], (D,), 0.05),
    }

def reference(x, p, norm_mix_g, w_in, conv_w, conv_b, w_rg, b_rg, w_ig, b_ig, lru_lambda,
              w_pool, pool_scale, w_up_a, w_up_b, w_out, norm_ffn_g,
              w_router_group, b_router_group, w_router_expert, b_router_expert,
              w_gate_e, w_up_e, w_down_e, norm_ple_g, w_ple, w_ple_gate, final_norm_g):
    bsz, s, d = x.shape
    h = x
    for l in range(DEPTH):
        u = rms_norm(h, norm_mix_g[l])
        z = u @ w_in[l]
        xa = z[..., :D_LRU]
        ya = z[..., D_LRU:2 * D_LRU]
        xb = z[..., 2 * D_LRU:2 * D_LRU + D_POOL]
        gate_logits = z[..., 2 * D_LRU + D_POOL:]
        xa = causal_depthwise_conv(xa, conv_w[l], conv_b[l])
        ha = rg_lru(xa, w_rg[l], b_rg[l], w_ig[l], b_ig[l], lru_lambda[l]) * jax.nn.gelu(ya)
        hb = multiscale_pool(xb, w_pool[l], pool_scale[l])
        gates = jax.nn.sigmoid(gate_logits.astype(jnp.float32)).astype(h.dtype)
        merged = gates[..., :d] * (ha @ w_up_a[l]) + gates[..., d:] * (hb @ w_up_b[l])
        h = h + merged @ w_out[l]
        u = rms_norm(h, norm_ffn_g[l])
        moe_out = hierarchical_moe(u.reshape(bsz * s, d), w_router_group[l], b_router_group[l],
                                   w_router_expert[l], b_router_expert[l],
                                   w_gate_e[l], w_up_e[l], w_down_e[l])
        h = h + moe_out.reshape(bsz, s, d)
        u = rms_norm(h, norm_ple_g[l])
        ple_gate = jax.nn.sigmoid((u @ w_ple_gate[l]).astype(jnp.float32)).astype(h.dtype)
        h = h + ple_gate * (p[l] @ w_ple[l])
    return rms_norm(h, final_norm_g)


_drawn_inputs = setup_inputs


def setup_inputs(seed=0):
    import zlib

    import numpy as np

    out = dict(_drawn_inputs(seed))
    spreads = {}
    factors = {'b_rg': 23.68,
     'b_ig': 17.827,
     'b_router_group': 3.137,
     'b_router_expert': 3.835,
     'norm_ple_g': 6.846}
    for name, (base, spread) in spreads.items():
        noise = np.random.default_rng([zlib.crc32(name.encode()), seed]).standard_normal(out[name].shape)
        drawn = base * np.exp(spread * noise) if base else spread * noise
        out[name] = __import__('jax').numpy.asarray(drawn.astype(out[name].dtype))
    for name, factor in factors.items():
        out[name] = (out[name] * factor).astype(out[name].dtype)
    return out
```

```python
from contextlib import ExitStack

import concourse.bass as bass
from concourse import mybir

ALU = mybir.AluOpType
ACT = mybir.ActivationFunctionType
AX = mybir.AxisListType
F32 = mybir.dt.float32
BF16 = mybir.dt.bfloat16
I32 = mybir.dt.int32
U32 = mybir.dt.uint32

P = 128
EPS = 1e-6
LRU_C = 8.0
WINDOWS = (2, 4, 8, 16)
GELU_CUBIC = 0.044715
GELU_SCALE = 1.5957691216057308
SLOTS = 8
SLOT = 4096
C = 64
UNROLL = 8
BIG = 1e30


def build(nc, x, p, norm_mix_g, w_in, conv_w, conv_b, w_rg, b_rg, w_ig, b_ig, lru_lambda, w_pool, pool_scale,
          w_up_a, w_up_b, w_out, norm_ffn_g, w_router_group, b_router_group, w_router_expert, b_router_expert,
          w_gate_e, w_up_e, w_down_e, norm_ple_g, w_ple, w_ple_gate, final_norm_g, out):
    _, S, D = x.shape
    TT = S // P
    KD = D // P
    NX = conv_w.shape[2] // P
    NB = w_up_b.shape[1] // P
    NG = b_router_group.shape[1]
    NE = b_router_expert.shape[1]
    PG = NE // NG
    FE = w_gate_e.shape[3]
    KF = FE // P
    KP = p.shape[3] // P
    NL = NG + NE
    HALF = D // 2
    FAR = 4096
    assert NE % UNROLL == 0 and (3 * UNROLL) % SLOTS == 0 and S == 512 and D == 1024

    E_XA, E_XB, E_YA = (0, 1), 2, (3, 4)
    E_MERGE = SLOTS
    E_OUT = E_MERGE + 8
    E_EXP = E_OUT + 2
    SCRATCH_SLOT = 5

    y_rows = nc.dram_tensor("expert_rows", [2 * S, D], F32, kind="Internal").ap()
    y_halves = y_rows.rearrange("r (h d) -> (r h) d", h=2)

    ctx = ExitStack()
    with ctx:
        def sb(name, shape, dt=F32):
            return ctx.enter_context(nc.sbuf_tensor(name, shape, dt))

        def sem(name):
            return ctx.enter_context(nc.semaphore(name))

        ring = sb("ring", [P, SLOTS, SLOT])
        r1 = sb("r1", [P, KD * S])
        r2 = sb("r2", [P, KD * S])
        r3 = sb("r3", [P, KD * S])
        r4 = sb("r4", [P, NB * S])
        gain = sb("gain", [P, D])
        junk = sb("junk", [P, D])

        uT = r1[:, :].rearrange("p (k t) -> p k t", k=KD)
        h1 = r1[:, :].rearrange("p (i d) -> p i d", i=TT)
        xin = r2[:, :].rearrange("p (i d) -> p i d", i=TT)
        ha = r2[:, :].rearrange("p (c t) -> p c t", c=NX)
        u2 = r2[:, :].rearrange("p (i d) -> p i d", i=TT)
        merged = r3[:, :].rearrange("p (k t) -> p k t", k=KD)
        u2T = merged
        hb = r4[:, :].rearrange("p (g t) -> p g t", g=NB)
        diag = r3[:, 0:NX * 2 * P].rearrange("p (c w j) -> p c w j", c=NX, w=2)
        wpool = r3[:, NX * 2 * P:NX * 2 * P + NB * P].rearrange("p (g j) -> p g j", g=NB)
        scr = ring[:, SCRATCH_SLOT:SLOTS, :].rearrange("p s w -> p (s w)")
        xc = scr[:, 0:2 * S].rearrange("p (b t) -> p b t", b=2)
        lru_t = scr[:, 2 * S:4 * S].rearrange("p (b t) -> p b t", b=2)
        lru_i = scr[:, 4 * S:6 * S].rearrange("p (b t) -> p b t", b=2)
        lru_q = scr[:, 6 * S:8 * S].rearrange("p (b t) -> p b t", b=2)
        lru_a = scr[:, 8 * S:10 * S].rearrange("p (b t) -> p b t", b=2)
        gel = scr[:, 10 * S:12 * S].rearrange("p (b t) -> p b t", b=2)
        PAD = WINDOWS[-1]
        W = PAD + S
        o = 12 * S
        xbp = scr[:, o:o + NB * W].rearrange("p (g t) -> p g t", g=NB)
        o += NB * W
        wsum = scr[:, o:o + 2 * W].rearrange("p (b t) -> p b t", b=2)
        o += 2 * W
        assert o <= 3 * SLOT
        sg_a = junk[:, :].rearrange("p (b t) -> p b t", b=2)
        sg_b = gain[:, :].rearrange("p (b t) -> p b t", b=2)
        yrow = r4[:, 0:2 * HALF].rearrange("p (b d) -> p b d", b=2)
        xrow = r4[:, 2 * HALF:3 * HALF]
        xT = junk[:, :].rearrange("p (b k c) -> p b k c", b=2, k=KD)
        o = 0

        def r3_part(n):
            nonlocal o
            o += n
            return r3[:, o - n:o]

        hT = r3_part(KF * C).rearrange("p (k c) -> p k c", k=KF)
        sig = r3_part(FE // 2)
        hid = r3_part(FE // 2)
        pick = r3_part(2 * TT * C).rearrange("p (b i c) -> p b i c", b=2, i=TT)
        pinfo = r3_part(2 * TT * 2).rearrange("p (b i c) -> p b i c", b=2, i=TT)

        vecs = sb("vecs", [P, P])
        NV = 8 * NX + NB
        prm = sb("prm", [P, NV])
        tap = lambda j, c: prm[:, j * NX + c:j * NX + c + 1]
        col = lambda row, c: prm[:, row * NX + c:row * NX + c + 1]
        lam = prm[:, 7 * NX:8 * NX]
        spt = sb("spt", [P, 6, NX])
        decay = sb("decay", [P, NX])
        ident = sb("ident", [P, P])
        before = sb("before", [P, P], BF16)
        ones = sb("ones", [P, P], BF16)
        iota = sb("iota", [P, C])
        token = sb("token", [P, TT])
        rcount = sb("rcount", [P, PAD])
        eps = sb("eps", [P, 1])
        ssq = sb("ssq", [P, 4 * TT])
        std = sb("std", [P, 4 * TT])
        rstd = sb("rstd", [P, 4 * TT])
        wrt = sb("wrt", [P, KD, NL])
        brt = sb("brt", [P, NL])
        lg = sb("lg", [P, TT, NL])
        g4 = sb("g4", [P, 4, TT, NG])
        t4 = sb("t4", [P, 12, TT])
        el = sb("el", [P, TT, NE])
        cand = sb("cand", [P, TT, NE])
        oh1 = sb("oh1", [P, TT, NE])
        oh2 = sb("oh2", [P, TT, NE])
        routed = sb("routed", [P, TT, NE])
        routed_bf = sb("routed_bf", [P, TT, NE], BF16)
        place = sb("place", [P, NE + 1, TT])
        info = sb("info", [P, NE + 1, TT, 2])
        rounds_i = sb("rounds_i", [P, 1], I32)
        row_base = sb("row_base", [P, 1])
        row_i = sb("row_i", [P, 4], U32)
        gate_c = sb("gate_c", [P, 4])

        bank = [ctx.enter_context(nc.psum_tensor(f"bank{b}", [P, 512], F32)) for b in range(8)]

        x_in = [sem(f"x_in{i}") for i in range(TT)]
        x_back = [sem(f"x_back{i}") for i in range(TT)]
        small_in = sem("small_in")
        lru_in = sem("lru_in")
        gain_in = sem("gain_in")
        slot_full = [sem(f"slot_full{s}") for s in range(SLOTS)]
        const_ready = sem("const_ready")
        pool_step = sem("pool_step")
        zero_ready = sem("zero_ready")
        vec_psum = sem("vec_psum")
        prm_ready = sem("prm_ready")
        decay_exp = sem("decay_exp")
        decay_arg = sem("decay_arg")
        decay_ready = sem("decay_ready")
        sq_done = sem("sq_done")
        std_done = sem("std_done")
        norm_done = sem("norm_done")
        dve_chain = sem("dve_chain")
        act_chain = sem("act_chain")
        ut_psum = sem("ut_psum")
        ut_ready = sem("ut_ready")
        z_ready = sem("z_ready")
        conv_done = sem("conv_done")
        gates_psum = sem("gates_psum")
        i_ready = sem("i_ready")
        tanh_ready = sem("tanh_ready")
        sqrt_free = sem("sqrt_free")
        sqrt_ready = sem("sqrt_ready")
        scan_done = sem("scan_done")
        xb_copied = sem("xb_copied")
        pooled = sem("pooled")
        mixed = sem("mixed")
        hb_ready = sem("hb_ready")
        sq_ready = sem("sq_ready")
        garg_ready = sem("garg_ready")
        gsig_ready = sem("gsig_ready")
        ya_used = sem("ya_used")
        ha_ready = sem("ha_ready")
        merge_psum = sem("merge_psum")
        merge_sig = sem("merge_sig")
        merged_ready = sem("merged_ready")
        out_psum = sem("out_psum")
        h1_ready = sem("h1_ready")
        logits_psum = sem("logits_psum")
        gdiff_ready = sem("gdiff_ready")
        gexp_ready = sem("gexp_ready")
        ediff_ready = sem("ediff_ready")
        eexp_ready = sem("eexp_ready")
        routed_ready = sem("routed_ready")
        places_psum = sem("places_psum")
        rounds_ready = sem("rounds_ready")
        next_round = sem("next_round")
        pick_ready = sem("pick_ready")
        xrow_psum = sem("xrow_psum")
        xrow_ready = sem("xrow_ready")
        xT_psum = sem("xT_psum")
        xT_ready = sem("xT_ready")
        info_psum = sem("info_psum")
        info_ready = sem("info_ready")
        gate_psum = sem("gate_psum")
        gate_up_psum = sem("gate_up_psum")
        sig_ready = sem("sig_ready")
        gated = sem("gated")
        hidden_ready = sem("hidden_ready")
        hT_psum = sem("hT_psum")
        hT_ready = sem("hT_ready")
        y_psum = sem("y_psum")
        y_stored = sem("y_stored")
        rows_taken = sem("rows_taken")
        scattered = sem("scattered")
        row_free = sem("row_free")
        y_in = [sem(f"y_in{i}") for i in range(TT)]
        pT_psum = sem("pT_psum")
        pT_ready = sem("pT_ready")
        ple_psum = sem("ple_psum")
        ple_ready = sem("ple_ready")
        h2_ready = sem("h2_ready")
        pg_psum = sem("pg_psum")
        pg_sig = sem("pg_sig")
        h3_ready = sem("h3_ready")
        stored = sem("stored")

        def slots_at(n):
            return 16 * (n // SLOTS + (1 if n % SLOTS < SCRATCH_SLOT else 0))

        ztiles = ([("xa", c, E_XA[c // 4], c % 4) for c in range(NX)] +
                  [("xb", g, E_XB, g) for g in range(NB)] +
                  [("ya", c, E_YA[c // 4], c % 4) for c in range(NX)])
        NZ = len(ztiles)
        z_free = {"xa": conv_done, "xb": xb_copied, "ya": ya_used}

        def wslot(n, k):
            return ring[:, n % SLOTS, :].rearrange("p (k f) -> p k f", k=k)

        T_PLE = E_EXP
        T_PG = T_PLE + 1
        s0 = T_PLE % SLOTS
        wple = ring[:, s0, 0:KP * D].rearrange("p (k n) -> p k n", k=KP)
        p_rows = ring[:, s0, KP * D:KP * D + TT * KP * P].rearrange("p (i n) -> p i n", i=TT)
        pT = ring[:, s0, KP * D + TT * KP * P:KP * D + 2 * TT * KP * P].rearrange("p (k t) -> p k t", k=KP)
        y_back = ring[:, (s0 + 3) % SLOTS:(s0 + 3) % SLOTS + 2, :].rearrange("p s (i k d) -> p (s i) k d", i=2, k=2)
        ple = ring[:, (s0 + 5) % SLOTS, :].rearrange("p (i d) -> p i d", i=TT)
        u3T = ring[:, (s0 + 6) % SLOTS, :].rearrange("p (k t) -> p k t", k=KD)
        u3 = u2
        fin = ring[:, (s0 + 7) % SLOTS, :].rearrange("p (i d) -> p i d", i=TT)
        psig = r3[:, 0:2 * HALF].rearrange("p (b d) -> p b d", b=2)

        block = ctx.enter_context(nc.Block())

        @block.sync
        def _(sp):
            for i in range(TT):
                sp.dma_start(xin[:, i, :], x[0, i * P:(i + 1) * P, :]).then_inc(x_in[i], 16)

            def entry(n, src, k):
                wait_read(n - SLOTS)
                dst = ring[:, n % SLOTS, 0:k * src.shape[2]].rearrange("p (k f) -> p k f", k=k)
                sp.dma_start(dst, src).then_inc(slot_full[n % SLOTS], 16)

            def wait_read(n):
                if 0 <= n < SCRATCH_SLOT:
                    sp.wait_ge(z_ready, 4 * (n + 1))
                elif E_MERGE <= n < E_OUT:
                    sp.wait_ge(merge_psum, 4 * ((n - E_MERGE) // 4 + 1))
                elif n >= E_OUT:
                    sp.wait_ge(out_psum, TT * (n - E_OUT + 1))

            wi = w_in[0].rearrange("(k p) n -> p k n", p=P)
            for n, blk in enumerate((0, 1, 4, 2, 3)):
                entry(n, wi[:, :, blk * 512:(blk + 1) * 512], KD)
            ub = w_up_b[0].rearrange("(k p) n -> p k n", p=P)
            ua = w_up_a[0].rearrange("(k p) n -> p k n", p=P)
            for h in range(2):
                cols = slice(h * HALF, (h + 1) * HALF)
                n = E_MERGE + 4 * h
                entry(n, wi[:, :, (5 + h) * 512:(6 + h) * 512], KD)
                if h == 1:
                    sp.wait_ge(ha_ready, NX)
                    sp.wait_ge(mixed, NB)
                entry(n + 1, wi[:, :, (7 + h) * 512:(8 + h) * 512], KD)
                entry(n + 2, ub[:, :, cols], NB)
                entry(n + 3, ua[:, :, cols], KD)
            wo = w_out[0].rearrange("(k p) n -> p k n", p=P)
            for h in range(2):
                entry(E_OUT + h, wo[:, :, h * HALF:(h + 1) * HALF], KD)
            sp.wait_ge(merge_psum, KD)
            for i in range(TT):
                sp.dma_start(h1[:, i, :], x[0, i * P:(i + 1) * P, :]).then_inc(x_back[i], 16)

            def load_expert(m, e):
                n, k, w = E_EXP + m, (KD, KD, KF)[m % 3], (w_gate_e, w_up_e, w_down_e)[m % 3]
                src = w[0, e].rearrange("(k p) n -> p k n", p=P) if isinstance(e, int) else \
                    w[0, bass.ds(e, 1)].rearrange("o (k p) n -> p (o k) n", p=P)
                sp.dma_start(wslot(n, k), src).then_inc(slot_full[n % SLOTS], 16)

            for m in range(SLOTS):
                wait_read(E_EXP + m - SLOTS)
                load_expert(m, m // 3)
            sp.wait_ge(rounds_ready, 1)
            rounds = sp.value_load(rounds_i[0:1, 0:1], min_val=1, max_val=S // C)
            final = sp.snap(rounds * (NE // UNROLL) - 1)
            with sp.Fori(0, rounds) as r:
                with sp.Fori(0, NE // UNROLL) as g:
                    it = sp.snap(r * (NE // UNROLL) + g)
                    n0 = sp.snap(it * UNROLL)
                    after_body = sp.snap((g * UNROLL + UNROLL) % NE)

                    def wait_expert_read(m):
                        q = m - SLOTS
                        sp.wait_ge((gate_psum, gate_up_psum, y_psum)[q % 3], n0 + (q // 3 + 1))

                    for m in range(SLOTS, 3 * UNROLL):
                        wait_expert_read(m)
                        load_expert(m, g * UNROLL + m // 3)
                    with sp.If(it < final):
                        for m in range(3 * UNROLL, 3 * UNROLL + SLOTS):
                            wait_expert_read(m)
                            load_expert(m, after_body + (m // 3 - UNROLL))
                    with sp.Else():
                        wait_expert_read(3 * UNROLL)
                        sp.dma_start(wple, w_ple[0].rearrange("(k p) n -> p k n", p=P)).then_inc(slot_full[s0], 16)
                        sp.dma_start(p_rows, p[0, 0].rearrange("(i p) n -> p i n", p=P)).then_inc(slot_full[s0], 16)
                        wg = w_ple_gate[0].rearrange("(k p) n -> p k n", p=P)
                        for h in range(2):
                            wait_expert_read(3 * UNROLL + 1 + h)
                            sp.dma_start(wslot(T_PG + h, KD), wg[:, :, h * HALF:(h + 1) * HALF]).then_inc(
                                slot_full[(T_PG + h) % SLOTS], 16)
            sp.wait_ge(row_free, rounds * NE + 2)
            for i in range(TT):
                for k in range(2):
                    sp.dma_start(y_back[:, i, k, :], y_rows[k * S + i * P:k * S + (i + 1) * P, :]).then_inc(y_in[i], 16)
            for i in range(TT):
                sp.wait_ge(norm_done, 3 * TT + i + 1)
                sp.dma_start(out[0, i * P:(i + 1) * P, :], fin[:, i, :]).then_inc(stored, 16)
            sp.wait_ge(stored, 16 * TT)

        @block.gpsimd
        def _(pool):
            steps = 0

            def after(ins):
                nonlocal steps
                steps += 1
                ins.then_inc(pool_step, 1)
                pool.wait_ge(pool_step, steps)

            nc.gpsimd.memset(ident[:, :], 0.0).then_inc(pool_step, 1)
            nc.gpsimd.memset(before[:, :], 1.0).then_inc(pool_step, 1)
            steps = 2
            pool.wait_ge(pool_step, 2)
            nc.gpsimd.affine_select(out=ident[:, :], in_=ident[:, :], compare_op=ALU.not_equal, fill=1.0, base=0,
                                    pattern=[[-1, P]], channel_multiplier=1).then_inc(const_ready, 1)
            nc.gpsimd.memset(diag[:, :, :, :], 0.0).then_inc(zero_ready, 1)
            nc.gpsimd.memset(eps[:, :], EPS).then_inc(const_ready, 1)
            nc.gpsimd.affine_select(out=before[:, :], in_=before[:, :], compare_op=ALU.is_gt, fill=0.0, base=0,
                                    pattern=[[1, P]], channel_multiplier=-1).then_inc(const_ready, 1)
            nc.gpsimd.memset(ones[:, :], 1.0).then_inc(const_ready, 1)
            nc.gpsimd.iota(iota[:, :], pattern=[[1, C]], base=0, channel_multiplier=0,
                           allow_small_or_imprecise_dtypes=True).then_inc(const_ready, 1)
            nc.gpsimd.iota(token[:, :], pattern=[[2 * P, TT]], base=-FAR, channel_multiplier=2,
                           allow_small_or_imprecise_dtypes=True).then_inc(const_ready, 1)
            nc.gpsimd.memset(row_base[0:C, :], float(FAR)).then_inc(const_ready, 1)
            pool.wait_ge(const_ready, 7)
            nc.gpsimd.memset(row_base[C:P, :], float(FAR + 1)).then_inc(const_ready, 1)
            pool.wait_ge(const_ready, 8)
            nc.gpsimd.memset(xbp[:, :, 0:PAD], 0.0).then_inc(pool_step, 1)
            nc.gpsimd.memset(wsum[:, :, 0:PAD], 0.0).then_inc(pool_step, 1)
            steps += 2
            pool.wait_ge(pool_step, steps)
            pool.wait_ge(prm_ready, 2)
            for g, w in enumerate(WINDOWS):
                pool.wait_ge(xb_copied, g + 1)
                src, b, s = xbp[:, g, :], 0, 1
                while s < w:
                    dst = wsum[:, b, :]
                    after(nc.gpsimd.tensor_tensor(dst[:, PAD:W], src[:, PAD:W], src[:, PAD - s:W - s], ALU.add))
                    src, b, s = dst, 1 - b, 2 * s
                dst = wsum[:, b, :]
                after(nc.gpsimd.tensor_scalar(dst[:, PAD:W], src[:, PAD:W], 1.0 / w, None, ALU.mult))
                after(nc.gpsimd.tensor_tensor(dst[:, PAD:PAD + w], src[:, PAD:PAD + w], rcount[:, 0:w], ALU.mult))
                nc.gpsimd.tensor_tensor(xbp[:, g, PAD:W], dst[:, PAD:W], xbp[:, g, PAD:W],
                                        ALU.subtract).then_inc(pooled, 1)
                pool.wait_ge(pooled, g + 1)
            pool.wait_ge(rounds_ready, 1)
            rounds = pool.value_load(rounds_i[0:1, 0:1], min_val=1, max_val=S // C)
            pool.sem_inc(row_free, 2)
            last_row = pool.to_reg(4 * S - 1)
            with pool.Fori(0, rounds) as r:
                with pool.Fori(0, NE // UNROLL) as g:
                    n0 = pool.snap((r * (NE // UNROLL) + g) * UNROLL)
                    for m in range(UNROLL):
                        pool.wait_ge(y_stored, n0 + (m + 2))
                        pool.sem_inc(rows_taken, 1)
                        nc.gpsimd.indirect_dma_start(
                            out=y_halves, out_offset=bass.IndirectOffsetOnAxis(ap=row_i[:, m % 4:m % 4 + 1], axis=0),
                            in_=yrow[:, m % 2, :], in_offset=None, bounds_check=last_row,
                            oob_is_err=False).then_inc(scattered, 16)
                        pool.wait_ge(scattered, n0 * 16 + 16 * (m + 1))
                        pool.sem_inc(row_free, 1)

        @block.scalar
        def _(act):
            steps = 0

            def after(ins):
                nonlocal steps
                steps += 1
                ins.then_inc(act_chain, 1)
                act.wait_ge(act_chain, steps)

            row = 0
            for v in (conv_w[0].rearrange("w (c p) -> (w c) p", p=P), conv_b[0].rearrange("(c p) -> c p", p=P),
                      b_rg[0].rearrange("(c p) -> c p", p=P), b_ig[0].rearrange("(c p) -> c p", p=P),
                      lru_lambda[0].rearrange("(c p) -> c p", p=P), pool_scale[0].rearrange("(c p) -> c p", p=P)):
                act.dma_start(vecs[row:row + v.shape[0], :], v).then_inc(small_in, 16)
                row += v.shape[0]
            act.dma_start(gain[:, :], norm_mix_g[0].partition_broadcast(P)).then_inc(gain_in, 16)
            act.wait_ge(zero_ready, 1)
            for w, src in enumerate((w_rg, w_ig)):
                for odd in range(2):
                    act.dma_start(diag[64 * odd:64 * odd + 64, :, w, 64 * odd:64 * odd + 64],
                                  src[0].rearrange("(c two) i j -> two i c j", two=2)[odd]).then_inc(lru_in, 16)
            act.dma_start(wpool, w_pool[0].rearrange("g i j -> i g j")).then_inc(lru_in, 16)
            act.dma_start(wrt[:, :, 0:NG], w_router_group[0].rearrange("(k p) n -> p k n", p=P)).then_inc(lru_in, 16)
            act.dma_start(wrt[:, :, NG:NL], w_router_expert[0].rearrange("(k p) n -> p k n", p=P)).then_inc(lru_in, 16)
            act.dma_start(brt[:, 0:NG], b_router_group[0].partition_broadcast(P)).then_inc(lru_in, 16)
            act.dma_start(brt[:, NG:NL], b_router_expert[0].partition_broadcast(P)).then_inc(lru_in, 16)

            def norm(q, src):
                after(nc.scalar.activation(junk[:, :], src, ACT.Square, accum_out=ssq[:, q:q + 1]))
                nc.scalar.activation(std[:, q:q + 1], ssq[:, q:q + 1], ACT.Sqrt, bias=eps[:, 0:1],
                                     scale=1.0 / D).then_inc(std_done, 1)

            act.wait_ge(const_ready, 8)
            for i in range(TT):
                act.wait_ge(x_in[i], 16)
                norm(i, xin[:, i, :])

            def copy_transposed(q, dst, banks):
                i, h = q // 2, q % 2
                act.wait_ge(ut_psum, q + 1)
                dst_k = dst[:, 4 * h:4 * h + 4, (i % TT) * P:(i % TT + 1) * P]
                nc.scalar.activation(dst_k, bank[banks[q % 4]][:, :].rearrange("p (k t) -> p k t", k=4),
                                     ACT.Copy).then_inc(ut_ready, 1)

            for q in range(2 * TT):
                copy_transposed(q, uT, (4, 5, 6, 7))
            act.wait_ge(decay_arg, 1)
            nc.scalar.activation(spt[:, 1, :], spt[:, 0, :], ACT.Exp, scale=-1.0).then_inc(decay_exp, 1)
            act.wait_ge(decay_ready, 1)

            def lru_gates(c):
                b = c % 2
                act.wait_ge(gates_psum, c + 1)
                if c >= 2:
                    act.wait_ge(scan_done, c - 1)
                after(nc.scalar.activation(lru_t[:, b, :], bank[4 + 2 * b][:, :], ACT.Sigmoid, bias=col(5, c)))
                nc.scalar.activation(lru_i[:, b, :], bank[5 + 2 * b][:, :], ACT.Sigmoid, bias=col(6, c)).then_inc(i_ready, 1)
                nc.scalar.activation(lru_t[:, b, :], lru_t[:, b, :], ACT.Tanh, scale=decay[:, c:c + 1]).then_inc(tanh_ready, 1)
                act.wait_ge(tanh_ready, c + 1)
                act.wait_ge(sqrt_free, c + 1)
                nc.scalar.activation(lru_t[:, b, :], lru_t[:, b, :], ACT.Sqrt, scale=-4.0).then_inc(sqrt_ready, 1)

            def pool_copy(g):
                t = NX + g
                act.wait_ge(z_ready, t + 1)
                nc.scalar.activation(xbp[:, g, PAD:W], bank[t % 4][:, :], ACT.Copy).then_inc(xb_copied, 1)

            def gelu(c):
                t = NX + NB + c
                b = c % 2
                act.wait_ge(z_ready, t + 1)
                if c >= 2:
                    act.wait_ge(ya_used, c - 1)
                nc.scalar.activation(gel[:, b, :], bank[t % 4][:, :], ACT.Square).then_inc(sq_ready, 1)
                act.wait_ge(garg_ready, c + 1)
                nc.scalar.activation(gel[:, b, :], gel[:, b, :], ACT.Sigmoid, scale=GELU_SCALE).then_inc(gsig_ready, 1)

            def pool_scaled(g):
                act.wait_ge(mixed, g + 1)
                nc.scalar.activation(hb[:, g, :], bank[4 + g][:, :], ACT.Copy,
                                     scale=prm[:, 8 * NX + g:8 * NX + g + 1]).then_inc(hb_ready, 1)

            for t, (kind, c, _, _) in enumerate(ztiles):
                if kind == "xb":
                    pool_copy(c)
                if kind == "ya":
                    gelu(c)
                if 2 <= t < NX + 2:
                    lru_gates(t - 2)
            for g in range(NB):
                pool_scaled(g)
            for j in range(KD):
                s = 4 * (j % 2)
                act.wait_ge(merge_psum, j + 1)
                if j >= 2:
                    act.wait_ge(merged_ready, j - 1)
                nc.scalar.activation(sg_a[:, j % 2, :], bank[s][:, :], ACT.Sigmoid).then_inc(merge_sig, 1)
                nc.scalar.activation(sg_b[:, j % 2, :], bank[s + 1][:, :], ACT.Sigmoid).then_inc(merge_sig, 1)
            act.wait_ge(merged_ready, KD)
            act.dma_start(gain[:, :], norm_ffn_g[0].partition_broadcast(P)).then_inc(gain_in, 16)
            for i in range(TT):
                act.wait_ge(h1_ready, TT + i + 1)
                norm(TT + i, h1[:, i, :])
                if i >= 1:
                    copy_transposed(2 * (TT + i - 1), u2T, (0, 1, 2, 3))
                    copy_transposed(2 * (TT + i - 1) + 1, u2T, (0, 1, 2, 3))
            copy_transposed(4 * TT - 2, u2T, (0, 1, 2, 3))
            copy_transposed(4 * TT - 1, u2T, (0, 1, 2, 3))
            act.wait_ge(gdiff_ready, 1)
            nc.scalar.activation(g4[:, 3, :, :], g4[:, 0, :, :], ACT.Exp).then_inc(gexp_ready, 1)
            act.wait_ge(ediff_ready, 1)
            nc.scalar.activation(t4[:, 7, :], t4[:, 6, :], ACT.Exp).then_inc(eexp_ready, 1)

            act.wait_ge(rounds_ready, 1)
            rounds = act.value_load(rounds_i[0:1, 0:1], min_val=1, max_val=S // C)

            def copy_rows(n):
                act.wait_ge(xrow_psum, n)
                nc.scalar.activation(xrow, bank[0][:, :], ACT.Copy).then_inc(xrow_ready, 1)

            def copy_xT(b, n):
                act.wait_ge(xT_psum, n)
                nc.scalar.activation(xT[:, b, :, :].rearrange("p (h j) c -> p j h c", h=2),
                                     bank[4][:, :].rearrange("p (j h c) -> p j h c", j=4, h=2), ACT.Copy).then_inc(xT_ready, 1)

            copy_rows(1)
            copy_xT(0, 1)
            with act.Fori(0, rounds) as r:
                with act.Fori(0, NE // UNROLL) as g:
                    n0 = act.snap((r * (NE // UNROLL) + g) * UNROLL)
                    for m in range(UNROLL):
                        b = m % 2
                        act.wait_ge(gate_up_psum, n0 + (m + 1))
                        nc.scalar.activation(sig, bank[2][:, 0:FE // 2], ACT.Sigmoid).then_inc(sig_ready, 1)
                        copy_rows(n0 + (m + 2))
                        copy_xT(1 - b, n0 + (m + 2))
            for i in range(TT):
                for h in range(2):
                    q = 2 * i + h
                    act.wait_ge(ple_psum, q + 1)
                    nc.scalar.activation(ple[:, i, h * HALF:(h + 1) * HALF], bank[q % 4][:, :], ACT.Copy).then_inc(ple_ready, 1)
            act.dma_start(gain[:, :], norm_ple_g[0].partition_broadcast(P)).then_inc(gain_in, 16)
            for i in range(TT):
                act.wait_ge(h2_ready, i + 1)
                norm(2 * TT + i, h1[:, i, :])
                if i >= 1:
                    copy_transposed(2 * (2 * TT + i - 1), u3T, (4, 5, 6, 7))
                    copy_transposed(2 * (2 * TT + i - 1) + 1, u3T, (4, 5, 6, 7))
            copy_transposed(6 * TT - 2, u3T, (4, 5, 6, 7))
            copy_transposed(6 * TT - 1, u3T, (4, 5, 6, 7))
            act.wait_ge(norm_done, 3 * TT)
            act.dma_start(gain[:, :], final_norm_g.partition_broadcast(P)).then_inc(gain_in, 16)
            for i in range(TT):
                for h in range(2):
                    q = 2 * i + h
                    act.wait_ge(pg_psum, q + 1)
                    if q >= 2:
                        act.wait_ge(h3_ready, q - 1)
                    nc.scalar.activation(psig[:, q % 2, :], bank[q % 4][:, :], ACT.Sigmoid).then_inc(pg_sig, 1)
                act.wait_ge(h3_ready, 2 * i + 2)
                norm(3 * TT + i, h1[:, i, :])

        @block.vector
        def _(dve):
            v = nc.vector
            steps = 0

            def after(ins):
                nonlocal steps
                steps += 1
                ins.then_inc(dve_chain, 1)
                dve.wait_ge(dve_chain, steps)

            def normalise(q, src, dst):
                dve.wait_ge(std_done, q + 1)
                after(v.reciprocal(rstd[:, q:q + 1], std[:, q:q + 1]))
                v.scalar_tensor_tensor(out=dst, in0=src, scalar=rstd[:, q:q + 1], in1=gain[:, :], op0=ALU.mult,
                                       op1=ALU.mult).then_inc(norm_done, 1)

            dve.wait_ge(gain_in, 16)
            for i in range(TT):
                normalise(i, xin[:, i, :], xin[:, i, :])
            dve.wait_ge(const_ready, 8)
            dve.wait_ge(vec_psum, 1)
            v.tensor_copy(prm[:, :], bank[0][:, 0:NV]).then_inc(prm_ready, 1)
            dve.wait_ge(prm_ready, 1)
            after(v.tensor_scalar(rcount[:, :], iota[:, 0:PAD], 1.0, None, ALU.add))
            v.reciprocal(rcount[:, :], rcount[:, :]).then_inc(prm_ready, 1)
            after(v.tensor_scalar(spt[:, 2, :], lam, -1.0, None, ALU.mult))
            v.tensor_tensor(spt[:, 0, :], lam, spt[:, 2, :], ALU.max).then_inc(decay_arg, 1)
            after(v.tensor_scalar(spt[:, 2, :], spt[:, 2, :], 0.0, -LRU_C / 2, ALU.max, ALU.mult))
            dve.wait_ge(decay_exp, 1)
            after(v.tensor_scalar(spt[:, 3, :], spt[:, 1, :], 2.0, None, ALU.add))
            after(v.reciprocal(spt[:, 3, :], spt[:, 3, :]))
            after(v.tensor_tensor(spt[:, 3, :], spt[:, 3, :], spt[:, 1, :], ALU.mult))
            after(v.tensor_tensor(spt[:, 4, :], spt[:, 3, :], spt[:, 3, :], ALU.mult))
            after(v.tensor_scalar(spt[:, 5, :], spt[:, 4, :], 1.0 / 15, None, ALU.mult))
            for odd in (13, 11, 9, 7, 5, 3):
                after(v.scalar_tensor_tensor(out=spt[:, 5, :], in0=spt[:, 5, :], scalar=1.0 / odd, in1=spt[:, 4, :],
                                             op0=ALU.add, op1=ALU.mult))
            after(v.scalar_tensor_tensor(out=spt[:, 5, :], in0=spt[:, 5, :], scalar=1.0, in1=spt[:, 3, :],
                                         op0=ALU.add, op1=ALU.mult))
            v.scalar_tensor_tensor(out=decay[:, :], in0=spt[:, 5, :], scalar=-LRU_C, in1=spt[:, 2, :],
                                   op0=ALU.mult, op1=ALU.add).then_inc(decay_ready, 1)

            def conv(c):
                z, y = bank[c % 4], xc[:, c % 2, :]
                dve.wait_ge(z_ready, c + 1)
                after(v.tensor_scalar(y, z[:, :], tap(3, c), col(4, c), ALU.mult, ALU.add))
                for d in (1, 2, 3):
                    ins = v.scalar_tensor_tensor(out=y[:, d:S], in0=z[:, 0:S - d], scalar=tap(3 - d, c), in1=y[:, d:S],
                                                 op0=ALU.mult, op1=ALU.add)
                    if d < 3:
                        after(ins)
                    else:
                        ins.then_inc(conv_done, 1)

            def lru(c):
                b = c % 2
                t, q, a, i = lru_t[:, b, :], lru_q[:, b, :], lru_a[:, b, :], lru_i[:, b, :]
                dve.wait_ge(tanh_ready, c + 1)
                v.tensor_scalar(q, t, -1.0, 1.0, ALU.mult, ALU.add).then_inc(sqrt_free, 1)
                dve.wait_ge(sqrt_free, c + 1)
                after(v.reciprocal(q, q))
                after(v.tensor_scalar(a, q, 2.0, -1.0, ALU.mult, ALU.add))
                after(v.tensor_tensor(i, i, xc[:, b, :], ALU.mult))
                dve.wait_ge(sqrt_ready, c + 1)
                after(v.tensor_tensor(t, t, q, ALU.mult))
                after(v.tensor_tensor(t, t, i, ALU.mult))
                v.tensor_tensor_scan(ha[:, c, :], a, t, 0.0, ALU.mult, ALU.add).then_inc(scan_done, 1)

            def gelu(c):
                t, b = NX + NB + c, c % 2
                y, w = bank[t % 4], gel[:, b, :]
                dve.wait_ge(sq_ready, c + 1)
                after(v.tensor_scalar(w, w, GELU_CUBIC, 1.0, ALU.mult, ALU.add))
                v.tensor_tensor(w, w, y[:, :], ALU.mult).then_inc(garg_ready, 1)
                dve.wait_ge(gsig_ready, c + 1)
                v.tensor_tensor(w, w, y[:, :], ALU.mult).then_inc(ya_used, 1)
                dve.wait_ge(ya_used, c + 1)
                dve.wait_ge(scan_done, c + 1)
                v.tensor_tensor(ha[:, c, :], ha[:, c, :], w, ALU.mult).then_inc(ha_ready, 1)

            for t, (kind, c, _, _) in enumerate(ztiles):
                if kind == "xa":
                    if c >= 2:
                        dve.wait_ge(gates_psum, c - 1)
                    if c >= 2:
                        lru(c - 2)
                    conv(c)
                if t in (NX, NX + 1):
                    lru(t - 2)
                if kind == "ya":
                    gelu(c)
            for j in range(KD):
                s = 4 * (j % 2)
                dve.wait_ge(merge_sig, 2 * j + 1)
                v.tensor_tensor(sg_a[:, j % 2, :], sg_a[:, j % 2, :], bank[s + 3][:, :], ALU.mult).then_inc(dve_chain, 1)
                dve.wait_ge(merge_sig, 2 * j + 2)
                v.tensor_tensor(sg_b[:, j % 2, :], sg_b[:, j % 2, :], bank[s + 2][:, :], ALU.mult).then_inc(dve_chain, 1)
                steps += 2
                dve.wait_ge(dve_chain, steps)
                v.tensor_tensor(merged[:, j, :], sg_a[:, j % 2, :], sg_b[:, j % 2, :], ALU.add).then_inc(merged_ready, 1)
            for h in range(2):
                for i in range(TT):
                    dve.wait_ge(out_psum, h * TT + i + 1)
                    dve.wait_ge(x_back[i], 16)
                    res = h1[:, i, h * HALF:(h + 1) * HALF]
                    v.tensor_tensor(res, res, bank[h * TT + i][:, :], ALU.add).then_inc(h1_ready, 1)
            dve.wait_ge(gain_in, 32)
            dve.wait_ge(h1_ready, 2 * TT)
            for i in range(TT):
                normalise(TT + i, h1[:, i, :], u2[:, i, :])

            def bc(ap, n):
                return ap.unsqueeze(2).to_broadcast([P, ap.shape[1], n])

            def first_max(scores, n, best, index, cands, onehot):
                after(v.tensor_reduce(best, scores, AX.X, ALU.max))
                after(v.tensor_tensor(cands, scores, bc(best, n), ALU.is_equal))
                after(v.scalar_tensor_tensor(out=cands, in0=cands, scalar=-float(C),
                                             in1=iota[:, 0:n].unsqueeze(1).to_broadcast([P, TT, n]),
                                             op0=ALU.mult, op1=ALU.add))
                after(v.tensor_reduce(index, cands, AX.X, ALU.min))
                after(v.tensor_tensor(onehot, cands, bc(index, n), ALU.is_equal))

            gl = lg[:, :, 0:NG]
            dve.wait_ge(logits_psum, 1)
            dve.wait_ge(lru_in, 16 * 9)
            after(v.tensor_tensor(lg[:, :, :], bank[4][:, 0:TT * 64].rearrange("p (i n) -> p i n", i=TT)[:, :, 0:NL],
                                  brt[:, :].unsqueeze(1).to_broadcast([P, TT, NL]), ALU.add))
            first_max(gl, NG, t4[:, 0, :], t4[:, 1, :], g4[:, 1, :, :], g4[:, 2, :, :])
            v.tensor_tensor(g4[:, 0, :, :], gl, bc(t4[:, 0, :], NG), ALU.subtract).then_inc(gdiff_ready, 1)
            onehot_g = g4[:, 2, :, :].unsqueeze(3).to_broadcast([P, TT, NG, PG])
            el_g = el[:, :, :].rearrange("p i (g e) -> p i g e", g=NG)
            after(v.tensor_tensor(el_g, lg[:, :, NG:NL].rearrange("p i (g e) -> p i g e", g=NG), onehot_g, ALU.mult))
            after(v.tensor_scalar(g4[:, 1, :, :], g4[:, 2, :, :], BIG, -BIG, ALU.mult, ALU.add))
            after(v.tensor_tensor(el_g, el_g, g4[:, 1, :, :].unsqueeze(3).to_broadcast([P, TT, NG, PG]), ALU.add))
            first_max(el[:, :, :], NE, t4[:, 2, :], t4[:, 3, :], cand[:, :, :], oh1[:, :, :])
            after(v.scalar_tensor_tensor(out=el[:, :, :], in0=oh1[:, :, :], scalar=-2 * BIG, in1=el[:, :, :],
                                         op0=ALU.mult, op1=ALU.add))
            first_max(el[:, :, :], NE, t4[:, 4, :], t4[:, 5, :], cand[:, :, :], oh2[:, :, :])
            v.tensor_tensor(t4[:, 6, :], t4[:, 4, :], t4[:, 2, :], ALU.subtract).then_inc(ediff_ready, 1)
            after(v.tensor_tensor(routed[:, :, :], oh1[:, :, :], oh2[:, :, :], ALU.add))
            v.tensor_copy(routed_bf[:, :, :], routed[:, :, :]).then_inc(routed_ready, 1)
            dve.wait_ge(gexp_ready, 1)
            after(v.tensor_reduce(t4[:, 8, :], g4[:, 3, :, :], AX.X, ALU.add))
            dve.wait_ge(eexp_ready, 1)
            after(v.tensor_scalar(t4[:, 9, :], t4[:, 7, :], 1.0, None, ALU.add))
            after(v.tensor_tensor(t4[:, 9, :], t4[:, 9, :], t4[:, 8, :], ALU.mult))
            after(v.reciprocal(t4[:, 10, :], t4[:, 9, :]))
            after(v.tensor_tensor(t4[:, 11, :], t4[:, 10, :], t4[:, 7, :], ALU.mult))
            info_row = info[:, 0:NE, :, 0].rearrange("p e i -> p i e")
            info_gate = info[:, 0:NE, :, 1].rearrange("p e i -> p i e")
            after(v.tensor_tensor(cand[:, :, :], oh1[:, :, :], bc(t4[:, 10, :], NE), ALU.mult))
            after(v.tensor_tensor(el[:, :, :], oh2[:, :, :], bc(t4[:, 11, :], NE), ALU.mult))
            after(v.tensor_tensor(info_gate, cand[:, :, :], el[:, :, :], ALU.add))
            after(v.scalar_tensor_tensor(out=info_row, in0=oh2[:, :, :], scalar=2.0 * S, in1=bc(token[:, :], NE),
                                         op0=ALU.mult, op1=ALU.add))
            after(v.tensor_copy(info[:, NE, :, :], info[:, 0, :, :]))
            dve.wait_ge(places_psum, 1)
            after(v.scalar_tensor_tensor(out=cand[:, :, :], in0=bank[5][:, 0:TT * NE].rearrange("p (i e) -> p i e", i=TT),
                                         scalar=1.0, in1=routed[:, :, :], op0=ALU.add, op1=ALU.mult))
            after(v.tensor_scalar(place[:, 0:NE, :].rearrange("p e i -> p i e"), cand[:, :, :], -1.0, None, ALU.add))
            after(v.tensor_scalar(place[:, NE, :], place[:, 0, :], -float(C), None, ALU.add))
            after(v.tensor_reduce(t4[:, 0, 0:1], bank[5][:, TT * NE:(TT + 1) * NE], AX.X, ALU.max))
            v.tensor_scalar(rounds_i[:, :], t4[:, 0, 0:1], 1.0 / C, 0.5 - 0.5 / C, ALU.mult, ALU.add).then_inc(rounds_ready, 1)

            def make_pick(b, e):
                where = place[:, e, :] if isinstance(e, int) else place[:, bass.ds(e, 1), :].rearrange("p o i -> p (o i)")
                v.tensor_tensor(pick[:, b, :, :], iota[:, :].unsqueeze(1).to_broadcast([P, TT, C]), bc(where, C),
                                ALU.is_equal).then_inc(pick_ready, 1)

            def make_info(b, e):
                src = info[:, e, :, :] if isinstance(e, int) else \
                    info[:, bass.ds(e, 1), :, :].rearrange("p o i c -> p (o i) c")
                v.tensor_copy(pinfo[:, b, :, :], src).then_inc(pick_ready, 1)

            def take_info(b4):
                v.tensor_scalar(row_i[:, b4:b4 + 1], bank[1][:, 0:1], row_base[:, 0:1], None, ALU.add).then_inc(info_ready, 1)
                v.tensor_copy(gate_c[:, b4:b4 + 1], bank[1][:, 1:2]).then_inc(info_ready, 1)

            dve.wait_ge(rounds_ready, 1)
            make_pick(0, 0)
            make_info(0, 0)
            dve.wait_ge(info_psum, 1)
            take_info(0)
            dve.sem_inc(y_stored, 1)
            rounds = dve.value_load(rounds_i[0:1, 0:1], min_val=1, max_val=S // C)
            with dve.Fori(0, rounds) as r:
                with dve.Fori(0, NE // UNROLL) as g:
                    n0 = dve.snap((r * (NE // UNROLL) + g) * UNROLL)
                    for m in range(UNROLL):
                        b = m % 2
                        nxt = g * UNROLL + (m + 1)
                        make_pick(1 - b, nxt)
                        make_info(1 - b, nxt)
                        dve.wait_ge(sig_ready, n0 + (m + 1))
                        v.tensor_tensor(hid, sig, bank[2][:, 0:FE // 2], ALU.mult).then_inc(gated, 1)
                        dve.wait_ge(gated, n0 + (m + 1))
                        v.tensor_tensor(hid, hid, bank[2][:, FE // 2:FE], ALU.mult).then_inc(hidden_ready, 1)
                        dve.wait_ge(hT_psum, n0 + (m + 1))
                        v.tensor_copy(hT.rearrange("p (h j) c -> p j h c", h=2),
                                      bank[3][:, 0:FE // 2].rearrange("p (j h c) -> p j h c", j=2, h=2)).then_inc(hT_ready, 1)
                        dve.wait_ge(info_psum, n0 + (m + 2))
                        take_info((m + 1) % 4)
                        dve.wait_ge(y_psum, n0 + (m + 1))
                        dve.wait_ge(row_free, n0 + (m + 1))
                        v.tensor_scalar(yrow[:, b, :], bank[5][:, :], gate_c[:, m % 4:m % 4 + 1], None,
                                        ALU.mult).then_inc(y_stored, 1)
                dve.wait_ge(pick_ready, r * (2 * NE) + 2 * (NE + 1))
                v.tensor_scalar(place[:, :, :], place[:, :, :], -float(C), None, ALU.add).then_inc(next_round, 1)
                dve.wait_ge(next_round, r + 1)
            dve.wait_ge(pT_psum, 1)
            for k in range(KP):
                v.tensor_copy(pT[:, k, :], bank[4 + k][:, :]).then_inc(pT_ready, 1)
            for i in range(TT):
                dve.wait_ge(y_in[i], 32)
                after(v.tensor_tensor(y_back[:, i, 0, :], y_back[:, i, 0, :], y_back[:, i, 1, :], ALU.add))
                v.tensor_tensor(h1[:, i, :], h1[:, i, :], y_back[:, i, 0, :], ALU.add).then_inc(h2_ready, 1)
            dve.wait_ge(gain_in, 48)
            for i in range(TT):
                normalise(2 * TT + i, h1[:, i, :], u3[:, i, :])
            dve.wait_ge(h2_ready, TT)
            dve.wait_ge(ple_ready, 2 * TT)
            for i in range(TT):
                for h in range(2):
                    q = 2 * i + h
                    cols = slice(h * HALF, (h + 1) * HALF)
                    dve.wait_ge(pg_sig, q + 1)
                    after(v.tensor_tensor(psig[:, q % 2, :], psig[:, q % 2, :], ple[:, i, cols], ALU.mult))
                    v.tensor_tensor(h1[:, i, cols], h1[:, i, cols], psig[:, q % 2, :], ALU.add).then_inc(h3_ready, 1)
                dve.wait_ge(gain_in, 64)
                dve.wait_ge(h3_ready, 2 * i + 2)
                normalise(3 * TT + i, h1[:, i, :], fin[:, i, :])

        @block.tensor
        def _(pe):
            def mm(*a, **k):
                return nc.tensor.matmul(*a, **k)

            pe.wait_ge(const_ready, 1)
            pe.wait_ge(small_in, 16 * 6)
            nc.tensor.transpose(bank[0][:, 0:NV], vecs[0:NV, :], ident[0:NV, 0:NV]).then_inc(vec_psum, 1)

            def transpose_rows(q, src, banks):
                i, h = q // 2, q % 2
                if h == 0:
                    pe.wait_ge(norm_done, i + 1)
                if q % (2 * TT) >= 4:
                    pe.wait_ge(ut_ready, q - 3)
                for k in range(4):
                    ins = nc.tensor.transpose(bank[banks[q % 4]][:, k * P:(k + 1) * P],
                                              src[:, i % TT, (4 * h + k) * P:(4 * h + k + 1) * P], ident[:, :])
                ins.then_inc(ut_psum, 1)

            for q in range(2 * TT):
                transpose_rows(q, xin, (4, 5, 6, 7))
            pe.wait_ge(ut_ready, 2 * TT)

            def lru_gates(c):
                pe.wait_ge(conv_done, c + 1)
                if c >= 2:
                    pe.wait_ge(i_ready, c - 1)
                if c == 0:
                    pe.wait_ge(lru_in, 16 * 9)
                for w in range(2):
                    ins = mm(bank[4 + 2 * (c % 2) + w][:, :], diag[:, c, w, :], xc[:, c % 2, :], start=True, stop=True)
                ins.then_inc(gates_psum, 1)

            def mix(g):
                pe.wait_ge(pooled, g + 1)
                if g == 0:
                    pe.wait_ge(i_ready, NX)
                mm(bank[4 + g][:, :], wpool[:, g, :], xbp[:, g, PAD:W], start=True, stop=True).then_inc(mixed, 1)

            for t, (kind, c, n, blk) in enumerate(ztiles):
                if t == 0:
                    pe.wait_ge(prm_ready, 1)
                if blk == 0:
                    pe.wait_ge(slot_full[n], slots_at(n))
                if t >= 4:
                    before_kind, before_c = ztiles[t - 4][:2]
                    pe.wait_ge(z_free[before_kind], before_c + 1)
                w = wslot(n, KD)
                for k in range(KD):
                    ins = mm(bank[t % 4][:, :], w[:, k, blk * P:(blk + 1) * P], uT[:, k, :], start=(k == 0), stop=(k == KD - 1))
                ins.then_inc(z_ready, 1)
                if 2 <= t < NX + 2:
                    lru_gates(t - 2)
                if NZ - NB <= t:
                    mix(t - (NZ - NB))

            def product(out_, n, k_tiles, cols, rhs, done=None):
                w = wslot(n, KD) if k_tiles == KD else \
                    ring[:, n % SLOTS, 0:NB * HALF].rearrange("p (k f) -> p k f", k=NB)
                for k in range(k_tiles):
                    ins = mm(out_, w[:, k, cols], rhs[:, k, :], start=(k == 0), stop=(k == k_tiles - 1))
                return ins

            for j in range(KD):
                h, cols = j // 4, slice((j % 4) * P, (j % 4 + 1) * P)
                n = E_MERGE + 4 * h
                s = 4 * (j % 2)
                if j == 0:
                    pe.wait_ge(ya_used, NX)
                if j == 1:
                    pe.wait_ge(hb_ready, NB)
                if j >= 2:
                    pe.wait_ge(merged_ready, j - 1)
                if j % 4 == 0:
                    pe.wait_ge(slot_full[n % SLOTS], slots_at(n))
                    pe.wait_ge(slot_full[(n + 1) % SLOTS], slots_at(n + 1))
                product(bank[s][:, :], n, KD, cols, uT)
                product(bank[s + 1][:, :], n + 1, KD, cols, uT)
                if j % 4 == 0:
                    pe.wait_ge(slot_full[(n + 2) % SLOTS], slots_at(n + 2))
                    pe.wait_ge(slot_full[(n + 3) % SLOTS], slots_at(n + 3))
                if j == 0:
                    pe.wait_ge(hb_ready, NB)
                    pe.wait_ge(ha_ready, NX)
                product(bank[s + 2][:, :], n + 2, NB, cols, hb)
                product(bank[s + 3][:, :], n + 3, KD, cols, ha).then_inc(merge_psum, 1)
            for h in range(2):
                n = E_OUT + h
                pe.wait_ge(slot_full[n % SLOTS], slots_at(n))
                w = wslot(n, KD)
                for i in range(TT):
                    if h == 0 and i == 0:
                        pe.wait_ge(merged_ready, KD)
                    for k in range(KD):
                        ins = mm(bank[h * TT + i][:, :], merged[:, k, i * P:(i + 1) * P], w[:, k, :],
                                 start=(k == 0), stop=(k == KD - 1))
                    ins.then_inc(out_psum, 1)
            pe.wait_ge(h1_ready, 2 * TT)

            def logits(i):
                pe.wait_ge(ut_ready, 2 * (TT + i + 1))
                for k in range(KD):
                    ins = mm(bank[4][:, i * 64:i * 64 + NL], u2T[:, k, i * P:(i + 1) * P], wrt[:, k, :],
                             start=(k == 0), stop=(k == KD - 1))
                return ins

            for i in range(TT):
                transpose_rows(2 * (TT + i), u2, (0, 1, 2, 3))
                transpose_rows(2 * (TT + i) + 1, u2, (0, 1, 2, 3))
                if i >= 1:
                    logits(i - 1)
            logits(TT - 1).then_inc(logits_psum, 1)
            pe.wait_ge(routed_ready, 1)
            pe.wait_ge(const_ready, 8)
            for i in range(TT):
                dst = bank[5][:, i * NE:(i + 1) * NE]
                mm(dst, before[:, :], routed_bf[:, i, :], start=True, stop=(i == 0))
                for j in range(i):
                    mm(dst, ones[:, :], routed_bf[:, j, :], start=False, stop=(j == i - 1))
            for i in range(TT):
                ins = mm(bank[5][:, TT * NE:(TT + 1) * NE], ones[:, :], routed_bf[:, i, :], start=(i == 0), stop=(i == TT - 1))
            ins.then_inc(places_psum, 1)

            def gather(b):
                for i in range(TT):
                    for h in range(2):
                        ins = mm(bank[0][h * C:(h + 1) * C, :], pick[:, b, i, :], u2[:, i, h * HALF:(h + 1) * HALF],
                                 start=(i == 0), stop=(i == TT - 1))
                ins.then_inc(xrow_psum, 1)

            def gather_info(b):
                for i in range(TT):
                    for h in range(2):
                        ins = mm(bank[1][h * C:(h + 1) * C, 0:2], pick[:, b, i, :], pinfo[:, b, i, :],
                                 start=(i == 0), stop=(i == TT - 1))
                ins.then_inc(info_psum, 1)

            def transpose_x():
                for j in range(4):
                    ins = nc.tensor.transpose(bank[4][:, j * P:(j + 1) * P], xrow[:, j * P:(j + 1) * P], ident[:, :])
                ins.then_inc(xT_psum, 1)

            pe.wait_ge(pick_ready, 2)
            gather(0)
            gather_info(0)
            pe.wait_ge(xrow_ready, 1)
            transpose_x()
            rounds = pe.value_load(rounds_i[0:1, 0:1], min_val=1, max_val=S // C)
            with pe.Fori(0, rounds) as r:
                with pe.Fori(0, NE // UNROLL) as g:
                    it = pe.snap(r * (NE // UNROLL) + g)
                    n0 = pe.snap(it * UNROLL)
                    laps = pe.snap(it * (16 * 3 * UNROLL // SLOTS))
                    for m in range(UNROLL):
                        b = m % 2
                        pe.wait_ge(xT_ready, n0 + (m + 1))
                        for which in range(2):
                            n = E_EXP + 3 * m + which
                            pe.wait_ge(slot_full[n % SLOTS], laps + slots_at(n))
                            w = wslot(n, KD)
                            for k in range(KD):
                                for h in range(2):
                                    ins = mm(bank[2][h * C:(h + 1) * C, which * (FE // 2):(which + 1) * (FE // 2)],
                                             xT[:, b, k, :], w[:, k, h * (FE // 2):(h + 1) * (FE // 2)],
                                             start=(k == 0), stop=(k == KD - 1))
                            ins.then_inc(gate_up_psum if which else gate_psum, 1)
                        pe.wait_ge(pick_ready, n0 * 2 + 2 * (m + 2))
                        gather(1 - b)
                        pe.wait_ge(hidden_ready, n0 + (m + 1))
                        for j in range(2):
                            ins = nc.tensor.transpose(bank[3][:, j * P:(j + 1) * P], hid[:, j * P:(j + 1) * P], ident[:, :])
                        ins.then_inc(hT_psum, 1)
                        pe.wait_ge(info_ready, n0 * 2 + 2 * (m + 1))
                        gather_info(1 - b)
                        pe.wait_ge(xrow_ready, n0 + (m + 2))
                        transpose_x()
                        n = E_EXP + 3 * m + 2
                        pe.wait_ge(slot_full[n % SLOTS], laps + slots_at(n))
                        pe.wait_ge(y_stored, n0 + (m + 1))
                        pe.wait_ge(hT_ready, n0 + (m + 1))
                        w = wslot(n, KF)
                        for k in range(KF):
                            for h in range(2):
                                ins = mm(bank[5][h * C:(h + 1) * C, :], hT[:, k, :], w[:, k, h * HALF:(h + 1) * HALF],
                                         start=(k == 0), stop=(k == KF - 1))
                        ins.then_inc(y_psum, 1)

            last = pe.snap(rounds * (16 * 3 * NE // SLOTS))
            pe.wait_ge(y_stored, rounds * NE + 1)
            pe.wait_ge(xT_ready, rounds * NE + 1)
            pe.wait_ge(info_ready, rounds * (2 * NE) + 2)
            pe.wait_ge(slot_full[s0], last + slots_at(T_PLE) + 16)
            for i in range(TT):
                for k in range(KP):
                    ins = nc.tensor.transpose(bank[4 + k][:, i * P:(i + 1) * P], p_rows[:, i, k * P:(k + 1) * P], ident[:, :])
            ins.then_inc(pT_psum, 1)
            pe.wait_ge(pT_ready, KP)
            for i in range(TT):
                for h in range(2):
                    q = 2 * i + h
                    if q >= 4:
                        pe.wait_ge(ple_ready, q - 3)
                    for k in range(KP):
                        ins = mm(bank[q % 4][:, :], pT[:, k, i * P:(i + 1) * P], wple[:, k, h * HALF:(h + 1) * HALF],
                                 start=(k == 0), stop=(k == KP - 1))
                    ins.then_inc(ple_psum, 1)
            pe.wait_ge(ple_ready, 2 * TT)

            def ple_gate(i):
                pe.wait_ge(ut_ready, 2 * (2 * TT + i + 1))
                for h in range(2):
                    q = 2 * i + h
                    n = T_PG + h
                    if i == 0:
                        pe.wait_ge(slot_full[n % SLOTS], last + slots_at(n))
                    if q >= 4:
                        pe.wait_ge(pg_sig, q - 3)
                    for k in range(KD):
                        ins = mm(bank[q % 4][:, :], u3T[:, k, i * P:(i + 1) * P], wslot(n, KD)[:, k, :],
                                 start=(k == 0), stop=(k == KD - 1))
                    ins.then_inc(pg_psum, 1)

            for i in range(TT):
                transpose_rows(2 * (2 * TT + i), u3, (4, 5, 6, 7))
                transpose_rows(2 * (2 * TT + i) + 1, u3, (4, 5, 6, 7))
                if i >= 1:
                    ple_gate(i - 1)
            ple_gate(TT - 1)


_INS = ["x", "p", "norm_mix_g", "w_in", "conv_w", "conv_b", "w_rg", "b_rg", "w_ig", "b_ig", "lru_lambda", "w_pool",
        "pool_scale", "w_up_a", "w_up_b", "w_out", "norm_ffn_g", "w_router_group", "b_router_group", "w_router_expert",
        "b_router_expert", "w_gate_e", "w_up_e", "w_down_e", "norm_ple_g", "w_ple", "w_ple_gate", "final_norm_g"]
_OUTS = [((1, 512, 1024), "float32")]


def kernel(**inputs):
    import numpy as _np
    import concourse.bacc as _bacc
    from concourse import mybir as _mybir
    from concourse.bass_utils import run_bass_kernel_spmd as _run

    nc = _bacc.Bacc("TRN2", target_bir_lowering=False, num_devices=1)
    arrays, args = {}, []
    for name in _INS:
        a = _np.ascontiguousarray(inputs[name])
        arrays[f"in_{name}_dram"] = a
        args.append(nc.dram_tensor(f"in_{name}_dram", a.shape, _mybir.dt.from_np(a.dtype), kind="ExternalInput").ap())
    for i, (shape, dtype) in enumerate(_OUTS):
        dt = _mybir.dt.from_np(_np.dtype(dtype))
        args.append(nc.dram_tensor(f"out_{i}_dram", shape, dt, kind="ExternalOutput").ap())
    build(nc, *args)
    r = _run(nc, [arrays], core_ids=[0])
    got = tuple(r.results[0][f"out_{i}_dram"] for i in range(len(_OUTS)))
    return got[0]
```

```python
from contextlib import ExitStack

import concourse.bass as bass
from concourse import mybir

ALU = mybir.AluOpType
ACT = mybir.ActivationFunctionType
AX = mybir.AxisListType
F32 = mybir.dt.float32
F32R = mybir.dt.float32r
BF16 = mybir.dt.bfloat16
I32 = mybir.dt.int32
U32 = mybir.dt.uint32

P = 128
EPS = 1e-6
LRU_C = 8.0
WINDOWS = (2, 4, 8, 16)
GELU_CUBIC = 0.044715
GELU_SCALE = 1.5957691216057308
SLOTS = 8
SLOT = 4096
C = 64
UNROLL = 8
BIG = 1e30


def build(nc, x, p, norm_mix_g, w_in, conv_w, conv_b, w_rg, b_rg, w_ig, b_ig, lru_lambda, w_pool, pool_scale,
          w_up_a, w_up_b, w_out, norm_ffn_g, w_router_group, b_router_group, w_router_expert, b_router_expert,
          w_gate_e, w_up_e, w_down_e, norm_ple_g, w_ple, w_ple_gate, final_norm_g, out):
    _, S, D = x.shape
    TT = S // P
    KD = D // P
    NX = conv_w.shape[2] // P
    NB = w_up_b.shape[1] // P
    NG = b_router_group.shape[1]
    NE = b_router_expert.shape[1]
    PG = NE // NG
    FE = w_gate_e.shape[3]
    KF = FE // P
    KP = p.shape[3] // P
    NL = NG + NE
    HALF = D // 2
    FAR = 4096
    assert NE % UNROLL == 0 and (3 * UNROLL) % SLOTS == 0 and S == 512 and D == 1024

    blocks = [("xa", 0, KD), ("xb", 0, KD), ("ya", 0, KD), ("xa", 4, KD), ("ya", 4, KD)]
    for j in (0, 4):
        blocks += [("gb", j, KD), ("ub", j, NB), ("ga", j, KD), ("ua", j, KD)]
    blocks += [("out", 0, KD), ("out", TT, KD)]
    FIRST_MERGE = 5
    FIRST_OUT = len(blocks) - 2
    halves = [(n, h) for n, (_, _, kt) in enumerate(blocks) for h in range(kt // 4)]
    block_of = {}
    tiles = []
    for n, (kind, first, _) in enumerate(blocks):
        for i in range(4):
            block_of[kind, first + i] = n
            tiles.append((kind, first + i))
    low_engine = {(n, h): "pool" if n <= FIRST_MERGE and (n, h) != (0, 1) else "vector" for n, h in halves}
    position = {tile: t for t, tile in enumerate(tiles)}

    y_rows = nc.dram_tensor("expert_rows", [2 * S, D], F32, kind="Internal").ap()
    y_halves = y_rows.rearrange("r (h d) -> (r h) d", h=2)

    ctx = ExitStack()
    with ctx:
        def sb(name, shape, dt=F32):
            return ctx.enter_context(nc.sbuf_tensor(name, shape, dt))

        def sem(name):
            return ctx.enter_context(nc.semaphore(name))

        def sb_twin(name, words):
            offset = -(-nc.sbuf_base // 32) * 32
            return sb(name, [P, words]), [
                nc.alloc_sbuf_tensor_at(f"{name}_rounded{w // SLOT}", [P, min(SLOT, words - w)], F32R, offset=offset + 4 * w)
                for w in range(0, words, SLOT)]

        PAD = WINDOWS[-1]
        W = PAD + S
        ring_words, slot_r = sb_twin("ring", SLOTS * SLOT)
        ring = ring_words[:, :].rearrange("p (s w) -> p s w", s=SLOTS)
        r1, (r1_r,) = sb_twin("r1", KD * S)
        r2, (r2_r,) = sb_twin("r2", KD * S)
        r3, (r3_r,) = sb_twin("r3", KD * S)
        r4, (r4_r,) = sb_twin("r4", NB * W)
        gain = sb("gain", [P, D])
        junk = sb("junk", [P, D])

        h1 = r1[:, :].rearrange("p (i d) -> p i d", i=TT)
        xin = r2[:, :].rearrange("p (i d) -> p i d", i=TT)
        ha = r2[:, :].rearrange("p (c t) -> p c t", c=NX)
        u2 = r2[:, :].rearrange("p (i d) -> p i d", i=TT)
        merged = r3[:, :].rearrange("p (k t) -> p k t", k=KD)
        u2T = ring[:, 7, :].rearrange("p (k t) -> p k t", k=KD)
        diag = r3[:, 0:NX * 2 * P].rearrange("p (c w j) -> p c w j", c=NX, w=2)
        wpool = r3[:, NX * 2 * P:NX * 2 * P + NB * P].rearrange("p (g j) -> p g j", g=NB)
        scr = ring[:, 5:7, :].rearrange("p s w -> p (s w)")
        xc = scr[:, 12 * S:16 * S].rearrange("p (b t) -> p b t", b=4)
        lru_t = scr[:, 2 * S:4 * S].rearrange("p (b t) -> p b t", b=2)
        lru_i = scr[:, 4 * S:6 * S].rearrange("p (b t) -> p b t", b=2)
        lru_q = scr[:, 6 * S:8 * S].rearrange("p (b t) -> p b t", b=2)
        lru_a = scr[:, 8 * S:10 * S].rearrange("p (b t) -> p b t", b=2)
        gel = scr[:, 10 * S:12 * S].rearrange("p (b t) -> p b t", b=2)
        xbp = r4[:, :].rearrange("p (g t) -> p g t", g=NB)
        o = NX * 2 * P + NB * P
        wsum = r3[:, o:o + 2 * W].rearrange("p (b t) -> p b t", b=2)
        uT_high = r1_r[:, :].rearrange("p (k t) -> p k t", k=KD)
        uT_low = slot_r[0][:, :].rearrange("p (k t) -> p k t", k=KD)
        ha_high = slot_r[7][:, :].rearrange("p (c t) -> p c t", c=NX)
        ha_low = r2_r[:, :].rearrange("p (c t) -> p c t", c=NX)
        hb_high = r4_r[:, :].rearrange("p (g t) -> p g t", g=NB)[:, :, PAD:W]
        hb_low = slot_r[6][:, SLOT - NB * S:SLOT].rearrange("p (g t) -> p g t", g=NB)
        merged_high = slot_r[5][:, :].rearrange("p (k t) -> p k t", k=KD)
        merged_low = r3_r[:, :].rearrange("p (k t) -> p k t", k=KD)

        def block_half(slot, h):
            return slot.rearrange("p (k f) -> p k f", k=KD)[:, 4 * h:4 * h + 4, :]

        def high_half(n, h):
            return block_half(slot_r[1 + 2 * (n % 2)][:, :], h)

        def whole_half(n, h):
            return block_half(ring[:, 2 + 2 * (n % 2), :], h)

        def low_half(n, h):
            return block_half(slot_r[2 + 2 * (n % 2)][:, :], h)

        def gate_a(j):
            return (junk, gain)[j % 4 // 2][:, (j % 2) * S:(j % 2 + 1) * S]

        yrow = r4[:, 0:4 * HALF].rearrange("p (b d) -> p b d", b=4)
        xT = junk[:, :].rearrange("p (b k c) -> p b k c", b=2, k=KD)
        o = 0

        def r3_part(n):
            nonlocal o
            o += n
            return r3[:, o - n:o]

        xrow = r3_part(HALF)
        hT = r3_part(KF * C).rearrange("p (k c) -> p k c", k=KF)
        sig = r3_part(FE // 2)
        hid = r3_part(FE // 2)
        pick = r3_part(2 * TT * C).rearrange("p (b i c) -> p b i c", b=2, i=TT)
        pinfo = r3_part(2 * TT * 2).rearrange("p (b i c) -> p b i c", b=2, i=TT)

        vecs = sb("vecs", [P, P])
        NV = 8 * NX + NB
        prm = sb("prm", [P, NV])
        tap = lambda j, c: prm[:, j * NX + c:j * NX + c + 1]
        col = lambda row, c: prm[:, row * NX + c:row * NX + c + 1]
        lam = prm[:, 7 * NX:8 * NX]
        spt = sb("spt", [P, 6, NX])
        decay = sb("decay", [P, NX])
        ident = sb("ident", [P, P])
        before = sb("before", [P, P], BF16)
        ones = sb("ones", [P, P], BF16)
        iota = sb("iota", [P, C])
        token = sb("token", [P, TT])
        rcount = sb("rcount", [P, PAD])
        eps = sb("eps", [P, 1])
        ssq = sb("ssq", [P, 4 * TT])
        std = sb("std", [P, 4 * TT])
        rstd = sb("rstd", [P, 4 * TT])
        wrt = sb("wrt", [P, KD, NL])
        brt = sb("brt", [P, NL])
        lg = sb("lg", [P, TT, NL])
        g4 = sb("g4", [P, 4, TT, NG])
        t4 = sb("t4", [P, 12, TT])
        el = sb("el", [P, TT, NE])
        cand = sb("cand", [P, TT, NE])
        oh1 = sb("oh1", [P, TT, NE])
        oh2 = sb("oh2", [P, TT, NE])
        routed = sb("routed", [P, TT, NE])
        routed_bf = sb("routed_bf", [P, TT, NE], BF16)
        place = sb("place", [P, NE + 1, TT])
        info = sb("info", [P, NE + 1, TT, 2])
        rounds_i = sb("rounds_i", [P, 1], I32)
        row_base = sb("row_base", [P, 1])
        row_i = sb("row_i", [P, UNROLL], U32)
        gate_c = sb("gate_c", [P, UNROLL])

        bank = [ctx.enter_context(nc.psum_tensor(f"bank{b}", [P, 512], F32)) for b in range(8)]

        x_in = [sem(f"x_in{i}") for i in range(TT)]
        x_back = [sem(f"x_back{i}") for i in range(TT)]
        small_in = sem("small_in")
        lru_in = sem("lru_in")
        gain_in = sem("gain_in")
        slot_full = [sem(f"slot_full{s}") for s in range(SLOTS)]
        const_ready = sem("const_ready")
        pool_step = sem("pool_step")
        zero_ready = sem("zero_ready")
        vec_psum = sem("vec_psum")
        prm_ready = sem("prm_ready")
        decay_exp = sem("decay_exp")
        decay_arg = sem("decay_arg")
        decay_ready = sem("decay_ready")
        sq_done = sem("sq_done")
        std_done = sem("std_done")
        norm_done = sem("norm_done")
        dve_chain = sem("dve_chain")
        act_chain = sem("act_chain")
        ut_psum = sem("ut_psum")
        ut_ready = sem("ut_ready")
        half_in = [[sem(f"half_in{q}{h}") for h in range(2)] for q in range(2)]
        high_ready = sem("high_ready")
        low_ready = {"pool": sem("pool_low_ready"), "vector": sem("vector_low_ready")}
        ut_low = sem("ut_low")
        tile_done = sem("tile_done")
        conv_base = sem("conv_base")
        conv_done = sem("conv_done")
        gates_psum = sem("gates_psum")
        i_ready = sem("i_ready")
        tanh_ready = sem("tanh_ready")
        sqrt_free = sem("sqrt_free")
        sqrt_ready = sem("sqrt_ready")
        scan_done = sem("scan_done")
        xb_copied = sem("xb_copied")
        pooled = sem("pooled")
        mixed = sem("mixed")
        hb_ready = sem("hb_ready")
        sq_ready = sem("sq_ready")
        garg_ready = sem("garg_ready")
        gsig_ready = sem("gsig_ready")
        ya_used = sem("ya_used")
        ha_ready = sem("ha_ready")
        ha_high_ready = sem("ha_high_ready")
        ha_low_ready = sem("ha_low_ready")
        hb_low_ready = sem("hb_low_ready")
        gate_a_ready = sem("gate_a_ready")
        gate_b_ready = sem("gate_b_ready")
        up_a_used = sem("up_a_used")
        up_b_used = sem("up_b_used")
        merged_sum = sem("merged_sum")
        merged_high_ready = sem("merged_high_ready")
        merged_low_ready = sem("merged_low_ready")
        h1_ready = sem("h1_ready")
        logits_psum = sem("logits_psum")
        gdiff_ready = sem("gdiff_ready")
        gexp_ready = sem("gexp_ready")
        ediff_ready = sem("ediff_ready")
        eexp_ready = sem("eexp_ready")
        routed_ready = sem("routed_ready")
        places_psum = sem("places_psum")
        rounds_ready = sem("rounds_ready")
        next_round = sem("next_round")
        pick_ready = sem("pick_ready")
        xrow_psum = sem("xrow_psum")
        xrow_ready = sem("xrow_ready")
        xT_psum = sem("xT_psum")
        xT_ready = sem("xT_ready")
        info_psum = sem("info_psum")
        info_ready = sem("info_ready")
        gate_psum = sem("gate_psum")
        gate_up_psum = sem("gate_up_psum")
        sig_ready = sem("sig_ready")
        gated = sem("gated")
        hidden_ready = sem("hidden_ready")
        hT_psum = sem("hT_psum")
        hT_ready = sem("hT_ready")
        y_psum = sem("y_psum")
        y_stored = sem("y_stored")
        rows_taken = sem("rows_taken")
        scattered = [sem(f"scattered{b}") for b in range(4)]
        row_free = sem("row_free")
        y_in = [sem(f"y_in{i}") for i in range(TT)]
        pT_psum = sem("pT_psum")
        pT_ready = sem("pT_ready")
        ple_psum = sem("ple_psum")
        ple_ready = sem("ple_ready")
        h2_ready = sem("h2_ready")
        pg_high_ready = sem("pg_high_ready")
        pg_low_ready = [sem(f"pg_low_ready{h}") for h in range(2)]
        final_gain_in = sem("final_gain_in")
        pg_psum = sem("pg_psum")
        pg_sig = sem("pg_sig")
        h3_ready = sem("h3_ready")
        stored = sem("stored")

        def slots_at(m):
            return 16 * (m // SLOTS + 1)

        bank_read = {"xa": conv_done, "xb": xb_copied, "ya": ya_used, "ga": gate_a_ready, "ua": up_a_used,
                     "gb": gate_b_ready, "ub": up_b_used, "out": h1_ready}

        def split_high(act, n, h):
            act.wait_ge(half_in[n % 2][h], 16 * sum(1 for m, g in halves if m <= n and m % 2 == n % 2 and g == h))
            nc.scalar.activation(high_half(n, h), whole_half(n, h), ACT.Copy).then_inc(high_ready, 1)

        def split_low(eng, api, n, h):
            eng.wait_ge(high_ready, halves.index((n, h)) + 1)
            api.tensor_tensor(low_half(n, h), whole_half(n, h), high_half(n, h),
                              ALU.subtract).then_inc(low_ready[low_engine[n, h]], 1)

        def gate_low(eng, api, h):
            eng.wait_ge(pg_high_ready, h + 1)
            api.tensor_tensor(gate_part("low", h), gate_part("whole", h), gate_part("high", h),
                              ALU.subtract).then_inc(pg_low_ready[h], 1)

        def lows_at(n, h):
            at = [x for x in halves if low_engine[x] == low_engine[n, h]]
            return low_ready[low_engine[n, h]], at.index((n, h)) + 1

        def wslot(n, k):
            return ring[:, n % SLOTS, :].rearrange("p (k f) -> p k f", k=k)

        T_PLE = 0
        T_PG = T_PLE + 1
        s0 = T_PLE % SLOTS
        wple = ring[:, s0, 0:KP * D].rearrange("p (k n) -> p k n", k=KP)
        p_rows = ring[:, s0, KP * D:KP * D + TT * KP * P].rearrange("p (i n) -> p i n", i=TT)
        pT = ring[:, s0, KP * D + TT * KP * P:KP * D + 2 * TT * KP * P].rearrange("p (k t) -> p k t", k=KP)
        y_back = ring[:, 5:7, :].rearrange("p s (i k d) -> p (s i) k d", i=2, k=2)
        ple = ring[:, 7, :].rearrange("p (i d) -> p i d", i=TT)
        u3 = u2
        u3T_high = slot_r[0][:, :].rearrange("p (k t) -> p k t", k=KD)
        u3T_low = merged_low
        psig = r4[:, 0:2 * HALF].rearrange("p (b d) -> p b d", b=2)
        final_gain = r4[:, 2 * HALF:4 * HALF]

        def gate_part(kind, h):
            of = {"whole": ring[:, T_PG + h, :], "low": slot_r[T_PG + h][:, :], "high": slot_r[T_PG + 2 + h][:, :]}[kind]
            return of.rearrange("p (k f) -> p k f", k=KD)

        block = ctx.enter_context(nc.Block())

        @block.sync
        def _(sp):
            for i in range(TT):
                sp.dma_start(xin[:, i, :], x[0, i * P:(i + 1) * P, :]).then_inc(x_in[i], 16)

            def dense(w, k0, cols):
                return w[0].rearrange("(k p) n -> p k n", p=P)[:, k0:k0 + 4, cols:cols + 512]

            def small_loads():
                row = 0
                for v in (conv_w[0].rearrange("w (c p) -> (w c) p", p=P), conv_b[0].rearrange("(c p) -> c p", p=P),
                          b_rg[0].rearrange("(c p) -> c p", p=P), b_ig[0].rearrange("(c p) -> c p", p=P),
                          lru_lambda[0].rearrange("(c p) -> c p", p=P), pool_scale[0].rearrange("(c p) -> c p", p=P)):
                    sp.dma_start(vecs[row:row + v.shape[0], :], v).then_inc(small_in, 16)
                    row += v.shape[0]
                sp.wait_ge(zero_ready, 1)
                for w, src in enumerate((w_rg, w_ig)):
                    for odd in range(2):
                        sp.dma_start(diag[64 * odd:64 * odd + 64, :, w, 64 * odd:64 * odd + 64],
                                     src[0].rearrange("(c two) i j -> two i c j", two=2)[odd]).then_inc(lru_in, 16)
                sp.dma_start(wpool, w_pool[0].rearrange("g i j -> i g j")).then_inc(lru_in, 16)
                sp.dma_start(wrt[:, :, 0:NG], w_router_group[0].rearrange("(k p) n -> p k n", p=P)).then_inc(lru_in, 16)
                sp.dma_start(wrt[:, :, NG:NL], w_router_expert[0].rearrange("(k p) n -> p k n", p=P)).then_inc(lru_in, 16)
                sp.dma_start(brt[:, 0:NG], b_router_group[0].partition_broadcast(P)).then_inc(lru_in, 16)
                sp.dma_start(brt[:, NG:NL], b_router_expert[0].partition_broadcast(P)).then_inc(lru_in, 16)

            for n, h in halves:
                kind, first, _ = blocks[n]
                if (n, h) == (1, 0):
                    small_loads()
                if n >= 2:
                    sp.wait_ge(tile_done, 4 * (n - 1))
                w, col0 = {"xa": (w_in, 0), "ya": (w_in, 1024), "xb": (w_in, 2048), "ga": (w_in, 2560), "gb": (w_in, 3584),
                           "ua": (w_up_a, 0), "ub": (w_up_b, 0), "out": (w_out, 0)}[kind]
                sp.dma_start(whole_half(n, h), dense(w, 4 * h, col0 + first * P)).then_inc(half_in[n % 2][h], 16)
                if (n, h) == (FIRST_OUT, 1):
                    for i in range(TT):
                        sp.dma_start(h1[:, i, :], x[0, i * P:(i + 1) * P, :]).then_inc(x_back[i], 16)

            def load_expert(m, e):
                n, k, w = m, (KD, KD, KF)[m % 3], (w_gate_e, w_up_e, w_down_e)[m % 3]
                src = w[0, e].rearrange("(k p) n -> p k n", p=P) if isinstance(e, int) else \
                    w[0, bass.ds(e, 1)].rearrange("o (k p) n -> p (o k) n", p=P)
                sp.dma_start(wslot(n, k), src).then_inc(slot_full[n % SLOTS], 16)

            for m, n in ((0, FIRST_OUT), (6, FIRST_OUT), (3, FIRST_OUT + 1), (4, FIRST_OUT + 1),
                         (1, FIRST_OUT + 2), (2, FIRST_OUT + 2), (5, FIRST_OUT + 2), (7, FIRST_OUT + 2)):
                sp.wait_ge(tile_done, 4 * n)
                if m == 7:
                    sp.wait_ge(logits_psum, 1)
                load_expert(m, m // 3)
            sp.wait_ge(rounds_ready, 1)
            rounds = sp.value_load(rounds_i[0:1, 0:1], min_val=1, max_val=S // C)
            final = sp.snap(rounds * (NE // UNROLL) - 1)
            with sp.Fori(0, rounds) as r:
                with sp.Fori(0, NE // UNROLL) as g:
                    it = sp.snap(r * (NE // UNROLL) + g)
                    n0 = sp.snap(it * UNROLL)
                    after_body = sp.snap((g * UNROLL + UNROLL) % NE)

                    def wait_expert_read(m):
                        q = m - SLOTS
                        sp.wait_ge((gate_psum, gate_up_psum, y_psum)[q % 3], n0 + (q // 3 + 1))

                    for m in range(SLOTS, 3 * UNROLL):
                        wait_expert_read(m)
                        load_expert(m, g * UNROLL + m // 3)
                    with sp.If(it < final):
                        for m in range(3 * UNROLL, 3 * UNROLL + SLOTS):
                            wait_expert_read(m)
                            load_expert(m, after_body + (m // 3 - UNROLL))
                    with sp.Else():
                        wait_expert_read(3 * UNROLL)
                        sp.dma_start(wple, w_ple[0].rearrange("(k p) n -> p k n", p=P)).then_inc(slot_full[s0], 16)
                        sp.dma_start(p_rows, p[0, 0].rearrange("(i p) n -> p i n", p=P)).then_inc(slot_full[s0], 16)
                        wg = w_ple_gate[0].rearrange("(k p) n -> p k n", p=P)
                        for h in range(2):
                            wait_expert_read(3 * UNROLL + 1 + h)
                            sp.dma_start(wslot(T_PG + h, KD), wg[:, :, h * HALF:(h + 1) * HALF]).then_inc(
                                slot_full[(T_PG + h) % SLOTS], 16)
            sp.wait_ge(row_free, rounds * NE + 4)
            for i in range(TT):
                for k in range(2):
                    sp.dma_start(y_back[:, i, k, :], y_rows[k * S + i * P:k * S + (i + 1) * P, :]).then_inc(y_in[i], 16)
            sp.dma_start(final_gain, final_norm_g.partition_broadcast(P)).then_inc(final_gain_in, 16)
            for i in range(TT):
                sp.wait_ge(norm_done, 3 * TT + i + 1)
                sp.dma_start(out[0, i * P:(i + 1) * P, :], u3[:, i, :]).then_inc(stored, 16)
            sp.wait_ge(stored, 16 * TT)

        @block.gpsimd
        def _(pool):
            steps = 0

            def after(ins):
                nonlocal steps
                steps += 1
                ins.then_inc(pool_step, 1)
                pool.wait_ge(pool_step, steps)

            nc.gpsimd.memset(eps[:, :], EPS).then_inc(const_ready, 1)
            nc.gpsimd.memset(ident[:, :], 0.0).then_inc(pool_step, 1)
            nc.gpsimd.memset(before[:, :], 1.0).then_inc(pool_step, 1)
            steps = 2
            pool.wait_ge(pool_step, 2)
            nc.gpsimd.affine_select(out=ident[:, :], in_=ident[:, :], compare_op=ALU.not_equal, fill=1.0, base=0,
                                    pattern=[[-1, P]], channel_multiplier=1).then_inc(const_ready, 1)
            nc.gpsimd.memset(diag[:, :, :, :], 0.0).then_inc(zero_ready, 1)
            nc.gpsimd.affine_select(out=before[:, :], in_=before[:, :], compare_op=ALU.is_gt, fill=0.0, base=0,
                                    pattern=[[1, P]], channel_multiplier=-1).then_inc(const_ready, 1)
            nc.gpsimd.memset(ones[:, :], 1.0).then_inc(const_ready, 1)
            nc.gpsimd.iota(iota[:, :], pattern=[[1, C]], base=0, channel_multiplier=0,
                           allow_small_or_imprecise_dtypes=True).then_inc(const_ready, 1)
            nc.gpsimd.iota(token[:, :], pattern=[[2 * P, TT]], base=-FAR, channel_multiplier=2,
                           allow_small_or_imprecise_dtypes=True).then_inc(const_ready, 1)
            nc.gpsimd.memset(row_base[0:C, :], float(FAR)).then_inc(const_ready, 1)
            pool.wait_ge(const_ready, 7)
            nc.gpsimd.memset(row_base[C:P, :], float(FAR + 1)).then_inc(const_ready, 1)
            pool.wait_ge(const_ready, 8)
            nc.gpsimd.memset(xbp[:, :, 0:PAD], 0.0).then_inc(pool_step, 1)
            nc.gpsimd.memset(wsum[:, :, 0:PAD], 0.0).then_inc(pool_step, 1)
            steps += 2
            pool.wait_ge(pool_step, steps)

            def low(n):
                for h in range(2):
                    if low_engine[n, h] == "pool":
                        split_low(pool, nc.gpsimd, n, h)

            low(0)
            low(1)
            low(2)
            pool.wait_ge(prm_ready, 2)
            for g, w in enumerate(WINDOWS):
                if g == 2:
                    low(3)
                pool.wait_ge(xb_copied, g + 1)
                src, b, s = xbp[:, g, :], 0, 1
                while s < w:
                    dst = wsum[:, b, :]
                    after(nc.gpsimd.tensor_tensor(dst[:, PAD:W], src[:, PAD:W], src[:, PAD - s:W - s], ALU.add))
                    src, b, s = dst, 1 - b, 2 * s
                dst = wsum[:, b, :]
                after(nc.gpsimd.tensor_scalar(dst[:, PAD:W], src[:, PAD:W], 1.0 / w, None, ALU.mult))
                after(nc.gpsimd.tensor_tensor(dst[:, PAD:PAD + w], src[:, PAD:PAD + w], rcount[:, 0:w], ALU.mult))
                nc.gpsimd.tensor_tensor(xbp[:, g, PAD:W], dst[:, PAD:W], xbp[:, g, PAD:W],
                                        ALU.subtract).then_inc(pooled, 1)
                pool.wait_ge(pooled, g + 1)
            low(4)
            low(5)
            pool.wait_ge(rounds_ready, 1)
            rounds = pool.value_load(rounds_i[0:1, 0:1], min_val=1, max_val=S // C)
            pool.sem_inc(row_free, 4)
            last_row = pool.to_reg(4 * S - 1)

            def release_row(n0, m):
                pool.wait_ge(scattered[m % 4], n0 * 4 + 16 * (m // 4 + 1))
                pool.sem_inc(row_free, 1)

            with pool.Fori(0, rounds) as r:
                with pool.Fori(0, NE // UNROLL) as g:
                    n0 = pool.snap((r * (NE // UNROLL) + g) * UNROLL)
                    for m in range(UNROLL):
                        pool.wait_ge(y_stored, n0 + (m + 2))
                        pool.sem_inc(rows_taken, 1)
                        nc.gpsimd.indirect_dma_start(
                            out=y_halves, out_offset=bass.IndirectOffsetOnAxis(ap=row_i[:, m:m + 1], axis=0),
                            in_=yrow[:, m % 4, :], in_offset=None, bounds_check=last_row,
                            oob_is_err=False).then_inc(scattered[m % 4], 16)
                        if m >= 2:
                            release_row(n0, m - 2)
                    for m in (UNROLL - 2, UNROLL - 1):
                        release_row(n0, m)
            gate_low(pool, nc.gpsimd, 1)

        @block.scalar
        def _(act):
            steps = 0

            def after(ins):
                nonlocal steps
                steps += 1
                ins.then_inc(act_chain, 1)
                act.wait_ge(act_chain, steps)

            act.dma_start(gain[:, :], norm_mix_g[0].partition_broadcast(P)).then_inc(gain_in, 16)

            def norm(q, src):
                after(nc.scalar.activation(junk[:, :], src, ACT.Square, accum_out=ssq[:, q:q + 1]))
                nc.scalar.activation(std[:, q:q + 1], ssq[:, q:q + 1], ACT.Sqrt, bias=eps[:, 0:1],
                                     scale=1.0 / D).then_inc(std_done, 1)

            def copy_transposed(q, dst, banks):
                i, h = q // 2, q % 2
                act.wait_ge(ut_psum, q + 1)
                dst_k = dst[:, 4 * h:4 * h + 4, (i % TT) * P:(i % TT + 1) * P]
                nc.scalar.activation(dst_k, bank[banks[q % 4]][:, :].rearrange("p (k t) -> p k t", k=4),
                                     ACT.Copy).then_inc(ut_ready, 1)

            act.wait_ge(const_ready, 1)
            for i in range(TT):
                act.wait_ge(x_in[i], 16)
                norm(i, xin[:, i, :])
                if i >= 2:
                    split_high(act, 0, i - 2)
                if i >= 1:
                    copy_transposed(2 * i - 2, uT_high, (4, 5, 6, 7))
                    copy_transposed(2 * i - 1, uT_high, (4, 5, 6, 7))
            copy_transposed(2 * TT - 2, uT_high, (4, 5, 6, 7))
            copy_transposed(2 * TT - 1, uT_high, (4, 5, 6, 7))
            for h in range(2):
                split_high(act, 1, h)
            act.wait_ge(decay_arg, 1)
            nc.scalar.activation(spt[:, 1, :], spt[:, 0, :], ACT.Exp, scale=-1.0).then_inc(decay_exp, 1)
            act.wait_ge(decay_ready, 1)

            def conv_tap(c):
                t = position["xa", c]
                act.wait_ge(tile_done, t + 1)
                if c >= 4:
                    act.wait_ge(gates_psum, c - 3)
                    act.wait_ge(scan_done, c - 3)
                nc.scalar.activation(xc[:, c % 4, :], bank[t % 4][:, :], ACT.Identity, bias=col(4, c),
                                     scale=tap(3, c)).then_inc(conv_base, 1)

            def lru_gates(c):
                b = c % 2
                act.wait_ge(gates_psum, c + 1)
                if c >= 2:
                    act.wait_ge(scan_done, c - 1)
                after(nc.scalar.activation(lru_t[:, b, :], bank[4 + 2 * b][:, :], ACT.Sigmoid, bias=col(5, c)))
                nc.scalar.activation(lru_i[:, b, :], bank[5 + 2 * b][:, :], ACT.Sigmoid, bias=col(6, c)).then_inc(i_ready, 1)
                nc.scalar.activation(lru_t[:, b, :], lru_t[:, b, :], ACT.Tanh, scale=decay[:, c:c + 1]).then_inc(tanh_ready, 1)
                act.wait_ge(tanh_ready, c + 1)
                act.wait_ge(sqrt_free, c + 1)
                nc.scalar.activation(lru_t[:, b, :], lru_t[:, b, :], ACT.Sqrt, scale=-4.0).then_inc(sqrt_ready, 1)

            def pool_copy(g):
                t = position["xb", g]
                act.wait_ge(tile_done, t + 1)
                nc.scalar.activation(xbp[:, g, PAD:W], bank[t % 4][:, :], ACT.Copy).then_inc(xb_copied, 1)

            def gelu(c):
                t = position["ya", c]
                b = c % 2
                act.wait_ge(tile_done, t + 1)
                if c >= 2:
                    act.wait_ge(ya_used, c - 1)
                nc.scalar.activation(gel[:, b, :], bank[t % 4][:, :], ACT.Square).then_inc(sq_ready, 1)
                act.wait_ge(garg_ready, c + 1)
                nc.scalar.activation(gel[:, b, :], gel[:, b, :], ACT.Sigmoid, scale=GELU_SCALE).then_inc(gsig_ready, 1)

            def ha_split(c):
                act.wait_ge(ha_ready, c + 1)
                nc.scalar.activation(ha_high[:, c, :], ha[:, c, :], ACT.Copy).then_inc(ha_high_ready, 1)

            def pool_scaled(g):
                act.wait_ge(mixed, g + 1)
                nc.scalar.activation(hb_high[:, g, :], bank[4 + g][:, :], ACT.Copy,
                                     scale=prm[:, 8 * NX + g:8 * NX + g + 1]).then_inc(hb_ready, 1)

            def merge_gate(kind, j):
                t = position[kind, j]
                act.wait_ge(tile_done, t + 1)
                if kind == "gb":
                    nc.scalar.activation(merged[:, j, :], bank[t % 4][:, :], ACT.Sigmoid).then_inc(gate_b_ready, 1)
                else:
                    if j >= 4:
                        act.wait_ge(merged_sum, j - 3)
                    nc.scalar.activation(gate_a(j), bank[t % 4][:, :], ACT.Sigmoid).then_inc(gate_a_ready, 1)

            def merged_split(j):
                act.wait_ge(merged_sum, j + 1)
                nc.scalar.activation(merged_high[:, j, :], merged[:, j, :], ACT.Copy).then_inc(merged_high_ready, 1)

            for t, (kind, c) in enumerate(tiles):
                n = t // 4
                if n >= 1 and (n + 1, t % 4) in halves:
                    split_high(act, n + 1, t % 4)
                if n == FIRST_MERGE and t % 4 < 2:
                    for d in range(2):
                        pool_scaled(2 * (t % 4) + d)
                if n == FIRST_MERGE + 1:
                    for d in range(2):
                        ha_split(2 * (t % 4) + d)
                if kind == "xa":
                    conv_tap(c)
                if kind == "xb":
                    pool_copy(c)
                if kind == "ya":
                    gelu(c)
                if kind in ("ga", "gb"):
                    merge_gate(kind, c)
                if kind == "ua":
                    merged_split(c)
                if t >= 2 and tiles[t - 2][0] == "xa":
                    lru_gates(tiles[t - 2][1])
            act.dma_start(gain[:, :], norm_ffn_g[0].partition_broadcast(P)).then_inc(gain_in, 16)
            for i in range(TT):
                act.wait_ge(h1_ready, TT + i + 1)
                norm(TT + i, h1[:, i, :])
                if i >= 1:
                    copy_transposed(2 * (TT + i - 1), u2T, (4, 5, 6, 7))
                    copy_transposed(2 * (TT + i - 1) + 1, u2T, (4, 5, 6, 7))
            copy_transposed(4 * TT - 2, u2T, (4, 5, 6, 7))
            copy_transposed(4 * TT - 1, u2T, (4, 5, 6, 7))
            act.wait_ge(gdiff_ready, 1)
            nc.scalar.activation(g4[:, 3, :, :], g4[:, 0, :, :], ACT.Exp).then_inc(gexp_ready, 1)
            act.wait_ge(ediff_ready, 1)
            nc.scalar.activation(t4[:, 7, :], t4[:, 6, :], ACT.Exp).then_inc(eexp_ready, 1)

            act.wait_ge(norm_done, 2 * TT)
            act.dma_start(gain[:, :], norm_ple_g[0].partition_broadcast(P)).then_inc(gain_in, 16)
            act.wait_ge(rounds_ready, 1)
            rounds = act.value_load(rounds_i[0:1, 0:1], min_val=1, max_val=S // C)

            def copy_rows(n):
                act.wait_ge(xrow_psum, n)
                nc.scalar.activation(xrow, bank[0][:, :], ACT.Copy).then_inc(xrow_ready, 1)

            def copy_xT(b, n):
                act.wait_ge(xT_psum, n)
                nc.scalar.activation(xT[:, b, :, :].rearrange("p (h j) c -> p j h c", h=2),
                                     bank[4][:, :].rearrange("p (j h c) -> p j h c", j=4, h=2), ACT.Copy).then_inc(xT_ready, 1)

            copy_rows(1)
            copy_xT(0, 1)
            with act.Fori(0, rounds) as r:
                with act.Fori(0, NE // UNROLL) as g:
                    n0 = act.snap((r * (NE // UNROLL) + g) * UNROLL)
                    for m in range(UNROLL):
                        b = m % 2
                        act.wait_ge(gate_up_psum, n0 + (m + 1))
                        nc.scalar.activation(sig, bank[2][:, 0:FE // 2], ACT.Sigmoid).then_inc(sig_ready, 1)
                        copy_rows(n0 + (m + 2))
                        copy_xT(1 - b, n0 + (m + 2))
            last = act.snap(rounds * (16 * 3 * NE // SLOTS))
            for h in range(2):
                act.wait_ge(slot_full[T_PG + h], last + slots_at(T_PG + h))
                nc.scalar.activation(gate_part("high", h), gate_part("whole", h), ACT.Copy).then_inc(pg_high_ready, 1)

            def copy_ple(q):
                act.wait_ge(ple_psum, q + 1)
                nc.scalar.activation(ple[:, q // 2, (q % 2) * HALF:(q % 2 + 1) * HALF], bank[q % 4][:, :],
                                     ACT.Copy).then_inc(ple_ready, 1)

            for q in range(2 * TT - 2):
                copy_ple(q)
            for i in range(TT):
                act.wait_ge(h2_ready, i + 1)
                norm(2 * TT + i, h1[:, i, :])
                if i == 0:
                    copy_ple(2 * TT - 2)
                    copy_ple(2 * TT - 1)
                else:
                    copy_transposed(2 * (2 * TT + i - 1), u3T_high, (4, 5, 6, 7))
                    copy_transposed(2 * (2 * TT + i - 1) + 1, u3T_high, (4, 5, 6, 7))
            copy_transposed(6 * TT - 2, u3T_high, (4, 5, 6, 7))
            copy_transposed(6 * TT - 1, u3T_high, (4, 5, 6, 7))
            for i in range(TT):
                for h in range(2):
                    q = 2 * i + h
                    act.wait_ge(pg_psum, q + 1)
                    if q >= 2:
                        act.wait_ge(h3_ready, q - 1)
                    nc.scalar.activation(psig[:, q % 2, :], bank[q % 4][:, :], ACT.Sigmoid).then_inc(pg_sig, 1)
                act.wait_ge(h3_ready, 2 * i + 2)
                norm(3 * TT + i, h1[:, i, :])

        @block.vector
        def _(dve):
            v = nc.vector
            steps = 0

            def after(ins):
                nonlocal steps
                steps += 1
                ins.then_inc(dve_chain, 1)
                dve.wait_ge(dve_chain, steps)

            def normalise(q, src, dst, by=gain[:, :]):
                dve.wait_ge(std_done, q + 1)
                after(v.reciprocal(rstd[:, q:q + 1], std[:, q:q + 1]))
                v.scalar_tensor_tensor(out=dst, in0=src, scalar=rstd[:, q:q + 1], in1=by, op0=ALU.mult,
                                       op1=ALU.mult).then_inc(norm_done, 1)

            def uT_split(q, high=uT_high, low=uT_low):
                i, h = q // 2 % TT, q % 2
                dve.wait_ge(ut_ready, q + 1)
                part = slice(4 * h, 4 * h + 4), slice(i * P, (i + 1) * P)
                v.tensor_tensor(low[:, part[0], part[1]], bank[4 + q % 4][:, :].rearrange("p (k t) -> p k t", k=4),
                                high[:, part[0], part[1]], ALU.subtract).then_inc(ut_low, 1)

            dve.wait_ge(gain_in, 16)
            for i in range(TT):
                normalise(i, xin[:, i, :], xin[:, i, :])
                if i >= 1:
                    uT_split(2 * i - 2)
                    uT_split(2 * i - 1)
            uT_split(2 * TT - 2)
            uT_split(2 * TT - 1)
            split_low(dve, v, 0, 1)
            dve.wait_ge(const_ready, 8)
            dve.wait_ge(vec_psum, 1)
            v.tensor_copy(prm[:, :], bank[0][:, 0:NV]).then_inc(prm_ready, 1)
            dve.wait_ge(prm_ready, 1)
            after(v.tensor_scalar(rcount[:, :], iota[:, 0:PAD], 1.0, None, ALU.add))
            v.reciprocal(rcount[:, :], rcount[:, :]).then_inc(prm_ready, 1)
            after(v.tensor_scalar(spt[:, 2, :], lam, -1.0, None, ALU.mult))
            v.tensor_tensor(spt[:, 0, :], lam, spt[:, 2, :], ALU.max).then_inc(decay_arg, 1)
            after(v.tensor_scalar(spt[:, 2, :], spt[:, 2, :], 0.0, -LRU_C / 2, ALU.max, ALU.mult))
            dve.wait_ge(decay_exp, 1)
            after(v.tensor_scalar(spt[:, 3, :], spt[:, 1, :], 2.0, None, ALU.add))
            after(v.reciprocal(spt[:, 3, :], spt[:, 3, :]))
            after(v.tensor_tensor(spt[:, 3, :], spt[:, 3, :], spt[:, 1, :], ALU.mult))
            after(v.tensor_tensor(spt[:, 4, :], spt[:, 3, :], spt[:, 3, :], ALU.mult))
            after(v.tensor_scalar(spt[:, 5, :], spt[:, 4, :], 1.0 / 15, None, ALU.mult))
            for odd in (13, 11, 9, 7, 5, 3):
                after(v.scalar_tensor_tensor(out=spt[:, 5, :], in0=spt[:, 5, :], scalar=1.0 / odd, in1=spt[:, 4, :],
                                             op0=ALU.add, op1=ALU.mult))
            after(v.scalar_tensor_tensor(out=spt[:, 5, :], in0=spt[:, 5, :], scalar=1.0, in1=spt[:, 3, :],
                                         op0=ALU.add, op1=ALU.mult))
            v.scalar_tensor_tensor(out=decay[:, :], in0=spt[:, 5, :], scalar=-LRU_C, in1=spt[:, 2, :],
                                   op0=ALU.mult, op1=ALU.add).then_inc(decay_ready, 1)

            def conv(c):
                t = position["xa", c]
                z, y = bank[t % 4], xc[:, c % 4, :]
                dve.wait_ge(conv_base, c + 1)
                for d in (1, 2, 3):
                    ins = v.scalar_tensor_tensor(out=y[:, d:S], in0=z[:, 0:S - d], scalar=tap(3 - d, c), in1=y[:, d:S],
                                                 op0=ALU.mult, op1=ALU.add)
                    if d < 3:
                        after(ins)
                    else:
                        ins.then_inc(conv_done, 1)

            def lru(c):
                b = c % 2
                t, q, a, i = lru_t[:, b, :], lru_q[:, b, :], lru_a[:, b, :], lru_i[:, b, :]
                dve.wait_ge(tanh_ready, c + 1)
                v.tensor_scalar(q, t, -1.0, 1.0, ALU.mult, ALU.add).then_inc(sqrt_free, 1)
                dve.wait_ge(sqrt_free, c + 1)
                after(v.reciprocal(q, q))
                after(v.tensor_scalar(a, q, 2.0, -1.0, ALU.mult, ALU.add))
                after(v.tensor_tensor(i, i, xc[:, c % 4, :], ALU.mult))
                dve.wait_ge(sqrt_ready, c + 1)
                after(v.tensor_tensor(t, t, q, ALU.mult))
                after(v.tensor_tensor(t, t, i, ALU.mult))
                v.tensor_tensor_scan(ha[:, c, :], a, t, 0.0, ALU.mult, ALU.add).then_inc(scan_done, 1)

            def gelu(c):
                t, b = position["ya", c], c % 2
                y, w = bank[t % 4], gel[:, b, :]
                dve.wait_ge(sq_ready, c + 1)
                after(v.tensor_scalar(w, w, GELU_CUBIC, 1.0, ALU.mult, ALU.add))
                v.tensor_tensor(w, w, y[:, :], ALU.mult).then_inc(garg_ready, 1)
                dve.wait_ge(gsig_ready, c + 1)
                v.tensor_tensor(w, w, y[:, :], ALU.mult).then_inc(ya_used, 1)
                dve.wait_ge(ya_used, c + 1)
                dve.wait_ge(scan_done, c + 1)
                v.tensor_tensor(ha[:, c, :], ha[:, c, :], w, ALU.mult).then_inc(ha_ready, 1)

            def ha_split(c):
                dve.wait_ge(ha_high_ready, c + 1)
                v.tensor_tensor(ha_low[:, c, :], ha[:, c, :], ha_high[:, c, :], ALU.subtract).then_inc(ha_low_ready, 1)

            def pool_split(g):
                dve.wait_ge(hb_ready, g + 1)
                v.scalar_tensor_tensor(out=hb_low[:, g, :], in0=bank[4 + g][:, :],
                                       scalar=prm[:, 8 * NX + g:8 * NX + g + 1], in1=hb_high[:, g, :], op0=ALU.mult,
                                       op1=ALU.subtract).then_inc(hb_low_ready, 1)

            def merge_up(kind, j):
                t = position[kind, j]
                dve.wait_ge(tile_done, t + 1)
                if kind == "ub":
                    dve.wait_ge(gate_b_ready, j + 1)
                    v.tensor_tensor(merged[:, j, :], merged[:, j, :], bank[t % 4][:, :], ALU.mult).then_inc(up_b_used, 1)
                else:
                    dve.wait_ge(gate_a_ready, j + 1)
                    v.tensor_tensor(gate_a(j), gate_a(j), bank[t % 4][:, :], ALU.mult).then_inc(up_a_used, 1)
                    dve.wait_ge(up_a_used, j + 1)
                    v.tensor_tensor(merged[:, j, :], merged[:, j, :], gate_a(j), ALU.add).then_inc(merged_sum, 1)

            def merged_split(j):
                dve.wait_ge(merged_high_ready, j + 1)
                v.tensor_tensor(merged_low[:, j, :], merged[:, j, :], merged_high[:, j, :],
                                ALU.subtract).then_inc(merged_low_ready, 1)

            def residual(q):
                t, h, i = position["out", q], q // TT, q % TT
                dve.wait_ge(tile_done, t + 1)
                dve.wait_ge(x_back[i], 16)
                res = h1[:, i, h * HALF:(h + 1) * HALF]
                v.tensor_tensor(res, res, bank[t % 4][:, :], ALU.add).then_inc(h1_ready, 1)

            for t, (kind, c) in enumerate(tiles):
                n = t // 4
                if kind == "ya":
                    gelu(c)
                if kind == "xa":
                    conv(c)
                if t >= 2 and tiles[t - 2][0] == "xa":
                    lru(tiles[t - 2][1])
                if n == FIRST_MERGE and t % 4 < 2:
                    for d in range(2):
                        pool_split(2 * (t % 4) + d)
                if n == FIRST_MERGE + 1:
                    for d in range(2):
                        ha_split(2 * (t % 4) + d)
                if kind in ("ua", "ub"):
                    merge_up(kind, c)
                if t >= 1 and tiles[t - 1][0] == "ua":
                    merged_split(tiles[t - 1][1])
                if kind == "out":
                    residual(c)
                    if c == TT:
                        dve.wait_ge(gain_in, 32)
                    if c > TT:
                        normalise(c - 1, h1[:, c - 1 - TT, :], u2[:, c - 1 - TT, :])
                if low_engine.get((n + 1, t % 4)) == "vector":
                    split_low(dve, v, n + 1, t % 4)
            normalise(2 * TT - 1, h1[:, TT - 1, :], u2[:, TT - 1, :])

            def bc(ap, n):
                return ap.unsqueeze(2).to_broadcast([P, ap.shape[1], n])

            def first_max(scores, n, best, index, cands, onehot):
                after(v.tensor_reduce(best, scores, AX.X, ALU.max))
                after(v.tensor_tensor(cands, scores, bc(best, n), ALU.is_equal))
                after(v.scalar_tensor_tensor(out=cands, in0=cands, scalar=-float(C),
                                             in1=iota[:, 0:n].unsqueeze(1).to_broadcast([P, TT, n]),
                                             op0=ALU.mult, op1=ALU.add))
                after(v.tensor_reduce(index, cands, AX.X, ALU.min))
                after(v.tensor_tensor(onehot, cands, bc(index, n), ALU.is_equal))

            gl = lg[:, :, 0:NG]
            dve.wait_ge(logits_psum, 1)
            dve.wait_ge(lru_in, 16 * 9)
            after(v.tensor_tensor(lg[:, :, :], bank[0][:, 0:TT * 64].rearrange("p (i n) -> p i n", i=TT)[:, :, 0:NL],
                                  brt[:, :].unsqueeze(1).to_broadcast([P, TT, NL]), ALU.add))
            first_max(gl, NG, t4[:, 0, :], t4[:, 1, :], g4[:, 1, :, :], g4[:, 2, :, :])
            v.tensor_tensor(g4[:, 0, :, :], gl, bc(t4[:, 0, :], NG), ALU.subtract).then_inc(gdiff_ready, 1)
            onehot_g = g4[:, 2, :, :].unsqueeze(3).to_broadcast([P, TT, NG, PG])
            el_g = el[:, :, :].rearrange("p i (g e) -> p i g e", g=NG)
            after(v.tensor_tensor(el_g, lg[:, :, NG:NL].rearrange("p i (g e) -> p i g e", g=NG), onehot_g, ALU.mult))
            after(v.tensor_scalar(g4[:, 1, :, :], g4[:, 2, :, :], BIG, -BIG, ALU.mult, ALU.add))
            after(v.tensor_tensor(el_g, el_g, g4[:, 1, :, :].unsqueeze(3).to_broadcast([P, TT, NG, PG]), ALU.add))
            first_max(el[:, :, :], NE, t4[:, 2, :], t4[:, 3, :], cand[:, :, :], oh1[:, :, :])
            after(v.scalar_tensor_tensor(out=el[:, :, :], in0=oh1[:, :, :], scalar=-2 * BIG, in1=el[:, :, :],
                                         op0=ALU.mult, op1=ALU.add))
            first_max(el[:, :, :], NE, t4[:, 4, :], t4[:, 5, :], cand[:, :, :], oh2[:, :, :])
            v.tensor_tensor(t4[:, 6, :], t4[:, 4, :], t4[:, 2, :], ALU.subtract).then_inc(ediff_ready, 1)
            after(v.tensor_tensor(routed[:, :, :], oh1[:, :, :], oh2[:, :, :], ALU.add))
            v.tensor_copy(routed_bf[:, :, :], routed[:, :, :]).then_inc(routed_ready, 1)
            dve.wait_ge(gexp_ready, 1)
            after(v.tensor_reduce(t4[:, 8, :], g4[:, 3, :, :], AX.X, ALU.add))
            dve.wait_ge(eexp_ready, 1)
            after(v.tensor_scalar(t4[:, 9, :], t4[:, 7, :], 1.0, None, ALU.add))
            after(v.tensor_tensor(t4[:, 9, :], t4[:, 9, :], t4[:, 8, :], ALU.mult))
            after(v.reciprocal(t4[:, 10, :], t4[:, 9, :]))
            after(v.tensor_tensor(t4[:, 11, :], t4[:, 10, :], t4[:, 7, :], ALU.mult))
            info_row = info[:, 0:NE, :, 0].rearrange("p e i -> p i e")
            info_gate = info[:, 0:NE, :, 1].rearrange("p e i -> p i e")
            after(v.tensor_tensor(cand[:, :, :], oh1[:, :, :], bc(t4[:, 10, :], NE), ALU.mult))
            after(v.tensor_tensor(el[:, :, :], oh2[:, :, :], bc(t4[:, 11, :], NE), ALU.mult))
            after(v.tensor_tensor(info_gate, cand[:, :, :], el[:, :, :], ALU.add))
            after(v.scalar_tensor_tensor(out=info_row, in0=oh2[:, :, :], scalar=2.0 * S, in1=bc(token[:, :], NE),
                                         op0=ALU.mult, op1=ALU.add))
            after(v.tensor_copy(info[:, NE, :, :], info[:, 0, :, :]))
            dve.wait_ge(places_psum, 1)
            after(v.scalar_tensor_tensor(out=cand[:, :, :], in0=bank[5][:, 0:TT * NE].rearrange("p (i e) -> p i e", i=TT),
                                         scalar=1.0, in1=routed[:, :, :], op0=ALU.add, op1=ALU.mult))
            after(v.tensor_scalar(place[:, 0:NE, :].rearrange("p e i -> p i e"), cand[:, :, :], -1.0, None, ALU.add))
            after(v.tensor_scalar(place[:, NE, :], place[:, 0, :], -float(C), None, ALU.add))
            after(v.tensor_reduce(t4[:, 0, 0:1], bank[5][:, TT * NE:(TT + 1) * NE], AX.X, ALU.max))
            v.tensor_scalar(rounds_i[:, :], t4[:, 0, 0:1], 1.0 / C, 0.5 - 0.5 / C, ALU.mult, ALU.add).then_inc(rounds_ready, 1)

            def make_pick(b, e):
                where = place[:, e, :] if isinstance(e, int) else place[:, bass.ds(e, 1), :].rearrange("p o i -> p (o i)")
                v.tensor_tensor(pick[:, b, :, :], iota[:, :].unsqueeze(1).to_broadcast([P, TT, C]), bc(where, C),
                                ALU.is_equal).then_inc(pick_ready, 1)

            def make_info(b, e):
                src = info[:, e, :, :] if isinstance(e, int) else \
                    info[:, bass.ds(e, 1), :, :].rearrange("p o i c -> p (o i) c")
                v.tensor_copy(pinfo[:, b, :, :], src).then_inc(pick_ready, 1)

            def take_info(at):
                v.tensor_scalar(row_i[:, at:at + 1], bank[1][:, 0:1], row_base[:, 0:1], None, ALU.add).then_inc(info_ready, 1)
                v.tensor_copy(gate_c[:, at:at + 1], bank[1][:, 1:2]).then_inc(info_ready, 1)

            dve.wait_ge(rounds_ready, 1)
            make_pick(0, 0)
            make_info(0, 0)
            dve.wait_ge(info_psum, 1)
            take_info(0)
            dve.sem_inc(y_stored, 1)
            rounds = dve.value_load(rounds_i[0:1, 0:1], min_val=1, max_val=S // C)
            with dve.Fori(0, rounds) as r:
                with dve.Fori(0, NE // UNROLL) as g:
                    n0 = dve.snap((r * (NE // UNROLL) + g) * UNROLL)
                    for m in range(UNROLL):
                        b = m % 2
                        nxt = g * UNROLL + (m + 1)
                        make_pick(1 - b, nxt)
                        make_info(1 - b, nxt)
                        dve.wait_ge(sig_ready, n0 + (m + 1))
                        v.tensor_tensor(hid, sig, bank[2][:, 0:FE // 2], ALU.mult).then_inc(gated, 1)
                        dve.wait_ge(gated, n0 + (m + 1))
                        v.tensor_tensor(hid, hid, bank[2][:, FE // 2:FE], ALU.mult).then_inc(hidden_ready, 1)
                        dve.wait_ge(hT_psum, n0 + (m + 1))
                        v.tensor_copy(hT.rearrange("p (h j) c -> p j h c", h=2),
                                      bank[3][:, 0:FE // 2].rearrange("p (j h c) -> p j h c", j=2, h=2)).then_inc(hT_ready, 1)
                        dve.wait_ge(info_psum, n0 + (m + 2))
                        take_info((m + 1) % UNROLL)
                        dve.wait_ge(y_psum, n0 + (m + 1))
                        dve.wait_ge(row_free, n0 + (m + 1))
                        v.tensor_scalar(yrow[:, m % 4, :], bank[5][:, :], gate_c[:, m:m + 1], None,
                                        ALU.mult).then_inc(y_stored, 1)
                dve.wait_ge(pick_ready, r * (2 * NE) + 2 * (NE + 1))
                v.tensor_scalar(place[:, :, :], place[:, :, :], -float(C), None, ALU.add).then_inc(next_round, 1)
                dve.wait_ge(next_round, r + 1)
            dve.wait_ge(pT_psum, 1)
            for k in range(KP):
                v.tensor_copy(pT[:, k, :], bank[4 + k][:, :]).then_inc(pT_ready, 1)
            gate_low(dve, v, 0)

            def add_experts(i):
                dve.wait_ge(y_in[i], 32)
                after(v.tensor_tensor(y_back[:, i, 0, :], y_back[:, i, 0, :], y_back[:, i, 1, :], ALU.add))
                v.tensor_tensor(h1[:, i, :], h1[:, i, :], y_back[:, i, 0, :], ALU.add).then_inc(h2_ready, 1)

            add_experts(0)
            dve.wait_ge(gain_in, 48)
            for i in range(TT):
                if i + 1 < TT:
                    add_experts(i + 1)
                normalise(2 * TT + i, h1[:, i, :], u3[:, i, :])
                if i >= 1:
                    uT_split(2 * (2 * TT + i - 1), u3T_high, u3T_low)
                    uT_split(2 * (2 * TT + i - 1) + 1, u3T_high, u3T_low)
            uT_split(6 * TT - 2, u3T_high, u3T_low)
            uT_split(6 * TT - 1, u3T_high, u3T_low)
            dve.wait_ge(h2_ready, TT)
            dve.wait_ge(ple_ready, 2 * TT)
            dve.wait_ge(final_gain_in, 16)
            for i in range(TT):
                for h in range(2):
                    q = 2 * i + h
                    cols = slice(h * HALF, (h + 1) * HALF)
                    dve.wait_ge(pg_sig, q + 1)
                    after(v.tensor_tensor(psig[:, q % 2, :], psig[:, q % 2, :], ple[:, i, cols], ALU.mult))
                    v.tensor_tensor(h1[:, i, cols], h1[:, i, cols], psig[:, q % 2, :], ALU.add).then_inc(h3_ready, 1)
                dve.wait_ge(h3_ready, 2 * i + 2)
                normalise(3 * TT + i, h1[:, i, :], u3[:, i, :], final_gain)

        @block.tensor
        def _(pe):
            def mm(*a, **k):
                return nc.tensor.matmul(*a, **k)

            pe.wait_ge(const_ready, 2)

            def transpose_rows(q, src, banks):
                i, h = q // 2, q % 2
                if h == 0:
                    pe.wait_ge(norm_done, i + 1)
                if q % (2 * TT) >= 4:
                    norm_ = q // (2 * TT)
                    pe.wait_ge(*((ut_low, q - 3), (ut_ready, q - 3), (ut_low, q - 2 * TT - 3))[norm_])
                for k in range(4):
                    ins = nc.tensor.transpose(bank[banks[q % 4]][:, k * P:(k + 1) * P],
                                              src[:, i % TT, (4 * h + k) * P:(4 * h + k + 1) * P], ident[:, :])
                ins.then_inc(ut_psum, 1)

            for q in range(2 * TT):
                transpose_rows(q, xin, (4, 5, 6, 7))
            pe.wait_ge(small_in, 16 * 6)
            nc.tensor.transpose(bank[0][:, 0:NV], vecs[0:NV, :], ident[0:NV, 0:NV]).then_inc(vec_psum, 1)
            pe.wait_ge(ut_low, 2 * TT)

            def lru_gates(c):
                pe.wait_ge(conv_done, c + 1)
                if c >= 2:
                    pe.wait_ge(i_ready, c - 1)
                if c == 0:
                    pe.wait_ge(lru_in, 16 * 9)
                for w in range(2):
                    ins = mm(bank[4 + 2 * (c % 2) + w][:, :], diag[:, c, w, :], xc[:, c % 4, :], start=True, stop=True)
                ins.then_inc(gates_psum, 1)

            def mix(g):
                pe.wait_ge(pooled, g + 1)
                if g % 2 == 0:
                    pe.wait_ge(i_ready, NX - 1 + g // 2)
                mm(bank[4 + g][:, :], wpool[:, g, :], xbp[:, g, PAD:W], start=True, stop=True).then_inc(mixed, 1)

            moving = {"xa": (uT_high, uT_low), "xb": (uT_high, uT_low), "ya": (uT_high, uT_low), "ga": (uT_high, uT_low), "gb": (uT_high, uT_low),
                      "ua": (ha_high, ha_low), "ub": (hb_high, hb_low)}
            for t, (kind, c) in enumerate(tiles):
                n = block_of[kind, c]
                k_tiles = blocks[n][2]
                dst = bank[t % 4][:, :]
                if t == 0:
                    pe.wait_ge(prm_ready, 1)
                if t >= 4:
                    read_kind, read_c = tiles[t - 4]
                    pe.wait_ge(bank_read[read_kind], read_c + 1)
                if (kind, c) == ("ua", 0):
                    pe.wait_ge(ha_low_ready, NX)
                if (kind, c) == ("ub", 0):
                    pe.wait_ge(hb_low_ready, NB)
                for k in range(k_tiles):
                    if t % 4 == 0 and k % 4 == 0:
                        pe.wait_ge(*lows_at(n, k // 4))
                    if (kind, c) == ("out", 0):
                        pe.wait_ge(merged_low_ready, k + 1)
                    wh, wl = high_half(n, k // 4)[:, k % 4, :], low_half(n, k // 4)[:, k % 4, :]
                    if kind == "out":
                        cols = slice((c % TT) * P, (c % TT + 1) * P)
                        passes = ((merged_high[:, k, cols], wh), (merged_high[:, k, cols], wl), (merged_low[:, k, cols], wh))
                    else:
                        cols = slice((t % 4) * P, (t % 4 + 1) * P)
                        xh, xl = moving[kind][0][:, k, :], moving[kind][1][:, k, :]
                        passes = ((wh[:, cols], xh), (wh[:, cols], xl), (wl[:, cols], xh))
                    for p_, (still, stream) in enumerate(passes):
                        ins = mm(dst, still, stream, start=(k == 0 and p_ == 0), stop=(k == k_tiles - 1 and p_ == 2))
                ins.then_inc(tile_done, 1)
                if kind == "out" and c > TT + 1:
                    transpose_rows(2 * (c - 2), u2, (4, 5, 6, 7))
                    transpose_rows(2 * (c - 2) + 1, u2, (4, 5, 6, 7))
                if t >= 2 and tiles[t - 2][0] == "xa":
                    lru_gates(tiles[t - 2][1])
                if t // 4 == FIRST_MERGE - 1 and t % 4 >= 2:
                    mix(2 * (t % 4) - 4)
                    mix(2 * (t % 4) - 3)
            pe.wait_ge(h1_ready, 2 * TT)

            def logits(i):
                pe.wait_ge(ut_ready, 2 * (TT + i + 1))
                for k in range(KD):
                    ins = mm(bank[0][:, i * 64:i * 64 + NL], u2T[:, k, i * P:(i + 1) * P], wrt[:, k, :],
                             start=(k == 0), stop=(k == KD - 1))
                return ins

            logits(0)
            logits(1)
            transpose_rows(4 * TT - 4, u2, (4, 5, 6, 7))
            transpose_rows(4 * TT - 3, u2, (4, 5, 6, 7))
            logits(2)
            transpose_rows(4 * TT - 2, u2, (4, 5, 6, 7))
            transpose_rows(4 * TT - 1, u2, (4, 5, 6, 7))
            logits(TT - 1).then_inc(logits_psum, 1)
            pe.wait_ge(routed_ready, 1)
            pe.wait_ge(const_ready, 8)
            for i in range(TT):
                dst = bank[5][:, i * NE:(i + 1) * NE]
                mm(dst, before[:, :], routed_bf[:, i, :], start=True, stop=(i == 0))
                for j in range(i):
                    mm(dst, ones[:, :], routed_bf[:, j, :], start=False, stop=(j == i - 1))
            for i in range(TT):
                ins = mm(bank[5][:, TT * NE:(TT + 1) * NE], ones[:, :], routed_bf[:, i, :], start=(i == 0), stop=(i == TT - 1))
            ins.then_inc(places_psum, 1)

            def gather(b):
                for i in range(TT):
                    for h in range(2):
                        ins = mm(bank[0][h * C:(h + 1) * C, :], pick[:, b, i, :], u2[:, i, h * HALF:(h + 1) * HALF],
                                 start=(i == 0), stop=(i == TT - 1))
                ins.then_inc(xrow_psum, 1)

            def gather_info(b):
                for i in range(TT):
                    for h in range(2):
                        ins = mm(bank[1][h * C:(h + 1) * C, 0:2], pick[:, b, i, :], pinfo[:, b, i, :],
                                 start=(i == 0), stop=(i == TT - 1))
                ins.then_inc(info_psum, 1)

            def transpose_x():
                for j in range(4):
                    ins = nc.tensor.transpose(bank[4][:, j * P:(j + 1) * P], xrow[:, j * P:(j + 1) * P], ident[:, :])
                ins.then_inc(xT_psum, 1)

            pe.wait_ge(pick_ready, 2)
            gather(0)
            gather_info(0)
            pe.wait_ge(xrow_ready, 1)
            transpose_x()
            rounds = pe.value_load(rounds_i[0:1, 0:1], min_val=1, max_val=S // C)
            with pe.Fori(0, rounds) as r:
                with pe.Fori(0, NE // UNROLL) as g:
                    it = pe.snap(r * (NE // UNROLL) + g)
                    n0 = pe.snap(it * UNROLL)
                    laps = pe.snap(it * (16 * 3 * UNROLL // SLOTS))
                    for m in range(UNROLL):
                        b = m % 2
                        pe.wait_ge(xT_ready, n0 + (m + 1))
                        for which in range(2):
                            n = 3 * m + which
                            pe.wait_ge(slot_full[n % SLOTS], laps + slots_at(n))
                            w = wslot(n, KD)
                            for k in range(KD):
                                for h in range(2):
                                    ins = mm(bank[2][h * C:(h + 1) * C, which * (FE // 2):(which + 1) * (FE // 2)],
                                             xT[:, b, k, :], w[:, k, h * (FE // 2):(h + 1) * (FE // 2)],
                                             start=(k == 0), stop=(k == KD - 1))
                            ins.then_inc(gate_up_psum if which else gate_psum, 1)
                        pe.wait_ge(pick_ready, n0 * 2 + 2 * (m + 2))
                        gather(1 - b)
                        pe.wait_ge(hidden_ready, n0 + (m + 1))
                        for j in range(2):
                            ins = nc.tensor.transpose(bank[3][:, j * P:(j + 1) * P], hid[:, j * P:(j + 1) * P], ident[:, :])
                        ins.then_inc(hT_psum, 1)
                        pe.wait_ge(info_ready, n0 * 2 + 2 * (m + 1))
                        gather_info(1 - b)
                        pe.wait_ge(xrow_ready, n0 + (m + 2))
                        transpose_x()
                        n = 3 * m + 2
                        pe.wait_ge(slot_full[n % SLOTS], laps + slots_at(n))
                        pe.wait_ge(y_stored, n0 + (m + 1))
                        pe.wait_ge(hT_ready, n0 + (m + 1))
                        w = wslot(n, KF)
                        for k in range(KF):
                            for h in range(2):
                                ins = mm(bank[5][h * C:(h + 1) * C, :], hT[:, k, :], w[:, k, h * HALF:(h + 1) * HALF],
                                         start=(k == 0), stop=(k == KF - 1))
                        ins.then_inc(y_psum, 1)

            last = pe.snap(rounds * (16 * 3 * NE // SLOTS))
            pe.wait_ge(y_stored, rounds * NE + 1)
            pe.wait_ge(xT_ready, rounds * NE + 1)
            pe.wait_ge(info_ready, rounds * (2 * NE) + 2)
            pe.wait_ge(slot_full[s0], last + slots_at(T_PLE) + 16)
            for i in range(TT):
                for k in range(KP):
                    ins = nc.tensor.transpose(bank[4 + k][:, i * P:(i + 1) * P], p_rows[:, i, k * P:(k + 1) * P], ident[:, :])
            ins.then_inc(pT_psum, 1)
            pe.wait_ge(pT_ready, KP)
            for i in range(TT):
                for h in range(2):
                    q = 2 * i + h
                    if q >= 4:
                        pe.wait_ge(ple_ready, q - 3)
                    for k in range(KP):
                        ins = mm(bank[q % 4][:, :], pT[:, k, i * P:(i + 1) * P], wple[:, k, h * HALF:(h + 1) * HALF],
                                 start=(k == 0), stop=(k == KP - 1))
                    ins.then_inc(ple_psum, 1)
            pe.wait_ge(ple_ready, 2 * TT)

            def ple_gate(i, h):
                q = 2 * i + h
                pe.wait_ge(ut_low, 2 * (TT + i + 1))
                if i == 0:
                    pe.wait_ge(pg_low_ready[h], 1)
                if q >= 4:
                    pe.wait_ge(pg_sig, q - 3)
                cols = slice(i * P, (i + 1) * P)
                for k in range(KD):
                    wh, wl = gate_part("high", h)[:, k, :], gate_part("low", h)[:, k, :]
                    for p_, (still, stream) in enumerate(((u3T_high, wh), (u3T_high, wl), (u3T_low, wh))):
                        ins = mm(bank[q % 4][:, :], still[:, k, cols], stream, start=(k == 0 and p_ == 0),
                                 stop=(k == KD - 1 and p_ == 2))
                ins.then_inc(pg_psum, 1)

            for q in range(2 * TT):
                if q < TT:
                    transpose_rows(2 * (2 * TT + q), u3, (4, 5, 6, 7))
                    transpose_rows(2 * (2 * TT + q) + 1, u3, (4, 5, 6, 7))
                ple_gate(q // 2, q % 2)


_INS = ["x", "p", "norm_mix_g", "w_in", "conv_w", "conv_b", "w_rg", "b_rg", "w_ig", "b_ig", "lru_lambda", "w_pool",
        "pool_scale", "w_up_a", "w_up_b", "w_out", "norm_ffn_g", "w_router_group", "b_router_group", "w_router_expert",
        "b_router_expert", "w_gate_e", "w_up_e", "w_down_e", "norm_ple_g", "w_ple", "w_ple_gate", "final_norm_g"]
_OUTS = [((1, 512, 1024), "float32")]


def kernel(**inputs):
    import numpy as _np
    import concourse.bacc as _bacc
    from concourse import mybir as _mybir
    from concourse.bass_utils import run_bass_kernel_spmd as _run

    nc = _bacc.Bacc("TRN2", target_bir_lowering=False, num_devices=1)
    arrays, args = {}, []
    for name in _INS:
        a = _np.ascontiguousarray(inputs[name])
        arrays[f"in_{name}_dram"] = a
        args.append(nc.dram_tensor(f"in_{name}_dram", a.shape, _mybir.dt.from_np(a.dtype), kind="ExternalInput").ap())
    for i, (shape, dtype) in enumerate(_OUTS):
        dt = _mybir.dt.from_np(_np.dtype(dtype))
        args.append(nc.dram_tensor(f"out_{i}_dram", shape, dt, kind="ExternalOutput").ap())
    build(nc, *args)
    r = _run(nc, [arrays], core_ids=[0])
    got = tuple(r.results[0][f"out_{i}_dram"] for i in range(len(_OUTS)))
    return got[0]
```

```python
from contextlib import ExitStack

import concourse.bass as bass
from concourse import mybir

ALU = mybir.AluOpType
ACT = mybir.ActivationFunctionType
AX = mybir.AxisListType
F32 = mybir.dt.float32
F32R = mybir.dt.float32r
BF16 = mybir.dt.bfloat16
I32 = mybir.dt.int32
U32 = mybir.dt.uint32

P = 128
EPS = 1e-6
LRU_C = 8.0
WINDOWS = (2, 4, 8, 16)
GELU_CUBIC = 0.044715
GELU_SCALE = 1.5957691216057308
SLOTS = 8
SLOT = 4096
C = 64
UNROLL = 8
BIG = 1e30


def build(nc, x, p, norm_mix_g, w_in, conv_w, conv_b, w_rg, b_rg, w_ig, b_ig, lru_lambda, w_pool, pool_scale,
          w_up_a, w_up_b, w_out, norm_ffn_g, w_router_group, b_router_group, w_router_expert, b_router_expert,
          w_gate_e, w_up_e, w_down_e, norm_ple_g, w_ple, w_ple_gate, final_norm_g, out):
    _, S, D = x.shape
    TT = S // P
    KD = D // P
    NX = conv_w.shape[2] // P
    NB = w_up_b.shape[1] // P
    NG = b_router_group.shape[1]
    NE = b_router_expert.shape[1]
    PG = NE // NG
    FE = w_gate_e.shape[3]
    KF = FE // P
    KP = p.shape[3] // P
    NL = NG + NE
    HALF = D // 2
    FAR = 4096
    assert NE % UNROLL == 0 and (3 * UNROLL) % SLOTS == 0 and S == 512 and D == 1024

    blocks = [("xa", 0, KD), ("xb", 0, KD), ("ya", 0, KD), ("xa", 4, KD), ("ya", 4, KD)]
    for j in (0, 4):
        blocks += [("gb", j, KD), ("ub", j, NB), ("ga", j, KD), ("ua", j, KD)]
    blocks += [("out", 0, KD), ("out", TT, KD)]
    FIRST_MERGE = 5
    FIRST_OUT = len(blocks) - 2
    halves = [(n, h) for n, (_, _, kt) in enumerate(blocks) for h in range(kt // 4)]
    block_of = {}
    tiles = []
    for n, (kind, first, _) in enumerate(blocks):
        for i in range(4):
            block_of[kind, first + i] = n
            tiles.append((kind, first + i))
    low_engine = {(n, h): "pool" if n <= FIRST_MERGE and (n, h) != (0, 1) else "vector" for n, h in halves}
    position = {tile: t for t, tile in enumerate(tiles)}

    y_rows = nc.dram_tensor("expert_rows", [2 * S, D], F32, kind="Internal").ap()
    y_halves = y_rows.rearrange("r (h d) -> (r h) d", h=2)

    ctx = ExitStack()
    with ctx:
        def sb(name, shape, dt=F32):
            return ctx.enter_context(nc.sbuf_tensor(name, shape, dt))

        def sem(name):
            return ctx.enter_context(nc.semaphore(name))

        def sb_twin(name, words):
            offset = -(-nc.sbuf_base // 32) * 32
            return sb(name, [P, words]), [
                nc.alloc_sbuf_tensor_at(f"{name}_rounded{w // SLOT}", [P, min(SLOT, words - w)], F32R, offset=offset + 4 * w)
                for w in range(0, words, SLOT)]

        PAD = WINDOWS[-1]
        W = PAD + S
        ring_words, slot_r = sb_twin("ring", SLOTS * SLOT)
        ring = ring_words[:, :].rearrange("p (s w) -> p s w", s=SLOTS)
        r1, (r1_r,) = sb_twin("r1", KD * S)
        r2, (r2_r,) = sb_twin("r2", KD * S)
        r3, (r3_r,) = sb_twin("r3", KD * S)
        r4, (r4_r,) = sb_twin("r4", NB * W)
        gain = sb("gain", [P, D])
        junk = sb("junk", [P, D])

        h1 = r1[:, :].rearrange("p (i d) -> p i d", i=TT)
        xin = r2[:, :].rearrange("p (i d) -> p i d", i=TT)
        ha = r2[:, :].rearrange("p (c t) -> p c t", c=NX)
        u2 = r2[:, :].rearrange("p (i d) -> p i d", i=TT)
        merged = r3[:, :].rearrange("p (k t) -> p k t", k=KD)
        u2T = ring[:, 7, :].rearrange("p (k t) -> p k t", k=KD)
        diag = r3[:, 0:NX * 2 * P].rearrange("p (c w j) -> p c w j", c=NX, w=2)
        wpool = r3[:, NX * 2 * P:NX * 2 * P + NB * P].rearrange("p (g j) -> p g j", g=NB)
        scr = ring[:, 5:7, :].rearrange("p s w -> p (s w)")
        xc = scr[:, 12 * S:16 * S].rearrange("p (b t) -> p b t", b=4)
        lru_t = scr[:, 2 * S:4 * S].rearrange("p (b t) -> p b t", b=2)
        lru_i = scr[:, 4 * S:6 * S].rearrange("p (b t) -> p b t", b=2)
        lru_q = scr[:, 6 * S:8 * S].rearrange("p (b t) -> p b t", b=2)
        lru_a = scr[:, 8 * S:10 * S].rearrange("p (b t) -> p b t", b=2)
        gel = scr[:, 10 * S:12 * S].rearrange("p (b t) -> p b t", b=2)
        xbp = r4[:, :].rearrange("p (g t) -> p g t", g=NB)
        o = NX * 2 * P + NB * P
        wsum = r3[:, o:o + 2 * W].rearrange("p (b t) -> p b t", b=2)
        uT_high = r1_r[:, :].rearrange("p (k t) -> p k t", k=KD)
        uT_low = slot_r[0][:, :].rearrange("p (k t) -> p k t", k=KD)
        ha_high = slot_r[7][:, :].rearrange("p (c t) -> p c t", c=NX)
        ha_low = r2_r[:, :].rearrange("p (c t) -> p c t", c=NX)
        hb_high = r4_r[:, :].rearrange("p (g t) -> p g t", g=NB)[:, :, PAD:W]
        hb_low = slot_r[6][:, SLOT - NB * S:SLOT].rearrange("p (g t) -> p g t", g=NB)
        merged_high = slot_r[5][:, :].rearrange("p (k t) -> p k t", k=KD)
        merged_low = r3_r[:, :].rearrange("p (k t) -> p k t", k=KD)

        def block_half(slot, h):
            return slot.rearrange("p (k f) -> p k f", k=KD)[:, 4 * h:4 * h + 4, :]

        def high_half(n, h):
            return block_half(slot_r[1 + 2 * (n % 2)][:, :], h)

        def whole_half(n, h):
            return block_half(ring[:, 2 + 2 * (n % 2), :], h)

        def low_half(n, h):
            return block_half(slot_r[2 + 2 * (n % 2)][:, :], h)

        def gate_a(j):
            return (junk, gain)[j % 4 // 2][:, (j % 2) * S:(j % 2 + 1) * S]

        lgT = r4[:, 0:S]
        logit_parts = (slice(0, (TT - 1) * P), slice((TT - 1) * P, S))
        yrow = r4[:, 0:4 * HALF].rearrange("p (b d) -> p b d", b=4)
        xT = junk[:, :].rearrange("p (b k c) -> p b k c", b=2, k=KD)
        o = 0

        def r3_part(n):
            nonlocal o
            o += n
            return r3[:, o - n:o]

        xrow = r3_part(HALF)
        hT = r3_part(KF * C).rearrange("p (k c) -> p k c", k=KF)
        sig = r3_part(FE // 2)
        hid = r3_part(FE // 2)
        pick = r3_part(2 * TT * C).rearrange("p (b i c) -> p b i c", b=2, i=TT)
        pinfo = r3_part(2 * TT * 2).rearrange("p (b i c) -> p b i c", b=2, i=TT)

        vecs = sb("vecs", [P, P])
        NV = 8 * NX + NB
        prm = sb("prm", [P, NV])
        tap = lambda j, c: prm[:, j * NX + c:j * NX + c + 1]
        col = lambda row, c: prm[:, row * NX + c:row * NX + c + 1]
        lam = prm[:, 7 * NX:8 * NX]
        spt = sb("spt", [P, 6, NX])
        decay = sb("decay", [P, NX])
        ident = sb("ident", [P, P])
        before = sb("before", [P, P], BF16)
        ones = sb("ones", [P, P], BF16)
        iota = sb("iota", [P, C])
        token = sb("token", [P, TT])
        rcount = sb("rcount", [P, PAD])
        eps = sb("eps", [P, 1])
        ssq = sb("ssq", [P, 4 * TT])
        std = sb("std", [P, 4 * TT])
        rstd = sb("rstd", [P, 4 * TT])
        wrt = sb("wrt", [P, KD, NL])
        brt = sb("brt", [P, NL])
        lg = sb("lg", [P, TT, NL])
        add_halves = sb("add_halves", [P, NL])
        g4 = sb("g4", [P, 4, TT, NG])
        t4 = sb("t4", [P, 12, TT])
        el = sb("el", [P, TT, NE])
        cand = sb("cand", [P, TT, NE])
        oh1 = sb("oh1", [P, TT, NE])
        oh2 = sb("oh2", [P, TT, NE])
        routed = sb("routed", [P, TT, NE])
        routed_bf = sb("routed_bf", [P, TT, NE], BF16)
        place = sb("place", [P, NE + 1, TT])
        info = sb("info", [P, NE + 1, TT, 2])
        rounds_i = sb("rounds_i", [P, 1], I32)
        row_base = sb("row_base", [P, 1])
        row_i = sb("row_i", [P, UNROLL], U32)
        gate_c = sb("gate_c", [P, UNROLL])

        bank = [ctx.enter_context(nc.psum_tensor(f"bank{b}", [P, 512], F32)) for b in range(8)]

        x_in = [sem(f"x_in{i}") for i in range(TT)]
        x_back = [sem(f"x_back{i}") for i in range(TT)]
        small_in = sem("small_in")
        lru_in = sem("lru_in")
        gain_in = sem("gain_in")
        slot_full = [sem(f"slot_full{s}") for s in range(SLOTS)]
        const_ready = sem("const_ready")
        pool_step = sem("pool_step")
        zero_ready = sem("zero_ready")
        vec_psum = sem("vec_psum")
        prm_ready = sem("prm_ready")
        decay_exp = sem("decay_exp")
        decay_arg = sem("decay_arg")
        decay_ready = sem("decay_ready")
        std_done = sem("std_done")
        norm_done = sem("norm_done")
        dve_chain = sem("dve_chain")
        act_chain = sem("act_chain")
        ut_psum = sem("ut_psum")
        ut_ready = sem("ut_ready")
        half_in = [[sem(f"half_in{q}{h}") for h in range(2)] for q in range(2)]
        high_ready = sem("high_ready")
        low_ready = {"pool": sem("pool_low_ready"), "vector": sem("vector_low_ready")}
        ut_low = sem("ut_low")
        tile_done = sem("tile_done")
        conv_base = sem("conv_base")
        conv_done = sem("conv_done")
        gates_psum = sem("gates_psum")
        i_ready = sem("i_ready")
        tanh_ready = sem("tanh_ready")
        sqrt_free = sem("sqrt_free")
        sqrt_ready = sem("sqrt_ready")
        scan_done = sem("scan_done")
        xb_copied = sem("xb_copied")
        pooled = sem("pooled")
        mixed = sem("mixed")
        hb_ready = sem("hb_ready")
        sq_ready = sem("sq_ready")
        garg_ready = sem("garg_ready")
        gsig_ready = sem("gsig_ready")
        ya_used = sem("ya_used")
        ha_ready = sem("ha_ready")
        ha_high_ready = sem("ha_high_ready")
        ha_low_ready = sem("ha_low_ready")
        hb_low_ready = sem("hb_low_ready")
        gate_a_ready = sem("gate_a_ready")
        gate_b_ready = sem("gate_b_ready")
        up_a_used = sem("up_a_used")
        up_b_used = sem("up_b_used")
        merged_sum = sem("merged_sum")
        merged_high_ready = sem("merged_high_ready")
        merged_low_ready = sem("merged_low_ready")
        h1_ready = sem("h1_ready")
        lgT_psum = sem("lgT_psum")
        lgT_cleared = sem("lgT_cleared")
        lgT_even_ready = sem("lgT_even_ready")
        lgT_odd_ready = sem("lgT_odd_ready")
        logits_psum = sem("logits_psum")
        gdiff_ready = sem("gdiff_ready")
        gexp_ready = sem("gexp_ready")
        ediff_ready = sem("ediff_ready")
        eexp_ready = sem("eexp_ready")
        routed_ready = sem("routed_ready")
        places_psum = sem("places_psum")
        rounds_ready = sem("rounds_ready")
        next_round = sem("next_round")
        pick_ready = sem("pick_ready")
        xrow_psum = sem("xrow_psum")
        xrow_ready = sem("xrow_ready")
        xT_psum = sem("xT_psum")
        xT_ready = sem("xT_ready")
        info_psum = sem("info_psum")
        info_ready = sem("info_ready")
        gate_psum = sem("gate_psum")
        gate_up_psum = sem("gate_up_psum")
        sig_ready = sem("sig_ready")
        gated = sem("gated")
        hidden_ready = sem("hidden_ready")
        hT_psum = sem("hT_psum")
        hT_ready = sem("hT_ready")
        y_psum = sem("y_psum")
        y_stored = sem("y_stored")
        rows_taken = sem("rows_taken")
        scattered = [sem(f"scattered{b}") for b in range(4)]
        row_free = sem("row_free")
        y_in = [[sem(f"y_in{k}_{i}") for i in range(TT)] for k in range(2)]
        pT_psum = sem("pT_psum")
        pT1_ready = sem("pT1_ready")
        pT0_ready = sem("pT0_ready")
        ple_psum = sem("ple_psum")
        ple_ready = sem("ple_ready")
        h2_ready = sem("h2_ready")
        pg_high_ready = sem("pg_high_ready")
        pg_low_ready = [sem(f"pg_low_ready{step}") for step in range(3)]
        final_gain_in = sem("final_gain_in")
        pg_psum = sem("pg_psum")
        pg_sig = sem("pg_sig")
        h3_ready = sem("h3_ready")
        final_ready = sem("final_ready")
        stored = sem("stored")

        def slots_at(m):
            return 16 * (m // SLOTS + 1)

        bank_read = {"xa": conv_done, "xb": xb_copied, "ya": ya_used, "ga": gate_a_ready, "ua": up_a_used,
                     "gb": gate_b_ready, "ub": up_b_used, "out": h1_ready}

        def split_high(act, n, h):
            act.wait_ge(half_in[n % 2][h], 16 * sum(1 for m, g in halves if m <= n and m % 2 == n % 2 and g == h))
            nc.scalar.activation(high_half(n, h), whole_half(n, h), ACT.Copy).then_inc(high_ready, 1)

        def split_low(eng, api, n, h):
            eng.wait_ge(high_ready, halves.index((n, h)) + 1)
            api.tensor_tensor(low_half(n, h), whole_half(n, h), high_half(n, h),
                              ALU.subtract).then_inc(low_ready[low_engine[n, h]], 1)

        gate_steps = ((0, slice(0, KD)), (1, slice(0, KD // 2)), (1, slice(KD // 2, KD)))

        def gate_low(eng, api, step):
            h, ks = gate_steps[step]
            eng.wait_ge(pg_high_ready, step + 1)
            api.tensor_tensor(gate_part("low", h)[:, ks, :], gate_part("whole", h)[:, ks, :], gate_part("high", h)[:, ks, :],
                              ALU.subtract).then_inc(pg_low_ready[step], 1)

        def lows_at(n, h):
            at = [x for x in halves if low_engine[x] == low_engine[n, h]]
            return low_ready[low_engine[n, h]], at.index((n, h)) + 1

        def wslot(n, k):
            return ring[:, n % SLOTS, :].rearrange("p (k f) -> p k f", k=k)

        T_PLE = 0
        T_PG = T_PLE + 1
        s0 = T_PLE % SLOTS
        wple = ring[:, s0, 0:KP * D].rearrange("p (k n) -> p k n", k=KP)
        p_rows = ring[:, s0, KP * D:KP * D + TT * KP * P].rearrange("p (i n) -> p i n", i=TT)
        pT = ring[:, s0, KP * D + TT * KP * P:KP * D + 2 * TT * KP * P].rearrange("p (k t) -> p k t", k=KP)
        y_back = ring[:, 5:7, :].rearrange("p s (i k d) -> p (s i) k d", i=2, k=2)
        ple = ring[:, 7, :].rearrange("p (i d) -> p i d", i=TT)
        u3 = u2
        u3T_high = slot_r[0][:, :].rearrange("p (k t) -> p k t", k=KD)
        u3T_low = merged_low
        psig = r4[:, 0:2 * HALF].rearrange("p (b d) -> p b d", b=2)
        final_gain = r4[:, 2 * HALF:4 * HALF]

        def ple_bank(q):
            return bank[q % 6]

        def gate_part(kind, h):
            of = {"whole": ring[:, T_PG + h, :], "low": slot_r[T_PG + h][:, :], "high": slot_r[T_PG + 2 + h][:, :]}[kind]
            return of.rearrange("p (k f) -> p k f", k=KD)

        block = ctx.enter_context(nc.Block())

        @block.sync
        def _(sp):
            for i in range(TT):
                sp.dma_start(xin[:, i, :], x[0, i * P:(i + 1) * P, :]).then_inc(x_in[i], 16)

            def dense(w, k0, cols):
                return w[0].rearrange("(k p) n -> p k n", p=P)[:, k0:k0 + 4, cols:cols + 512]

            def small_loads():
                row = 0
                for v in (conv_w[0].rearrange("w (c p) -> (w c) p", p=P), conv_b[0].rearrange("(c p) -> c p", p=P),
                          b_rg[0].rearrange("(c p) -> c p", p=P), b_ig[0].rearrange("(c p) -> c p", p=P),
                          lru_lambda[0].rearrange("(c p) -> c p", p=P), pool_scale[0].rearrange("(c p) -> c p", p=P)):
                    sp.dma_start(vecs[row:row + v.shape[0], :], v).then_inc(small_in, 16)
                    row += v.shape[0]
                sp.wait_ge(zero_ready, 1)
                for w, src in enumerate((w_rg, w_ig)):
                    for odd in range(2):
                        sp.dma_start(diag[64 * odd:64 * odd + 64, :, w, 64 * odd:64 * odd + 64],
                                     src[0].rearrange("(c two) i j -> two i c j", two=2)[odd]).then_inc(lru_in, 16)
                sp.dma_start(wpool, w_pool[0].rearrange("g i j -> i g j")).then_inc(lru_in, 16)
                sp.dma_start(wrt[:, :, 0:NG], w_router_group[0].rearrange("(k p) n -> p k n", p=P)).then_inc(lru_in, 16)
                sp.dma_start(wrt[:, :, NG:NL], w_router_expert[0].rearrange("(k p) n -> p k n", p=P)).then_inc(lru_in, 16)
                sp.dma_start(brt[:, 0:NG], b_router_group[0].partition_broadcast(P)).then_inc(lru_in, 16)
                sp.dma_start(brt[:, NG:NL], b_router_expert[0].partition_broadcast(P)).then_inc(lru_in, 16)

            for n, h in halves:
                kind, first, _ = blocks[n]
                if (n, h) == (1, 0):
                    small_loads()
                if n >= 2:
                    sp.wait_ge(tile_done, 4 * (n - 1))
                w, tile0 = {"xa": (w_in, 0), "ya": (w_in, NX), "xb": (w_in, 2 * NX), "ga": (w_in, 2 * NX + NB),
                            "gb": (w_in, 2 * NX + NB + KD), "ua": (w_up_a, 0), "ub": (w_up_b, 0), "out": (w_out, 0)}[kind]
                sp.dma_start(whole_half(n, h), dense(w, 4 * h, (tile0 + first) * P)).then_inc(half_in[n % 2][h], 16)
                if (n, h) == (FIRST_OUT, 1):
                    for i in range(TT):
                        sp.dma_start(h1[:, i, :], x[0, i * P:(i + 1) * P, :]).then_inc(x_back[i], 16)

            def load_expert(m, e):
                n, k, w = m, (KD, KD, KF)[m % 3], (w_gate_e, w_up_e, w_down_e)[m % 3]
                src = w[0, e].rearrange("(k p) n -> p k n", p=P) if isinstance(e, int) else \
                    w[0, bass.ds(e, 1)].rearrange("o (k p) n -> p (o k) n", p=P)
                sp.dma_start(wslot(n, k), src).then_inc(slot_full[n % SLOTS], 16)

            for m, n in ((0, FIRST_OUT), (6, FIRST_OUT), (3, FIRST_OUT + 1), (4, FIRST_OUT + 1),
                         (1, FIRST_OUT + 2), (2, FIRST_OUT + 2), (5, FIRST_OUT + 2), (7, FIRST_OUT + 2)):
                sp.wait_ge(tile_done, 4 * n)
                if m == 7:
                    sp.wait_ge(logits_psum, 1)
                load_expert(m, m // 3)
            sp.wait_ge(rounds_ready, 1)
            wg = w_ple_gate[0].rearrange("(k p) n -> p k n", p=P)
            rounds = sp.value_load(rounds_i[0:1, 0:1], min_val=1, max_val=S // C)
            final = sp.snap(rounds * (NE // UNROLL) - 1)
            with sp.Fori(0, rounds) as r:
                with sp.Fori(0, NE // UNROLL) as g:
                    it = sp.snap(r * (NE // UNROLL) + g)
                    n0 = sp.snap(it * UNROLL)
                    after_body = sp.snap((g * UNROLL + UNROLL) % NE)

                    def wait_expert_read(m):
                        q = m - SLOTS
                        sp.wait_ge((gate_psum, gate_up_psum, y_psum)[q % 3], n0 + (q // 3 + 1))

                    for m in range(SLOTS, 3 * UNROLL):
                        wait_expert_read(m)
                        load_expert(m, g * UNROLL + m // 3)
                    with sp.If(it < final):
                        for m in range(3 * UNROLL, 3 * UNROLL + SLOTS):
                            wait_expert_read(m)
                            load_expert(m, after_body + (m // 3 - UNROLL))
                    with sp.Else():
                        wait_expert_read(3 * UNROLL)
                        sp.dma_start(wple, w_ple[0].rearrange("(k p) n -> p k n", p=P)).then_inc(slot_full[s0], 16)
                        sp.dma_start(p_rows, p[0, 0].rearrange("(i p) n -> p i n", p=P)).then_inc(slot_full[s0], 16)
                        wait_expert_read(3 * UNROLL + 1)
                        sp.dma_start(wslot(T_PG, KD), wg[:, :, 0:HALF]).then_inc(slot_full[T_PG], 16)
            sp.wait_ge(row_free, rounds * NE + 4)
            for i in range(TT):
                for k in range(2):
                    sp.dma_start(y_back[:, i, k, :], y_rows[k * S + i * P:k * S + (i + 1) * P, :]).then_inc(y_in[k][i], 16)
            sp.dma_start(wslot(T_PG + 1, KD), wg[:, :, HALF:D]).then_inc(slot_full[T_PG + 1], 16)
            sp.dma_start(final_gain, final_norm_g.partition_broadcast(P)).then_inc(final_gain_in, 16)
            for q in range(2 * TT):
                i, part = q // 2, slice((q % 2) * HALF, (q % 2 + 1) * HALF)
                sp.wait_ge(final_ready, q + 1)
                sp.dma_start(out[0, i * P:(i + 1) * P, part], u3[:, i, part]).then_inc(stored, 16)
            sp.wait_ge(stored, 16 * 2 * TT)

        @block.gpsimd
        def _(pool):
            steps = 0

            def after(ins):
                nonlocal steps
                steps += 1
                ins.then_inc(pool_step, 1)
                pool.wait_ge(pool_step, steps)

            nc.gpsimd.memset(eps[:, :], EPS).then_inc(const_ready, 1)
            nc.gpsimd.memset(ident[:, :], 0.0).then_inc(pool_step, 1)
            nc.gpsimd.memset(before[:, :], 1.0).then_inc(pool_step, 1)
            steps = 2
            pool.wait_ge(pool_step, 2)
            nc.gpsimd.affine_select(out=ident[:, :], in_=ident[:, :], compare_op=ALU.not_equal, fill=1.0, base=0,
                                    pattern=[[-1, P]], channel_multiplier=1).then_inc(const_ready, 1)
            nc.gpsimd.memset(diag[:, :, :, :], 0.0).then_inc(zero_ready, 1)
            nc.gpsimd.affine_select(out=before[:, :], in_=before[:, :], compare_op=ALU.is_gt, fill=0.0, base=0,
                                    pattern=[[1, P]], channel_multiplier=-1).then_inc(const_ready, 1)
            nc.gpsimd.memset(ones[:, :], 1.0).then_inc(const_ready, 1)
            nc.gpsimd.iota(iota[:, :], pattern=[[1, C]], base=0, channel_multiplier=0,
                           allow_small_or_imprecise_dtypes=True).then_inc(const_ready, 1)
            nc.gpsimd.iota(token[:, :], pattern=[[2 * P, TT]], base=-FAR, channel_multiplier=2,
                           allow_small_or_imprecise_dtypes=True).then_inc(const_ready, 1)
            nc.gpsimd.memset(row_base[0:C, :], float(FAR)).then_inc(const_ready, 1)
            pool.wait_ge(const_ready, 7)
            nc.gpsimd.memset(row_base[C:P, :], float(FAR + 1)).then_inc(const_ready, 1)
            pool.wait_ge(const_ready, 8)
            nc.gpsimd.memset(xbp[:, :, 0:PAD], 0.0).then_inc(pool_step, 1)
            nc.gpsimd.memset(wsum[:, :, 0:PAD], 0.0).then_inc(pool_step, 1)
            steps += 2
            pool.wait_ge(pool_step, steps)

            def low(n):
                for h in range(2):
                    if low_engine[n, h] == "pool":
                        split_low(pool, nc.gpsimd, n, h)

            low(0)
            low(1)
            low(2)
            pool.wait_ge(prm_ready, 3)
            for g, w in enumerate(WINDOWS):
                if g == 2:
                    low(3)
                pool.wait_ge(xb_copied, g + 1)
                src, b, s = xbp[:, g, :], 0, 1
                while s < w:
                    dst = wsum[:, b, :]
                    after(nc.gpsimd.tensor_tensor(dst[:, PAD:W], src[:, PAD:W], src[:, PAD - s:W - s], ALU.add))
                    src, b, s = dst, 1 - b, 2 * s
                dst = wsum[:, b, :]
                after(nc.gpsimd.tensor_scalar(dst[:, PAD:W], src[:, PAD:W], 1.0 / w, None, ALU.mult))
                after(nc.gpsimd.tensor_tensor(dst[:, PAD:PAD + w], src[:, PAD:PAD + w], rcount[:, 0:w], ALU.mult))
                nc.gpsimd.tensor_tensor(xbp[:, g, PAD:W], dst[:, PAD:W], xbp[:, g, PAD:W],
                                        ALU.subtract).then_inc(pooled, 1)
                pool.wait_ge(pooled, g + 1)
            low(4)
            low(5)
            pool.wait_ge(tile_done, 4 * FIRST_OUT)
            nc.gpsimd.memset(lgT, 0.0).then_inc(lgT_cleared, 1)
            pool.wait_ge(rounds_ready, 1)
            rounds = pool.value_load(rounds_i[0:1, 0:1], min_val=1, max_val=S // C)
            pool.sem_inc(row_free, 4)
            last_row = pool.to_reg(4 * S - 1)

            def release_row(n0, m):
                pool.wait_ge(scattered[m % 4], n0 * 4 + 16 * (m // 4 + 1))
                pool.sem_inc(row_free, 1)

            with pool.Fori(0, rounds) as r:
                with pool.Fori(0, NE // UNROLL) as g:
                    n0 = pool.snap((r * (NE // UNROLL) + g) * UNROLL)
                    for m in range(UNROLL):
                        pool.wait_ge(y_stored, n0 + (m + 2))
                        pool.sem_inc(rows_taken, 1)
                        nc.gpsimd.indirect_dma_start(
                            out=y_halves, out_offset=bass.IndirectOffsetOnAxis(ap=row_i[:, m:m + 1], axis=0),
                            in_=yrow[:, m % 4, :], in_offset=None, bounds_check=last_row,
                            oob_is_err=False).then_inc(scattered[m % 4], 16)
                        if m >= 2:
                            release_row(n0, m - 2)
                    for m in (UNROLL - 2, UNROLL - 1):
                        release_row(n0, m)
            gate_low(pool, nc.gpsimd, 0)
            gate_low(pool, nc.gpsimd, 2)

        @block.scalar
        def _(act):
            steps = 0

            def after(ins):
                nonlocal steps
                steps += 1
                ins.then_inc(act_chain, 1)
                act.wait_ge(act_chain, steps)

            act.dma_start(gain[:, :], norm_mix_g[0].partition_broadcast(P)).then_inc(gain_in, 16)

            def norm(q, src):
                after(nc.scalar.activation(junk[:, :], src, ACT.Square, accum_out=ssq[:, q:q + 1]))
                nc.scalar.activation(std[:, q:q + 1], ssq[:, q:q + 1], ACT.Sqrt, bias=eps[:, 0:1],
                                     scale=1.0 / D).then_inc(std_done, 1)

            def copy_transposed(q, dst, banks):
                i, h = q // 2, q % 2
                act.wait_ge(ut_psum, q + 1)
                dst_k = dst[:, 4 * h:4 * h + 4, (i % TT) * P:(i % TT + 1) * P]
                nc.scalar.activation(dst_k, bank[banks[q % 4]][:, :].rearrange("p (k t) -> p k t", k=4),
                                     ACT.Copy).then_inc(ut_ready, 1)

            act.wait_ge(const_ready, 1)
            after(nc.scalar.activation(std[:, 0:1], eps[:, :], ACT.Sqrt))
            for i in range(TT):
                act.wait_ge(x_in[i], 16)
                norm(i, xin[:, i, :])
                if i == TT - 1:
                    split_high(act, 0, 0)
                if i >= 1:
                    copy_transposed(2 * i - 2, uT_high, (4, 5, 6, 7))
                    copy_transposed(2 * i - 1, uT_high, (4, 5, 6, 7))
            copy_transposed(2 * TT - 2, uT_high, (4, 5, 6, 7))
            copy_transposed(2 * TT - 1, uT_high, (4, 5, 6, 7))
            split_high(act, 0, 1)
            for h in range(2):
                split_high(act, 1, h)
            act.wait_ge(decay_arg, 1)
            nc.scalar.activation(spt[:, 1, :], spt[:, 0, :], ACT.Exp, scale=-1.0).then_inc(decay_exp, 1)
            act.wait_ge(decay_ready, 1)

            def conv_tap(c):
                t = position["xa", c]
                act.wait_ge(tile_done, t + 1)
                if c >= 4:
                    act.wait_ge(gates_psum, c - 3)
                    act.wait_ge(scan_done, c - 3)
                nc.scalar.activation(xc[:, c % 4, :], bank[t % 4][:, :], ACT.Identity, bias=col(4, c),
                                     scale=tap(3, c)).then_inc(conv_base, 1)

            def lru_gates(c):
                b = c % 2
                act.wait_ge(gates_psum, c + 1)
                if c >= 2:
                    act.wait_ge(scan_done, c - 1)
                after(nc.scalar.activation(lru_t[:, b, :], bank[4 + 2 * b][:, :], ACT.Sigmoid, bias=col(5, c)))
                nc.scalar.activation(lru_i[:, b, :], bank[5 + 2 * b][:, :], ACT.Sigmoid, bias=col(6, c)).then_inc(i_ready, 1)
                nc.scalar.activation(lru_t[:, b, :], lru_t[:, b, :], ACT.Tanh, scale=decay[:, c:c + 1]).then_inc(tanh_ready, 1)
                act.wait_ge(tanh_ready, c + 1)
                act.wait_ge(sqrt_free, c + 1)
                nc.scalar.activation(lru_t[:, b, :], lru_t[:, b, :], ACT.Sqrt, scale=-4.0).then_inc(sqrt_ready, 1)

            def pool_copy(g):
                t = position["xb", g]
                act.wait_ge(tile_done, t + 1)
                nc.scalar.activation(xbp[:, g, PAD:W], bank[t % 4][:, :], ACT.Copy).then_inc(xb_copied, 1)

            def gelu(c):
                t = position["ya", c]
                b = c % 2
                act.wait_ge(tile_done, t + 1)
                if c >= 2:
                    act.wait_ge(ya_used, c - 1)
                nc.scalar.activation(gel[:, b, :], bank[t % 4][:, :], ACT.Square).then_inc(sq_ready, 1)
                act.wait_ge(garg_ready, c + 1)
                nc.scalar.activation(gel[:, b, :], gel[:, b, :], ACT.Sigmoid, scale=GELU_SCALE).then_inc(gsig_ready, 1)

            def ha_split(c):
                act.wait_ge(ha_ready, c + 1)
                nc.scalar.activation(ha_high[:, c, :], ha[:, c, :], ACT.Copy).then_inc(ha_high_ready, 1)

            def pool_scaled(g):
                act.wait_ge(mixed, g + 1)
                nc.scalar.activation(hb_high[:, g, :], bank[4 + g][:, :], ACT.Copy,
                                     scale=prm[:, 8 * NX + g:8 * NX + g + 1]).then_inc(hb_ready, 1)

            def merge_gate(kind, j):
                t = position[kind, j]
                act.wait_ge(tile_done, t + 1)
                if kind == "gb":
                    nc.scalar.activation(merged[:, j, :], bank[t % 4][:, :], ACT.Sigmoid).then_inc(gate_b_ready, 1)
                else:
                    if j >= 4:
                        act.wait_ge(merged_sum, j - 3)
                    nc.scalar.activation(gate_a(j), bank[t % 4][:, :], ACT.Sigmoid).then_inc(gate_a_ready, 1)

            def merged_split(j):
                act.wait_ge(merged_sum, j + 1)
                nc.scalar.activation(merged_high[:, j, :], merged[:, j, :], ACT.Copy).then_inc(merged_high_ready, 1)

            for t, (kind, c) in enumerate(tiles):
                n = t // 4
                if n >= 1 and (n + 1, t % 4) in halves:
                    split_high(act, n + 1, t % 4)
                if n == FIRST_MERGE and t % 4 < 2:
                    for d in range(2):
                        pool_scaled(2 * (t % 4) + d)
                if n == FIRST_MERGE + 1:
                    for d in range(2):
                        ha_split(2 * (t % 4) + d)
                if kind == "xa":
                    conv_tap(c)
                if kind == "xb":
                    pool_copy(c)
                if kind == "ya":
                    gelu(c)
                if kind in ("ga", "gb"):
                    merge_gate(kind, c)
                if kind == "ua":
                    merged_split(c)
                if t >= 2 and tiles[t - 2][0] == "xa":
                    lru_gates(tiles[t - 2][1])
            act.dma_start(gain[:, :], norm_ffn_g[0].partition_broadcast(P)).then_inc(gain_in, 16)
            for i in range(TT):
                act.wait_ge(h1_ready, TT + i + 1)
                norm(TT + i, h1[:, i, :])
                if i >= 1:
                    copy_transposed(2 * (TT + i - 1), u2T, (4, 5, 6, 7))
                    copy_transposed(2 * (TT + i - 1) + 1, u2T, (4, 5, 6, 7))

            def copy_logits(part):
                act.wait_ge(lgT_psum, part + 1)
                act.wait_ge(lgT_cleared, 1)
                nc.scalar.activation(lgT[0:NL, logit_parts[part]], bank[0][0:NL, logit_parts[part]],
                                     ACT.Copy).then_inc(lgT_even_ready, 1)

            copy_logits(0)
            copy_transposed(4 * TT - 2, u2T, (4, 5, 6, 7))
            copy_transposed(4 * TT - 1, u2T, (4, 5, 6, 7))
            copy_logits(1)
            act.wait_ge(gdiff_ready, 1)
            nc.scalar.activation(g4[:, 3, :, :], g4[:, 0, :, :], ACT.Exp).then_inc(gexp_ready, 1)
            act.wait_ge(ediff_ready, 1)
            nc.scalar.activation(t4[:, 7, :], t4[:, 6, :], ACT.Exp).then_inc(eexp_ready, 1)

            act.wait_ge(norm_done, 2 * TT)
            act.dma_start(gain[:, :], norm_ple_g[0].partition_broadcast(P)).then_inc(gain_in, 16)
            act.wait_ge(rounds_ready, 1)
            rounds = act.value_load(rounds_i[0:1, 0:1], min_val=1, max_val=S // C)

            def copy_rows(n):
                act.wait_ge(xrow_psum, n)
                nc.scalar.activation(xrow, bank[0][:, :], ACT.Copy).then_inc(xrow_ready, 1)

            def copy_xT(b, n):
                act.wait_ge(xT_psum, n)
                nc.scalar.activation(xT[:, b, :, :].rearrange("p (h j) c -> p j h c", h=2),
                                     bank[4][:, :].rearrange("p (j h c) -> p j h c", j=4, h=2), ACT.Copy).then_inc(xT_ready, 1)

            copy_rows(1)
            copy_xT(0, 1)
            with act.Fori(0, rounds) as r:
                with act.Fori(0, NE // UNROLL) as g:
                    n0 = act.snap((r * (NE // UNROLL) + g) * UNROLL)
                    for m in range(UNROLL):
                        b = m % 2
                        act.wait_ge(gate_up_psum, n0 + (m + 1))
                        nc.scalar.activation(sig, bank[2][:, 0:FE // 2], ACT.Sigmoid).then_inc(sig_ready, 1)
                        copy_rows(n0 + (m + 2))
                        copy_xT(1 - b, n0 + (m + 2))
            last = act.snap(rounds * (16 * 3 * NE // SLOTS))

            def gate_high(step):
                h, ks = gate_steps[step]
                act.wait_ge(slot_full[T_PG + h], last + slots_at(T_PG + h))
                nc.scalar.activation(gate_part("high", h)[:, ks, :], gate_part("whole", h)[:, ks, :],
                                     ACT.Copy).then_inc(pg_high_ready, 1)

            def copy_ple(q):
                act.wait_ge(ple_psum, q + 1)
                nc.scalar.activation(ple[:, q // 2, (q % 2) * HALF:(q % 2 + 1) * HALF], ple_bank(q)[:, :],
                                     ACT.Copy).then_inc(ple_ready, 1)

            act.wait_ge(pT_psum, 1)
            nc.scalar.activation(pT[:, 0, :], bank[6][:, :], ACT.Copy).then_inc(pT0_ready, 1)
            gate_high(0)
            after(nc.scalar.activation(std[:, 2 * TT:2 * TT + 1], eps[:, :], ACT.Sqrt))
            for q in range(4):
                copy_ple(q)
            for i in range(TT):
                act.wait_ge(h2_ready, i + 1)
                norm(2 * TT + i, h1[:, i, :])
                if i == 0:
                    copy_ple(4)
                    copy_ple(5)
                if i >= 2:
                    gate_high(i - 1)
                copy_transposed(2 * (2 * TT + i), u3T_high, (4, 5, 6, 7))
                copy_transposed(2 * (2 * TT + i) + 1, u3T_high, (4, 5, 6, 7))
                if i == 0:
                    copy_ple(6)
                    copy_ple(7)
            for q in range(2 * TT):
                act.wait_ge(pg_psum, q + 1)
                if q >= 2:
                    act.wait_ge(h3_ready, q - 1)
                nc.scalar.activation(psig[:, q % 2, :], bank[q % 4][:, :], ACT.Sigmoid).then_inc(pg_sig, 1)
                if q >= TT:
                    after(nc.scalar.activation(std[:, 2 * TT + q:2 * TT + q + 1], eps[:, :], ACT.Sqrt))
                    act.wait_ge(h3_ready, q + 1)
                    norm(2 * TT + q, h1[:, q - TT, :])

        @block.vector
        def _(dve):
            v = nc.vector
            steps = 0

            def after(ins):
                nonlocal steps
                steps += 1
                ins.then_inc(dve_chain, 1)
                dve.wait_ge(dve_chain, steps)

            def normalise(q, src, dst):
                dve.wait_ge(std_done, q + 1)
                after(v.reciprocal(rstd[:, q:q + 1], std[:, q:q + 1]))
                v.scalar_tensor_tensor(out=dst, in0=src, scalar=rstd[:, q:q + 1], in1=gain[:, :], op0=ALU.mult,
                                       op1=ALU.mult).then_inc(norm_done, 1)

            def uT_split(q, high=uT_high, low=uT_low):
                i, h = q // 2 % TT, q % 2
                dve.wait_ge(ut_ready, q + 1)
                part = slice(4 * h, 4 * h + 4), slice(i * P, (i + 1) * P)
                v.tensor_tensor(low[:, part[0], part[1]], bank[4 + q % 4][:, :].rearrange("p (k t) -> p k t", k=4),
                                high[:, part[0], part[1]], ALU.subtract).then_inc(ut_low, 1)

            dve.wait_ge(gain_in, 16)
            for i in range(TT):
                normalise(i, xin[:, i, :], xin[:, i, :])
                if i >= 1:
                    uT_split(2 * i - 2)
                    uT_split(2 * i - 1)
            uT_split(2 * TT - 2)
            uT_split(2 * TT - 1)
            dve.wait_ge(const_ready, 8)
            dve.wait_ge(vec_psum, 1)
            v.tensor_copy(prm[:, :], bank[3][:, 0:NV]).then_inc(prm_ready, 1)
            split_low(dve, v, 0, 1)
            dve.wait_ge(prm_ready, 1)
            v.tensor_tensor(add_halves[:, :], ident[:, 0:NL], ident[:, 64:64 + NL], ALU.add).then_inc(prm_ready, 1)
            after(v.tensor_scalar(rcount[:, :], iota[:, 0:PAD], 1.0, None, ALU.add))
            v.reciprocal(rcount[:, :], rcount[:, :]).then_inc(prm_ready, 1)
            after(v.tensor_scalar(spt[:, 2, :], lam, -1.0, None, ALU.mult))
            v.tensor_tensor(spt[:, 0, :], lam, spt[:, 2, :], ALU.max).then_inc(decay_arg, 1)
            after(v.tensor_scalar(spt[:, 2, :], spt[:, 2, :], 0.0, -LRU_C / 2, ALU.max, ALU.mult))
            dve.wait_ge(decay_exp, 1)
            after(v.tensor_scalar(spt[:, 3, :], spt[:, 1, :], 2.0, None, ALU.add))
            after(v.reciprocal(spt[:, 3, :], spt[:, 3, :]))
            after(v.tensor_tensor(spt[:, 3, :], spt[:, 3, :], spt[:, 1, :], ALU.mult))
            after(v.tensor_tensor(spt[:, 4, :], spt[:, 3, :], spt[:, 3, :], ALU.mult))
            after(v.tensor_scalar(spt[:, 5, :], spt[:, 4, :], 1.0 / 15, None, ALU.mult))
            for odd in (13, 11, 9, 7, 5, 3):
                after(v.scalar_tensor_tensor(out=spt[:, 5, :], in0=spt[:, 5, :], scalar=1.0 / odd, in1=spt[:, 4, :],
                                             op0=ALU.add, op1=ALU.mult))
            after(v.scalar_tensor_tensor(out=spt[:, 5, :], in0=spt[:, 5, :], scalar=1.0, in1=spt[:, 3, :],
                                         op0=ALU.add, op1=ALU.mult))
            v.scalar_tensor_tensor(out=decay[:, :], in0=spt[:, 5, :], scalar=-LRU_C, in1=spt[:, 2, :],
                                   op0=ALU.mult, op1=ALU.add).then_inc(decay_ready, 1)

            def conv(c):
                t = position["xa", c]
                z, y = bank[t % 4], xc[:, c % 4, :]
                dve.wait_ge(conv_base, c + 1)
                for d in (1, 2, 3):
                    ins = v.scalar_tensor_tensor(out=y[:, d:S], in0=z[:, 0:S - d], scalar=tap(3 - d, c), in1=y[:, d:S],
                                                 op0=ALU.mult, op1=ALU.add)
                    if d < 3:
                        after(ins)
                    else:
                        ins.then_inc(conv_done, 1)

            def lru(c):
                b = c % 2
                t, q, a, i = lru_t[:, b, :], lru_q[:, b, :], lru_a[:, b, :], lru_i[:, b, :]
                dve.wait_ge(tanh_ready, c + 1)
                v.tensor_scalar(q, t, -1.0, 1.0, ALU.mult, ALU.add).then_inc(sqrt_free, 1)
                dve.wait_ge(sqrt_free, c + 1)
                after(v.reciprocal(q, q))
                after(v.tensor_scalar(a, q, 2.0, -1.0, ALU.mult, ALU.add))
                after(v.tensor_tensor(i, i, xc[:, c % 4, :], ALU.mult))
                dve.wait_ge(sqrt_ready, c + 1)
                after(v.tensor_tensor(t, t, q, ALU.mult))
                after(v.tensor_tensor(t, t, i, ALU.mult))
                v.tensor_tensor_scan(ha[:, c, :], a, t, 0.0, ALU.mult, ALU.add).then_inc(scan_done, 1)

            def gelu(c):
                t, b = position["ya", c], c % 2
                y, w = bank[t % 4], gel[:, b, :]
                dve.wait_ge(sq_ready, c + 1)
                after(v.tensor_scalar(w, w, GELU_CUBIC, 1.0, ALU.mult, ALU.add))
                v.tensor_tensor(w, w, y[:, :], ALU.mult).then_inc(garg_ready, 1)
                dve.wait_ge(gsig_ready, c + 1)
                v.tensor_tensor(w, w, y[:, :], ALU.mult).then_inc(ya_used, 1)
                dve.wait_ge(ya_used, c + 1)
                dve.wait_ge(scan_done, c + 1)
                v.tensor_tensor(ha[:, c, :], ha[:, c, :], w, ALU.mult).then_inc(ha_ready, 1)

            def ha_split(c):
                dve.wait_ge(ha_high_ready, c + 1)
                v.tensor_tensor(ha_low[:, c, :], ha[:, c, :], ha_high[:, c, :], ALU.subtract).then_inc(ha_low_ready, 1)

            def pool_split(g):
                dve.wait_ge(hb_ready, g + 1)
                v.scalar_tensor_tensor(out=hb_low[:, g, :], in0=bank[4 + g][:, :],
                                       scalar=prm[:, 8 * NX + g:8 * NX + g + 1], in1=hb_high[:, g, :], op0=ALU.mult,
                                       op1=ALU.subtract).then_inc(hb_low_ready, 1)

            def merge_up(kind, j):
                t = position[kind, j]
                dve.wait_ge(tile_done, t + 1)
                if kind == "ub":
                    dve.wait_ge(gate_b_ready, j + 1)
                    v.tensor_tensor(merged[:, j, :], merged[:, j, :], bank[t % 4][:, :], ALU.mult).then_inc(up_b_used, 1)
                else:
                    dve.wait_ge(gate_a_ready, j + 1)
                    v.tensor_tensor(gate_a(j), gate_a(j), bank[t % 4][:, :], ALU.mult).then_inc(up_a_used, 1)
                    dve.wait_ge(up_a_used, j + 1)
                    v.tensor_tensor(merged[:, j, :], merged[:, j, :], gate_a(j), ALU.add).then_inc(merged_sum, 1)

            def merged_split(j):
                dve.wait_ge(merged_high_ready, j + 1)
                v.tensor_tensor(merged_low[:, j, :], merged[:, j, :], merged_high[:, j, :],
                                ALU.subtract).then_inc(merged_low_ready, 1)

            def residual(q):
                t, h, i = position["out", q], q // TT, q % TT
                dve.wait_ge(tile_done, t + 1)
                dve.wait_ge(x_back[i], 16)
                res = h1[:, i, h * HALF:(h + 1) * HALF]
                v.tensor_tensor(res, res, bank[t % 4][:, :], ALU.add).then_inc(h1_ready, 1)

            for t, (kind, c) in enumerate(tiles):
                n = t // 4
                if kind == "ya":
                    gelu(c)
                if kind == "xa":
                    conv(c)
                if t >= 2 and tiles[t - 2][0] == "xa":
                    lru(tiles[t - 2][1])
                if n == FIRST_MERGE and t % 4 < 2:
                    for d in range(2):
                        pool_split(2 * (t % 4) + d)
                if n == FIRST_MERGE + 1:
                    for d in range(2):
                        ha_split(2 * (t % 4) + d)
                if kind in ("ua", "ub"):
                    merge_up(kind, c)
                if t >= 1 and tiles[t - 1][0] == "ua":
                    merged_split(tiles[t - 1][1])
                if kind == "out":
                    residual(c)
                    if c == TT:
                        dve.wait_ge(gain_in, 32)
                    if c >= TT:
                        normalise(c, h1[:, c - TT, :], u2[:, c - TT, :])
                if low_engine.get((n + 1, t % 4)) == "vector":
                    split_low(dve, v, n + 1, t % 4)
            for part in range(2):
                dve.wait_ge(lgT_psum, part + 1)
                dve.wait_ge(lgT_cleared, 1)
                v.tensor_copy(lgT[64:64 + NL, logit_parts[part]], bank[0][64:64 + NL, logit_parts[part]]).then_inc(lgT_odd_ready, 1)

            def bc(ap, n):
                return ap.unsqueeze(2).to_broadcast([P, ap.shape[1], n])

            def first_max(scores, n, best, index, cands, onehot):
                after(v.tensor_reduce(best, scores, AX.X, ALU.max))
                after(v.tensor_tensor(cands, scores, bc(best, n), ALU.is_equal))
                after(v.scalar_tensor_tensor(out=cands, in0=cands, scalar=-float(C),
                                             in1=iota[:, 0:n].unsqueeze(1).to_broadcast([P, TT, n]),
                                             op0=ALU.mult, op1=ALU.add))
                after(v.tensor_reduce(index, cands, AX.X, ALU.min))
                after(v.tensor_tensor(onehot, cands, bc(index, n), ALU.is_equal))

            def make_pick(b, e):
                where = place[:, e, :] if isinstance(e, int) else place[:, bass.ds(e, 1), :].rearrange("p o i -> p (o i)")
                v.tensor_tensor(pick[:, b, :, :], iota[:, :].unsqueeze(1).to_broadcast([P, TT, C]), bc(where, C),
                                ALU.is_equal).then_inc(pick_ready, 1)

            gl = lg[:, :, 0:NG]
            dve.wait_ge(logits_psum, 1)
            dve.wait_ge(lru_in, 16 * 9)
            after(v.tensor_tensor(lg[:, :, :], bank[1][:, 0:TT * 64].rearrange("p (i n) -> p i n", i=TT)[:, :, 0:NL],
                                  brt[:, :].unsqueeze(1).to_broadcast([P, TT, NL]), ALU.add))
            first_max(gl, NG, t4[:, 0, :], t4[:, 1, :], g4[:, 1, :, :], g4[:, 2, :, :])
            el_g = el[:, :, :].rearrange("p i (g e) -> p i g e", g=NG)
            after(v.tensor_scalar(g4[:, 1, :, :], g4[:, 2, :, :], 2 * BIG, -BIG, ALU.mult, ALU.add))
            after(v.tensor_tensor(el_g, lg[:, :, NG:NL].rearrange("p i (g e) -> p i g e", g=NG),
                                  g4[:, 1, :, :].unsqueeze(3).to_broadcast([P, TT, NG, PG]), ALU.min))
            first_max(el[:, :, :], NE, t4[:, 2, :], t4[:, 3, :], cand[:, :, :], oh1[:, :, :])
            after(v.scalar_tensor_tensor(out=el[:, :, :], in0=oh1[:, :, :], scalar=-2 * BIG, in1=el[:, :, :],
                                         op0=ALU.mult, op1=ALU.add))
            first_max(el[:, :, :], NE, t4[:, 4, :], t4[:, 5, :], cand[:, :, :], oh2[:, :, :])
            v.tensor_tensor(routed_bf[:, :, :], oh1[:, :, :], oh2[:, :, :], ALU.add).then_inc(routed_ready, 1)
            v.tensor_tensor(g4[:, 0, :, :], gl, bc(t4[:, 0, :], NG), ALU.subtract).then_inc(gdiff_ready, 1)
            v.tensor_tensor(t4[:, 6, :], t4[:, 4, :], t4[:, 2, :], ALU.subtract).then_inc(ediff_ready, 1)
            after(v.tensor_tensor(routed[:, :, :], oh1[:, :, :], oh2[:, :, :], ALU.add))
            dve.wait_ge(places_psum, 1)
            after(v.scalar_tensor_tensor(out=cand[:, :, :], in0=bank[5][:, 0:TT * NE].rearrange("p (i e) -> p i e", i=TT),
                                         scalar=1.0, in1=routed[:, :, :], op0=ALU.add, op1=ALU.mult))
            after(v.tensor_scalar(place[:, 0:NE, :].rearrange("p e i -> p i e"), cand[:, :, :], -1.0, None, ALU.add))
            make_pick(0, 0)
            after(v.tensor_scalar(place[:, NE, :], place[:, 0, :], -float(C), None, ALU.add))
            dve.wait_ge(gexp_ready, 1)
            after(v.tensor_reduce(t4[:, 8, :], g4[:, 3, :, :], AX.X, ALU.add))
            dve.wait_ge(eexp_ready, 1)
            after(v.tensor_scalar(t4[:, 9, :], t4[:, 7, :], 1.0, None, ALU.add))
            after(v.tensor_tensor(t4[:, 9, :], t4[:, 9, :], t4[:, 8, :], ALU.mult))
            after(v.reciprocal(t4[:, 10, :], t4[:, 9, :]))
            after(v.tensor_tensor(t4[:, 11, :], t4[:, 10, :], t4[:, 7, :], ALU.mult))
            info_row = info[:, 0:NE, :, 0].rearrange("p e i -> p i e")
            info_gate = info[:, 0:NE, :, 1].rearrange("p e i -> p i e")
            after(v.tensor_tensor(cand[:, :, :], oh1[:, :, :], bc(t4[:, 10, :], NE), ALU.mult))
            after(v.tensor_tensor(el[:, :, :], oh2[:, :, :], bc(t4[:, 11, :], NE), ALU.mult))
            after(v.tensor_tensor(info_gate, cand[:, :, :], el[:, :, :], ALU.add))
            after(v.scalar_tensor_tensor(out=info_row, in0=oh2[:, :, :], scalar=2.0 * S, in1=bc(token[:, :], NE),
                                         op0=ALU.mult, op1=ALU.add))
            after(v.tensor_copy(info[:, NE, :, :], info[:, 0, :, :]))
            after(v.tensor_reduce(t4[:, 0, 0:1], bank[5][:, TT * NE:(TT + 1) * NE], AX.X, ALU.max))
            v.tensor_scalar(rounds_i[:, :], t4[:, 0, 0:1], 1.0 / C, 0.5 - 0.5 / C, ALU.mult, ALU.add).then_inc(rounds_ready, 1)

            def make_info(b, e):
                src = info[:, e, :, :] if isinstance(e, int) else \
                    info[:, bass.ds(e, 1), :, :].rearrange("p o i c -> p (o i) c")
                v.tensor_copy(pinfo[:, b, :, :], src).then_inc(pick_ready, 1)

            def take_info(at):
                v.tensor_scalar(row_i[:, at:at + 1], bank[1][:, 0:1], row_base[:, 0:1], None, ALU.add).then_inc(info_ready, 1)
                v.tensor_copy(gate_c[:, at:at + 1], bank[1][:, 1:2]).then_inc(info_ready, 1)

            make_info(0, 0)
            dve.wait_ge(rounds_ready, 1)
            dve.wait_ge(info_psum, 1)
            take_info(0)
            dve.sem_inc(y_stored, 1)
            rounds = dve.value_load(rounds_i[0:1, 0:1], min_val=1, max_val=S // C)
            with dve.Fori(0, rounds) as r:
                with dve.Fori(0, NE // UNROLL) as g:
                    n0 = dve.snap((r * (NE // UNROLL) + g) * UNROLL)
                    for m in range(UNROLL):
                        b = m % 2
                        nxt = g * UNROLL + (m + 1)
                        make_pick(1 - b, nxt)
                        make_info(1 - b, nxt)
                        dve.wait_ge(sig_ready, n0 + (m + 1))
                        v.tensor_tensor(hid, sig, bank[2][:, 0:FE // 2], ALU.mult).then_inc(gated, 1)
                        dve.wait_ge(gated, n0 + (m + 1))
                        v.tensor_tensor(hid, hid, bank[2][:, FE // 2:FE], ALU.mult).then_inc(hidden_ready, 1)
                        dve.wait_ge(hT_psum, n0 + (m + 1))
                        v.tensor_copy(hT.rearrange("p (h j) c -> p j h c", h=2),
                                      bank[3][:, 0:FE // 2].rearrange("p (j h c) -> p j h c", j=2, h=2)).then_inc(hT_ready, 1)
                        dve.wait_ge(info_psum, n0 + (m + 2))
                        take_info((m + 1) % UNROLL)
                        dve.wait_ge(y_psum, n0 + (m + 1))
                        dve.wait_ge(row_free, n0 + (m + 1))
                        v.tensor_scalar(yrow[:, m % 4, :], bank[5][:, :], gate_c[:, m:m + 1], None,
                                        ALU.mult).then_inc(y_stored, 1)
                dve.wait_ge(pick_ready, r * (2 * NE) + 2 * (NE + 1))
                v.tensor_scalar(place[:, :, :], place[:, :, :], -float(C), None, ALU.add).then_inc(next_round, 1)
                dve.wait_ge(next_round, r + 1)
            dve.wait_ge(pT_psum, 1)
            v.tensor_copy(pT[:, 1, :], bank[7][:, :]).then_inc(pT1_ready, 1)
            def add_choice(i, k):
                dve.wait_ge(y_in[k][i], 16)
                ins = v.tensor_tensor(h1[:, i, :], h1[:, i, :], y_back[:, i, k, :], ALU.add)
                if k == 0:
                    after(ins)
                else:
                    ins.then_inc(h2_ready, 1)

            add_choice(0, 0)
            add_choice(0, 1)
            dve.wait_ge(gain_in, 48)
            for i in range(TT):
                if i == 0:
                    add_choice(1, 0)
                if i == TT - 1:
                    gate_low(dve, v, 1)
                normalise(2 * TT + i, h1[:, i, :], u3[:, i, :])
                if i == 0:
                    add_choice(1, 1)
                elif i + 1 < TT:
                    add_choice(i + 1, 0)
                    add_choice(i + 1, 1)
                uT_split(2 * (2 * TT + i), u3T_high, u3T_low)
                uT_split(2 * (2 * TT + i) + 1, u3T_high, u3T_low)
            dve.wait_ge(h2_ready, TT)
            dve.wait_ge(ple_ready, 2 * TT)
            dve.wait_ge(final_gain_in, 16)
            for q in range(2 * TT):
                h, i = q // TT, q % TT
                cols = slice(h * HALF, (h + 1) * HALF)
                dve.wait_ge(pg_sig, q + 1)
                after(v.tensor_tensor(psig[:, q % 2, :], psig[:, q % 2, :], ple[:, i, cols], ALU.mult))
                v.tensor_tensor(h1[:, i, cols], h1[:, i, cols], psig[:, q % 2, :], ALU.add).then_inc(h3_ready, 1)
                if h == 1:
                    dve.wait_ge(h3_ready, q + 1)
                    for g in range(2):
                        part = slice(g * HALF, (g + 1) * HALF)
                        if g == 0:
                            dve.wait_ge(std_done, 3 * TT + i + 1)
                            after(v.reciprocal(rstd[:, 3 * TT + i:3 * TT + i + 1], std[:, 3 * TT + i:3 * TT + i + 1]))
                        v.scalar_tensor_tensor(out=u3[:, i, part], in0=h1[:, i, part],
                                               scalar=rstd[:, 3 * TT + i:3 * TT + i + 1], in1=final_gain[:, part],
                                               op0=ALU.mult, op1=ALU.mult).then_inc(final_ready, 1)

        @block.tensor
        def _(pe):
            def mm(*a, **k):
                return nc.tensor.matmul(*a, **k)

            pe.wait_ge(const_ready, 2)

            def transpose_rows(q, src, banks):
                i, h = q // 2, q % 2
                if h == 0:
                    pe.wait_ge(norm_done, i + 1)
                if q % (2 * TT) >= 4:
                    norm_ = q // (2 * TT)
                    pe.wait_ge(*((ut_low, q - 3), (ut_ready, q - 3), (ut_low, q - 2 * TT - 3))[norm_])
                for k in range(4):
                    ins = nc.tensor.transpose(bank[banks[q % 4]][:, k * P:(k + 1) * P],
                                              src[:, i % TT, (4 * h + k) * P:(4 * h + k + 1) * P], ident[:, :])
                ins.then_inc(ut_psum, 1)

            for q in range(2 * TT):
                transpose_rows(q, xin, (4, 5, 6, 7))
            pe.wait_ge(small_in, 16 * 6)
            nc.tensor.transpose(bank[3][:, 0:NV], vecs[0:NV, :], ident[0:NV, 0:NV]).then_inc(vec_psum, 1)
            pe.wait_ge(ut_low, 2 * TT)

            def lru_gates(c):
                pe.wait_ge(conv_done, c + 1)
                if c >= 2:
                    pe.wait_ge(i_ready, c - 1)
                if c == 0:
                    pe.wait_ge(lru_in, 16 * 9)
                for w in range(2):
                    ins = mm(bank[4 + 2 * (c % 2) + w][:, :], diag[:, c, w, :], xc[:, c % 4, :], start=True, stop=True)
                ins.then_inc(gates_psum, 1)

            def mix(g):
                pe.wait_ge(pooled, g + 1)
                if g % 2 == 0:
                    pe.wait_ge(i_ready, NX - 1 + g // 2)
                mm(bank[4 + g][:, :], wpool[:, g, :], xbp[:, g, PAD:W], start=True, stop=True).then_inc(mixed, 1)

            parts_of = {"ua": (ha_high, ha_low), "ub": (hb_high, hb_low), "out": (merged_high, merged_low)}
            for t, (kind, c) in enumerate(tiles):
                n = block_of[kind, c]
                k_tiles = blocks[n][2]
                dst = bank[t % 4][:, :]
                if t == 3:
                    pe.wait_ge(prm_ready, 1)
                if t >= 4:
                    read_kind, read_c = tiles[t - 4]
                    pe.wait_ge(bank_read[read_kind], read_c + 1)
                if (kind, c) == ("ua", 0):
                    pe.wait_ge(ha_low_ready, NX)
                if (kind, c) == ("ub", 0):
                    pe.wait_ge(hb_low_ready, NB)
                for g in range(k_tiles // 4):
                    for part in ("high", "low"):
                        for k in range(4 * g, 4 * g + 4):
                            if t % 4 == 0 and k % 4 == 0:
                                if part == "high":
                                    pe.wait_ge(high_ready, halves.index((n, g)) + 1)
                                else:
                                    pe.wait_ge(*lows_at(n, g))
                            if (kind, c, part) == ("out", 0, "high"):
                                pe.wait_ge(merged_low_ready, k + 1)
                            w = (high_half if part == "high" else low_half)(n, g)[:, k % 4, :]
                            x_parts = parts_of.get(kind, (uT_high, uT_low))
                            for x_part, x_ in enumerate(x_parts if part == "high" else x_parts[0:1]):
                                flags = dict(start=(k == 0 and part == "high" and x_part == 0),
                                             stop=(k == k_tiles - 1 and part == "low"))
                                if kind == "out":
                                    ins = mm(dst, x_[:, k, (c % TT) * P:(c % TT + 1) * P], w, **flags)
                                else:
                                    ins = mm(dst, w[:, (t % 4) * P:(t % 4 + 1) * P], x_[:, k, :], **flags)
                ins.then_inc(tile_done, 1)
                if kind == "out" and c > TT:
                    transpose_rows(2 * (c - 1), u2, (4, 5, 6, 7))
                    transpose_rows(2 * (c - 1) + 1, u2, (4, 5, 6, 7))
                if t >= 2 and tiles[t - 2][0] == "xa":
                    lru_gates(tiles[t - 2][1])
                if t // 4 == FIRST_MERGE - 1 and t % 4 >= 2:
                    mix(2 * (t % 4) - 4)
                    mix(2 * (t % 4) - 3)
            pe.wait_ge(h1_ready, 2 * TT)

            def logits(part):
                for k in range(KD):
                    at = 64 * (k % 2)
                    ins = mm(bank[0][at:at + NL, logit_parts[part]], wrt[:, k, :], u2T[:, k, logit_parts[part]],
                             start=(k < 2), stop=(k >= KD - 2))
                ins.then_inc(lgT_psum, 1)

            def logits_by_token(i):
                return mm(bank[1][:, i * 64:i * 64 + NL], lgT[:, i * P:(i + 1) * P], add_halves[:, :], start=True, stop=True)

            pe.wait_ge(lru_in, 16 * 9)
            pe.wait_ge(ut_ready, 4 * TT - 2)
            logits(0)
            transpose_rows(4 * TT - 2, u2, (4, 5, 6, 7))
            transpose_rows(4 * TT - 1, u2, (4, 5, 6, 7))
            pe.wait_ge(lgT_even_ready, 1)
            pe.wait_ge(lgT_odd_ready, 1)
            pe.wait_ge(prm_ready, 2)
            for i in range(TT - 1):
                logits_by_token(i)
            pe.wait_ge(ut_ready, 4 * TT)
            logits(1)
            pe.wait_ge(lgT_even_ready, 2)
            pe.wait_ge(lgT_odd_ready, 2)
            logits_by_token(TT - 1).then_inc(logits_psum, 1)
            pe.wait_ge(routed_ready, 1)
            pe.wait_ge(const_ready, 8)
            for i in range(TT):
                dst = bank[5][:, i * NE:(i + 1) * NE]
                mm(dst, before[:, :], routed_bf[:, i, :], start=True, stop=(i == 0))
                for j in range(i):
                    mm(dst, ones[:, :], routed_bf[:, j, :], start=False, stop=(j == i - 1))
            for i in range(TT):
                ins = mm(bank[5][:, TT * NE:(TT + 1) * NE], ones[:, :], routed_bf[:, i, :], start=(i == 0), stop=(i == TT - 1))
            ins.then_inc(places_psum, 1)

            def gather(b):
                for i in range(TT):
                    for h in range(2):
                        ins = mm(bank[0][h * C:(h + 1) * C, :], pick[:, b, i, :], u2[:, i, h * HALF:(h + 1) * HALF],
                                 start=(i == 0), stop=(i == TT - 1))
                ins.then_inc(xrow_psum, 1)

            def gather_info(b):
                for i in range(TT):
                    for h in range(2):
                        ins = mm(bank[1][h * C:(h + 1) * C, 0:2], pick[:, b, i, :], pinfo[:, b, i, :],
                                 start=(i == 0), stop=(i == TT - 1))
                ins.then_inc(info_psum, 1)

            def transpose_x():
                for j in range(4):
                    ins = nc.tensor.transpose(bank[4][:, j * P:(j + 1) * P], xrow[:, j * P:(j + 1) * P], ident[:, :])
                ins.then_inc(xT_psum, 1)

            pe.wait_ge(pick_ready, 1)
            gather(0)
            pe.wait_ge(pick_ready, 2)
            gather_info(0)
            pe.wait_ge(xrow_ready, 1)
            transpose_x()
            rounds = pe.value_load(rounds_i[0:1, 0:1], min_val=1, max_val=S // C)
            with pe.Fori(0, rounds) as r:
                with pe.Fori(0, NE // UNROLL) as g:
                    it = pe.snap(r * (NE // UNROLL) + g)
                    n0 = pe.snap(it * UNROLL)
                    laps = pe.snap(it * (16 * 3 * UNROLL // SLOTS))
                    for m in range(UNROLL):
                        b = m % 2
                        pe.wait_ge(xT_ready, n0 + (m + 1))
                        for which in range(2):
                            n = 3 * m + which
                            pe.wait_ge(slot_full[n % SLOTS], laps + slots_at(n))
                            w = wslot(n, KD)
                            for k in range(KD):
                                for h in range(2):
                                    ins = mm(bank[2][h * C:(h + 1) * C, which * (FE // 2):(which + 1) * (FE // 2)],
                                             xT[:, b, k, :], w[:, k, h * (FE // 2):(h + 1) * (FE // 2)],
                                             start=(k == 0), stop=(k == KD - 1))
                            ins.then_inc(gate_up_psum if which else gate_psum, 1)
                        pe.wait_ge(pick_ready, n0 * 2 + 2 * (m + 2))
                        gather(1 - b)
                        pe.wait_ge(hidden_ready, n0 + (m + 1))
                        for j in range(2):
                            ins = nc.tensor.transpose(bank[3][:, j * P:(j + 1) * P], hid[:, j * P:(j + 1) * P], ident[:, :])
                        ins.then_inc(hT_psum, 1)
                        pe.wait_ge(info_ready, n0 * 2 + 2 * (m + 1))
                        gather_info(1 - b)
                        pe.wait_ge(xrow_ready, n0 + (m + 2))
                        transpose_x()
                        n = 3 * m + 2
                        pe.wait_ge(slot_full[n % SLOTS], laps + slots_at(n))
                        pe.wait_ge(y_stored, n0 + (m + 1))
                        pe.wait_ge(hT_ready, n0 + (m + 1))
                        w = wslot(n, KF)
                        for k in range(KF):
                            for h in range(2):
                                ins = mm(bank[5][h * C:(h + 1) * C, :], hT[:, k, :], w[:, k, h * HALF:(h + 1) * HALF],
                                         start=(k == 0), stop=(k == KF - 1))
                        ins.then_inc(y_psum, 1)

            last = pe.snap(rounds * (16 * 3 * NE // SLOTS))
            pe.wait_ge(slot_full[s0], last + slots_at(T_PLE) + 16)
            for i in range(TT):
                for k in range(KP):
                    ins = nc.tensor.transpose(bank[6 + k][:, i * P:(i + 1) * P], p_rows[:, i, k * P:(k + 1) * P], ident[:, :])
            ins.then_inc(pT_psum, 1)

            def transpose_u3(i):
                transpose_rows(2 * (2 * TT + i), u3, (4, 5, 6, 7))
                transpose_rows(2 * (2 * TT + i) + 1, u3, (4, 5, 6, 7))

            pe.wait_ge(y_stored, rounds * NE + 1)
            pe.wait_ge(xT_ready, rounds * NE + 1)
            pe.wait_ge(info_ready, rounds * (2 * NE) + 2)
            pe.wait_ge(pT0_ready, 1)
            pe.wait_ge(pT1_ready, 1)
            for i in range(TT):
                for h in range(2):
                    q = 2 * i + h
                    if q >= 6:
                        pe.wait_ge(ple_ready, q - 5)
                    for k in range(KP):
                        ins = mm(ple_bank(q)[:, :], pT[:, k, i * P:(i + 1) * P], wple[:, k, h * HALF:(h + 1) * HALF],
                                 start=(k == 0), stop=(k == KP - 1))
                    ins.then_inc(ple_psum, 1)
            def ple_gate(q):
                h, i = q // TT, q % TT
                pe.wait_ge(ut_low, 2 * (TT + i + 1))
                if q >= 4:
                    pe.wait_ge(pg_sig, q - 3)
                cols = slice(i * P, (i + 1) * P)
                for k in range(KD):
                    if k == KD // 2 and q < TT - 1:
                        transpose_u3(q + 1)
                    if i == 0:
                        for step, (block_, ks) in enumerate(gate_steps):
                            if (block_, ks.start) == (h, k):
                                pe.wait_ge(pg_low_ready[step], 1)
                    wh, wl = gate_part("high", h)[:, k, :], gate_part("low", h)[:, k, :]
                    for n, (still, stream) in enumerate(((u3T_high, wh), (u3T_high, wl), (u3T_low, wh))):
                        ins = mm(bank[q % 4][:, :], still[:, k, cols], stream, start=(k == 0 and n == 0),
                                 stop=(k == KD - 1 and n == 2))
                ins.then_inc(pg_psum, 1)

            pe.wait_ge(ple_ready, 6)
            transpose_u3(0)
            for q in range(2 * TT):
                if q == 0:
                    pe.wait_ge(ple_ready, 2 * TT)
                ple_gate(q)


_INS = ["x", "p", "norm_mix_g", "w_in", "conv_w", "conv_b", "w_rg", "b_rg", "w_ig", "b_ig", "lru_lambda", "w_pool",
        "pool_scale", "w_up_a", "w_up_b", "w_out", "norm_ffn_g", "w_router_group", "b_router_group", "w_router_expert",
        "b_router_expert", "w_gate_e", "w_up_e", "w_down_e", "norm_ple_g", "w_ple", "w_ple_gate", "final_norm_g"]
_OUTS = [((1, 512, 1024), "float32")]


def kernel(**inputs):
    import numpy as _np
    import concourse.bacc as _bacc
    from concourse import mybir as _mybir
    from concourse.bass_utils import run_bass_kernel_spmd as _run

    nc = _bacc.Bacc("TRN2", target_bir_lowering=False, num_devices=1)
    arrays, args = {}, []
    for name in _INS:
        a = _np.ascontiguousarray(inputs[name])
        arrays[f"in_{name}_dram"] = a
        args.append(nc.dram_tensor(f"in_{name}_dram", a.shape, _mybir.dt.from_np(a.dtype), kind="ExternalInput").ap())
    for i, (shape, dtype) in enumerate(_OUTS):
        dt = _mybir.dt.from_np(_np.dtype(dtype))
        args.append(nc.dram_tensor(f"out_{i}_dram", shape, dt, kind="ExternalOutput").ap())
    build(nc, *args)
    r = _run(nc, [arrays], core_ids=[0])
    got = tuple(r.results[0][f"out_{i}_dram"] for i in range(len(_OUTS)))
    return got[0]
```
